# Optimizing a Trainium2 kernel written in Bass

```python
import jax, jax.numpy as jnp
from jax import lax
import numpy as np

D_MODEL = 1024
BATCH = 1
SEQ = 256
DEPTH = 1

DN_HEADS = 4
DN_DK = 128
DN_DV = 128
DN_CHUNK = 64
SB_HEADS = 8
SB_DH = 64
SB_BLOCK = 128
LRU_WIDTH = 512
LRU_BLOCKS = 8
LRU_C = 8.0
CONV_W = 4
N_BRANCH = 3
N_EXPERTS = 16
N_GROUPS = 4
EXPERTS_PER_GROUP = N_EXPERTS // N_GROUPS
TOP_K = 2
D_FF = 512
DEEPNORM_ALPHA = (2.0 * DEPTH) ** 0.25
DEEPNORM_BETA = (8.0 * DEPTH) ** -0.25
LN_EPS = 1e-5
RMS_EPS = 1e-6

DN_QK = DN_HEADS * DN_DK
DN_V = DN_HEADS * DN_DV
SB_W = SB_HEADS * SB_DH
IN_SIZES = (DN_QK, DN_QK, DN_V, DN_V, DN_HEADS, DN_HEADS, SB_W, SB_W, SB_W, LRU_WIDTH, LRU_WIDTH)
IN_SPLITS = tuple(int(s) for s in np.cumsum(IN_SIZES)[:-1])
D_IN = int(sum(IN_SIZES))

kernel_name = 'hybrid_deltanet_stickbreak_rglru_grouped_moe'

def layer_norm(x, g, b):
    xf = x.astype(jnp.float32)
    mu = jnp.mean(xf, axis=-1, keepdims=True)
    xc = xf - mu
    var = jnp.mean(xc * xc, axis=-1, keepdims=True)
    return (xc * lax.rsqrt(var + LN_EPS) * g + b).astype(x.dtype)

def causal_depthwise_conv(x, w):
    return lax.conv_general_dilated(
        x, w[:, None, :], window_strides=(1,), padding=[(w.shape[0] - 1, 0)],
        dimension_numbers=('NWC', 'WIO', 'NWC'), feature_group_count=x.shape[-1])

def l2_normalize(x):
    xf = x.astype(jnp.float32)
    return xf * lax.rsqrt(jnp.sum(xf * xf, axis=-1, keepdims=True) + RMS_EPS)

def gated_rms_norm(o, z, w):
    of = o.astype(jnp.float32)
    n = of * lax.rsqrt(jnp.mean(of * of, axis=-1, keepdims=True) + RMS_EPS) * w
    return (n * jax.nn.silu(z.astype(jnp.float32))).astype(z.dtype)

def gated_delta_rule(q, k, v, g, beta):
    B, T, H, DK = q.shape
    DV = v.shape[-1]
    C = DN_CHUNK
    N = T // C
    f32 = jnp.float32

    def to_chunks(a):
        return a.astype(f32).reshape(B, N, C, H, -1).transpose(1, 0, 3, 2, 4)

    qc = to_chunks(q) * DK ** -0.5
    kc = to_chunks(k)
    vc = to_chunks(v)
    gc = to_chunks(g[..., None])[..., 0]
    bc = to_chunks(beta[..., None])[..., 0]
    g_cum = jnp.cumsum(gc, axis=-1)
    idx = jnp.arange(C)
    incl = idx[:, None] >= idx[None, :]
    strict = idx[:, None] > idx[None, :]
    diff = g_cum[..., :, None] - g_cum[..., None, :]
    decay = jnp.where(incl, jnp.exp(jnp.where(incl, diff, 0.0)), 0.0)
    kb = kc * bc[..., None]
    a_mat = jnp.where(strict, jnp.einsum('nbhid,nbhjd->nbhij', kb, kc) * decay, 0.0)
    eye = jnp.eye(C, dtype=f32)
    t_mat = lax.linalg.triangular_solve(a_mat + eye, jnp.broadcast_to(eye, a_mat.shape),
                                        left_side=True, lower=True, unit_diagonal=True)
    u = t_mat @ (vc * bc[..., None])
    w = t_mat @ (kb * jnp.exp(g_cum)[..., None])
    qk = jnp.einsum('nbhid,nbhjd->nbhij', qc, kc) * decay

    def step(S, inp):
        q_n, k_n, u_n, w_n, g_n, qk_n = inp
        v_new = u_n - w_n @ S
        o_n = (q_n * jnp.exp(g_n)[..., None]) @ S + qk_n @ v_new
        g_last = g_n[..., -1:]
        S = S * jnp.exp(g_last)[..., None] + jnp.einsum(
            'bhck,bhcv->bhkv', k_n * jnp.exp(g_last - g_n)[..., None], v_new)
        return S, o_n

    S0 = jnp.zeros((B, H, DK, DV), f32)
    _, o = lax.scan(step, S0, (qc, kc, u, w, g_cum, qk))
    return o.transpose(1, 0, 3, 2, 4).reshape(B, T, H, DV)

def stick_breaking_attention(q, k, v):
    B, T, H, Dh = q.shape
    nb = T // SB_BLOCK
    qb = q.reshape(B, nb, SB_BLOCK, H, Dh).transpose(1, 0, 3, 2, 4)
    kt = k.transpose(0, 2, 1, 3)
    vt = v.transpose(0, 2, 1, 3)
    key_pos = jnp.arange(T)

    def block(args):
        q_blk, blk = args
        z = jnp.einsum('bhqd,bhkd->bhqk', q_blk, kt).astype(jnp.float32) * Dh ** -0.5
        q_pos = blk * SB_BLOCK + jnp.arange(SB_BLOCK)
        past = key_pos[None, :] < q_pos[:, None]
        log_stay = jnp.where(past, jax.nn.log_sigmoid(-z), 0.0)
        log_after = lax.cumsum(log_stay, axis=3, reverse=True) - log_stay
        att = jnp.where(past, jnp.exp(jax.nn.log_sigmoid(z) + log_after), 0.0)
        return jnp.einsum('bhqk,bhkd->bhqd', att.astype(vt.dtype), vt)

    o = lax.map(block, (qb, jnp.arange(nb)))
    return o.transpose(1, 0, 3, 2, 4).reshape(B, T, H, Dh)

def rg_lru(x, w_a, b_a, w_x, b_x, lam):
    B, T, W = x.shape
    xh = x.reshape(B, T, LRU_BLOCKS, W // LRU_BLOCKS)
    gate_a = jnp.einsum('btnc,ncd->btnd', xh, w_a).reshape(B, T, W) + b_a
    gate_x = jnp.einsum('btnc,ncd->btnd', xh, w_x).reshape(B, T, W) + b_x
    r = jax.nn.sigmoid(gate_a.astype(jnp.float32))
    i = jax.nn.sigmoid(gate_x.astype(jnp.float32))
    log_a = -LRU_C * r * jax.nn.softplus(-lam.astype(jnp.float32))
    a = jnp.exp(log_a)
    b = jnp.sqrt(-jnp.expm1(2.0 * log_a)) * (i * x.astype(jnp.float32))

    def combine(left, right):
        a_l, b_l = left
        a_r, b_r = right
        return a_l * a_r, a_r * b_l + b_r

    _, h = lax.associative_scan(combine, (a, b), axis=1)
    return h.astype(x.dtype)

def hybrid_mixer(x, w_in, dn_conv_w, dn_a_log, dn_dt_bias, dn_norm_w, lru_conv_w, lru_conv_b,
                 lru_w_a, lru_b_a, lru_w_x, lru_b_x, lru_lambda, w_up_dn, w_up_sb, w_up_lru,
                 w_merge, b_merge, w_out):
    B, T, D = x.shape
    proj = x @ w_in
    (dn_q, dn_k, dn_v, dn_z, dn_b, dn_a, sb_q, sb_k, sb_v, lru_x, lru_y) = jnp.split(proj, IN_SPLITS, axis=-1)

    qkv = jax.nn.silu(causal_depthwise_conv(jnp.concatenate([dn_q, dn_k, dn_v], axis=-1), dn_conv_w))
    q, k, v = jnp.split(qkv, (DN_QK, 2 * DN_QK), axis=-1)
    q = l2_normalize(q.reshape(B, T, DN_HEADS, DN_DK))
    k = l2_normalize(k.reshape(B, T, DN_HEADS, DN_DK))
    v = v.reshape(B, T, DN_HEADS, DN_DV)
    beta = jax.nn.sigmoid(dn_b.astype(jnp.float32))
    g = -jnp.exp(dn_a_log.astype(jnp.float32)) * jax.nn.softplus(dn_a.astype(jnp.float32) + dn_dt_bias)
    o_a = gated_delta_rule(q, k, v, g, beta)
    y_a = gated_rms_norm(o_a, dn_z.reshape(B, T, DN_HEADS, DN_DV), dn_norm_w).reshape(B, T, DN_V)

    y_b = stick_breaking_attention(sb_q.reshape(B, T, SB_HEADS, SB_DH), sb_k.reshape(B, T, SB_HEADS, SB_DH),
                                   sb_v.reshape(B, T, SB_HEADS, SB_DH)).reshape(B, T, SB_W)

    xc = causal_depthwise_conv(lru_x, lru_conv_w) + lru_conv_b
    y_c = jax.nn.gelu(lru_y) * rg_lru(xc, lru_w_a, lru_b_a, lru_w_x, lru_b_x, lru_lambda)

    gates = jax.nn.sigmoid((x @ w_merge + b_merge).astype(jnp.float32)).reshape(B, T, N_BRANCH, D)
    merged = (gates[:, :, 0] * (y_a @ w_up_dn) + gates[:, :, 1] * (y_b @ w_up_sb)
              + gates[:, :, 2] * (y_c @ w_up_lru)).astype(x.dtype)
    return merged @ w_out

def grouped_moe(x, w_router, b_router, w1, w3, w2):
    B, T, D = x.shape
    N = B * T
    xf = x.reshape(N, D)
    scores = jax.nn.softmax((xf @ w_router).astype(jnp.float32), axis=-1)
    sel = (scores + b_router).reshape(N, N_GROUPS, EXPERTS_PER_GROUP)
    group_score = jnp.sum(lax.top_k(sel, TOP_K)[0], axis=-1)
    g_idx = jnp.argmax(group_score, axis=-1)
    in_group = jnp.take_along_axis(sel, g_idx[:, None, None], axis=1)[:, 0]
    _, e_local = lax.top_k(in_group, TOP_K)
    e_idx = g_idx[:, None] * EXPERTS_PER_GROUP + e_local
    w_sel = jnp.take_along_axis(scores, e_idx, axis=-1)
    w_sel = w_sel / jnp.sum(w_sel, axis=-1, keepdims=True)
    gate = jnp.sum(jax.nn.one_hot(e_idx, N_EXPERTS, dtype=jnp.float32) * w_sel[..., None], axis=1)
    h = jax.nn.silu(jnp.einsum('nd,edf->nef', xf, w1)) * jnp.einsum('nd,edf->nef', xf, w3)
    y = jnp.einsum('nef,efd->nd', (h * gate[:, :, None]).astype(x.dtype), w2)
    return y.reshape(B, T, D)

def setup_inputs(seed: int = 0) -> dict:
    key = jax.random.key(seed)
    ks = jax.random.split(key, 32)
    f32 = jnp.float32
    L = DEPTH

    def nrm(k, shape, scale):
        return jax.random.normal(k, shape, f32) * scale

    dt = jnp.exp(jax.random.uniform(ks[4], (L, DN_HEADS), f32, np.log(1e-3), np.log(1e-1)))
    u = jax.random.uniform(ks[12], (L, LRU_WIDTH), f32, 0.9, 0.999)
    s = u ** (1.0 / LRU_C)
    bw = LRU_WIDTH // LRU_BLOCKS
    return {
        'x': nrm(ks[0], (BATCH, SEQ, D_MODEL), 1.0),
        'w_in': nrm(ks[1], (L, D_MODEL, D_IN), D_MODEL ** -0.5),
        'dn_conv_w': nrm(ks[2], (L, CONV_W, 2 * DN_QK + DN_V), CONV_W ** -0.5),
        'dn_a_log': jnp.log(jax.random.uniform(ks[3], (L, DN_HEADS), f32, 1.0, 16.0)),
        'dn_dt_bias': dt + jnp.log(-jnp.expm1(-dt)),
        'dn_norm_w': 1.0 + nrm(ks[5], (L, DN_DV), 0.02),
        'lru_conv_w': nrm(ks[6], (L, CONV_W, LRU_WIDTH), CONV_W ** -0.5),
        'lru_conv_b': nrm(ks[7], (L, LRU_WIDTH), 0.01),
        'lru_w_a': nrm(ks[8], (L, LRU_BLOCKS, bw, bw), bw ** -0.5),
        'lru_b_a': nrm(ks[9], (L, LRU_WIDTH), 0.01),
        'lru_w_x': nrm(ks[10], (L, LRU_BLOCKS, bw, bw), bw ** -0.5),
        'lru_b_x': nrm(ks[11], (L, LRU_WIDTH), 0.01),
        'lru_lambda': jnp.log(s) - jnp.log1p(-s),
        'w_up_dn': nrm(ks[13], (L, DN_V, D_MODEL), DN_V ** -0.5),
        'w_up_sb': nrm(ks[14], (L, SB_W, D_MODEL), SB_W ** -0.5),
        'w_up_lru': nrm(ks[15], (L, LRU_WIDTH, D_MODEL), LRU_WIDTH ** -0.5),
        'w_merge': nrm(ks[16], (L, D_MODEL, N_BRANCH * D_MODEL), D_MODEL ** -0.5),
        'b_merge': nrm(ks[17], (L, N_BRANCH * D_MODEL), 0.01),
        'w_out': nrm(ks[18], (L, D_MODEL, D_MODEL), D_MODEL ** -0.5 * DEEPNORM_BETA),
        'ln1_g': 1.0 + nrm(ks[19], (L, D_MODEL), 0.02),
        'ln1_b': nrm(ks[20], (L, D_MODEL), 0.02),
        'w_router': nrm(ks[21], (D_MODEL, N_EXPERTS), D_MODEL ** -0.5),
        'b_router': nrm(ks[22], (N_EXPERTS,), 0.01),
        'moe_w1': nrm(ks[23], (L, N_EXPERTS, D_MODEL, D_FF), D_MODEL ** -0.5),
        'moe_w3': nrm(ks[24], (L, N_EXPERTS, D_MODEL, D_FF), D_MODEL ** -0.5),
        'moe_w2': nrm(ks[25], (L, N_EXPERTS, D_FF, D_MODEL), D_FF ** -0.5 * DEEPNORM_BETA),
        'ln2_g': 1.0 + nrm(ks[26], (L, D_MODEL), 0.02),
        'ln2_b': nrm(ks[27], (L, D_MODEL), 0.02),
    }

def reference(x, w_in, dn_conv_w, dn_a_log, dn_dt_bias, dn_norm_w, lru_conv_w, lru_conv_b, lru_w_a, lru_b_a,
              lru_w_x, lru_b_x, lru_lambda, w_up_dn, w_up_sb, w_up_lru, w_merge, b_merge, w_out, ln1_g, ln1_b,
              w_router, b_router, moe_w1, moe_w3, moe_w2, ln2_g, ln2_b):
    for l in range(DEPTH):
        mix = hybrid_mixer(x, w_in[l], dn_conv_w[l], dn_a_log[l], dn_dt_bias[l], dn_norm_w[l], lru_conv_w[l],
                           lru_conv_b[l], lru_w_a[l], lru_b_a[l], lru_w_x[l], lru_b_x[l], lru_lambda[l],
                           w_up_dn[l], w_up_sb[l], w_up_lru[l], w_merge[l], b_merge[l], w_out[l])
        x = layer_norm(DEEPNORM_ALPHA * x + mix, ln1_g[l], ln1_b[l])
        ffn = grouped_moe(x, w_router, b_router, moe_w1[l], moe_w3[l], moe_w2[l])
        x = layer_norm(DEEPNORM_ALPHA * x + ffn, ln2_g[l], ln2_b[l])
    return x


_drawn_inputs = setup_inputs


def setup_inputs(seed=0):
    import zlib

    import numpy as np

    out = dict(_drawn_inputs(seed))
    spreads = {}
    factors = {'dn_norm_w': 8.0,
     'lru_conv_b': 3.034,
     'lru_b_a': 64.0,
     'lru_b_x': 64.0,
     'b_merge': 8.0,
     'ln2_g': 7.833,
     'ln2_b': 8.712}
    for name, (base, spread) in spreads.items():
        noise = np.random.default_rng([zlib.crc32(name.encode()), seed]).standard_normal(out[name].shape)
        drawn = base * np.exp(spread * noise) if base else spread * noise
        out[name] = __import__('jax').numpy.asarray(drawn.astype(out[name].dtype))
    for name, factor in factors.items():
        out[name] = (out[name] * factor).astype(out[name].dtype)
    return out
```

```python
from contextlib import ExitStack

import concourse.bass as bass
from concourse import mybir

F32 = mybir.dt.float32
I32 = mybir.dt.int32
ALU = mybir.AluOpType
ACT = mybir.ActivationFunctionType
AX_X = mybir.AxisListType.X

P = 128
D = 1024
T = 256
TC = T // P
KD = D // P
DN_H = 4
SB_H = 8
SB_D = 64
LRU_CH = 4
LRU_C = 8.0
TAPS = 4
N_EXP = 16
GROUPS = 4
PER_GROUP = N_EXP // GROUPS
FF = 512
KF = FF // P
SLOTS = 64
PAIRS = N_EXP // 2
ALPHA = 2.0 ** 0.25
LN_EPS = 1e-5
RMS_EPS = 1e-6
N_UP = 3

SLOT = 4096
DENSE_SLOTS = 3
RING = 6

C_DNW, C_LW, C_LCB, C_BA, C_BX, C_LAM, C_BM, C_NW = 0, 48, 64, 68, 72, 76, 80, 104
N_ROWS = 105

Q0, K0, V0, Z0, BA0 = 0, 512, 1024, 1536, 2048
SQ0, SK0, SV0, LX0, LY0 = 2056, 2568, 3080, 3592, 4104
PIECES = [("q", Q0), ("k", K0), ("v", V0), ("z", Z0), ("sq", SQ0), ("sk", SK0), ("sv", SV0),
          ("lx", LX0), ("ly", LY0)] + [("gate", 512 * n) for n in range(6)]
N_PROJ = len(PIECES)
N_UNIT = 2 * N_PROJ
LEVELS = [2, 4, 8, 16, 32, 64]


def hybrid_layer(nc: bass.Bass, x, w_in, dn_conv_w, dn_a_log, dn_dt_bias, dn_norm_w, lru_conv_w,
                 lru_conv_b, lru_w_a, lru_b_a, lru_w_x, lru_b_x, lru_lambda, w_up_dn, w_up_sb,
                 w_up_lru, w_merge, b_merge, w_out, ln1_g, ln1_b, w_router, b_router, moe_w1,
                 moe_w3, moe_w2, ln2_g, ln2_b, out):
    with ExitStack() as ctx:
        def sb(name, shape, dt=F32):
            return ctx.enter_context(nc.sbuf_tensor(name, shape, dt))

        def sem(name):
            return ctx.enter_context(nc.semaphore(name))

        def flat(ap):
            names = "abcd"[:len(ap.shape) - 1]
            return ap.rearrange(f"p {' '.join(names)} -> p ({' '.join(names)})")

        def bc(ap, axis, n):
            a = ap.unsqueeze(axis)
            shape = list(a.shape)
            shape[axis] = n
            return a.broadcast_to(shape)

        ring = sb("ring", [P, RING, SLOT])
        hold = flat(ring[:, DENSE_SLOTS:RING, :])
        raw = {}
        for n, name in enumerate(("q", "k", "v", "z", "sq", "sk")):
            raw[name] = hold[:, n * 1024:(n + 1) * 1024].rearrange("p (c t) -> p c t", c=4)
        raw["sv"], raw["lx"], raw["ly"] = raw["q"], raw["k"], raw["v"]
        gates = hold[:, 6144:12288].rearrange("p (c t) -> p c t", c=24)
        xin = sb("xin", [P, TC, D])
        xT = sb("xT", [P, KD, T])
        qk = sb("qk", [P, DN_H, 2, T])
        vc = sb("vc", [P, DN_H, T])
        dn = sb("dn", [P, 8, 1024])
        yT = sb("yT", [P, 3, 4, T])
        vS = sb("vS", [P, TC, 512])
        tmp = sb("tmp", [P, 3, 1024])
        small = sb("small", [P, 512])
        ident = sb("ident", [P, P])
        alpha_ident = sb("alpha_ident", [P, P])
        upper = sb("upper", [P, P])
        strict = sb("strict", [P, P])
        lower = sb("lower", [P, P])
        negtri = sb("negtri", [P, P])
        ones = sb("ones", [P, P])
        negones = sb("negones", [P, P])
        past_bias = sb("past_bias", [P, 3, P])
        level = sb("level", [P, 1 + len(LEVELS), P])
        level1T = sb("level1T", [P, P])
        slot_ids = sb("slot_ids", [P, SLOTS])
        before = sb("before", [P, PER_GROUP, PER_GROUP])
        rows = sb("rows", [P, P])
        cols = sb("cols", [P, P])
        w_ba = sb("w_ba", [P, KD, 8])
        w_rt = sb("w_rt", [P, KD, N_EXP])
        w_bd = sb("w_bd", [P, 2, LRU_CH, P])
        eps = sb("eps", [P, 2])
        eps_ln, eps_rms = eps[:, 0:1], eps[:, 1:2]
        heads4 = sb("heads4", [P, 2, 4])
        b_rt = sb("b_rt", [P, N_EXP])
        rounds_i = sb("rounds_i", [P, 1], I32)
        tinyT = sb("tinyT", [N_EXP, T])

        def dn4(n):
            return dn[:, n, :].rearrange("p (c h t) -> p c h t", c=TC, h=DN_H)

        def dnh(n, half):
            return dn[:, n, half * 512:(half + 1) * 512].rearrange("p (h t) -> p h t", h=DN_H)

        vb = dn4(0)
        kdec, V0 = dnh(1, 0), dnh(1, 1)
        dec = dn4(2)
        R, V1 = dnh(2, 0), dnh(2, 1)
        AT, M, MT, XS, QKT = (dn4(n) for n in range(3, 8))
        decT = XS
        Amat = flat(vc[:]).rearrange("p (c h t) -> p c h t", c=TC, h=DN_H)
        qe = flat(vc[:])[:, 0:512].rearrange("p (h t) -> p h t", h=DN_H)
        norms = tmp[:, 0:2, :]
        eG1 = tmp[:, 2, 0:512].rearrange("p (h t) -> p h t", h=DN_H)
        S1 = tmp[:, 2, 512:1024].rearrange("p (h t) -> p h t", h=DN_H)
        zs = flat(dn[:, 0:3, :]).rearrange("p (h n) -> p h n", h=SB_H)
        att = flat(dn[:, 3:6, :]).rearrange("p (h n) -> p h n", h=SB_H)
        xc = flat(qk[:, 0:2]).rearrange("p (c t) -> p c t", c=4)
        lr = flat(qk[:, 2:4]).rearrange("p (c t) -> p c t", c=4)
        li = vc[:]
        la = dn[:, 6, :].rearrange("p (c t) -> p c t", c=4)
        far = dn[:, 7, :]
        lw, lq = tmp[:, 0, :], tmp[:, 1, :]
        merged = flat(dn[:, 0:2, :]).rearrange("p (m t) -> p m t", t=T)
        x1 = dn[:, 2:4, :]
        ln_gb = dn[:, 4:8, :]
        xg = flat(qk[:])[:, 0:1024]
        xgT = flat(qk[:])[:, 1024:2048].rearrange("p (k s) -> p k s", k=KD)
        yS = flat(vc[:])
        yflat = flat(yT[:])
        hS, gS = yflat[:, 0:512], yflat[:, 512:1024]
        hT = yflat[:, 1024:1536].rearrange("p (k s) -> p k s", k=KF)
        pick, pick_gate, pick_gateT = (yflat[:, a:a + 256].rearrange("p (c s) -> p c s", c=TC)
                                       for a in (1536, 1792, 2048))

        def sm(a, n):
            return small[:, a:a + n]

        v12, e12, z12, q12, sp12, m12 = (sm(12 * i, 12) for i in range(6))
        beta, g, gc, eg, kds = (sm(72 + 8 * i, 8) for i in range(5))
        ea, n8, negbeg = sm(112, 4), sm(116, 4), sm(120, 4)
        stats = sm(124, 12)
        mv = sm(136, 2)
        rstd = sm(138, 1)
        logit, score, sel, chosen, mask, tk = (sm(140 + 32 * i, 32) for i in range(6))
        mx, sume = sm(332, 2), sm(334, 2)
        gsum, gsel = sm(336, 8), sm(344, 8)
        posx = sm(352, 36).rearrange("p (c e) -> p c e", c=TC)
        gate = sm(388, 36).rearrange("p (c e) -> p c e", c=TC)
        cnt, rnd = sm(424, 1), sm(425, 4)
        cmp1, cmp2 = tmp[:, 0, 0:128], tmp[:, 0, 128:256]

        ps = ctx.enter_context(nc.psum_tensor("ps", [P, 8, 512], F32))

        def bank(b):
            return ps[:, b, :]

        def heads(b):
            return bank(b).rearrange("p (h t) -> p h t", h=4)

        S = {n: sem(n) for n in """x_in rows_in small_in bd_in bd_zeroed ln_in out_stored consts
            xT_psum rows_psum xT_ready cols_ready ba_psum ba_copied ba_tok
            unit_psum unit_read conv_done silu_done z_silu
            g_abs g_exp g_ready gb_psum gc_ready diff_ready dec_ready dec_masked sq_ready ss_psum
            rn_ready qk_ready tok_psum tok_ready kk_psum a_ready at_psum at_ready
            inv_x inv_xs inv_z inv_m inv_t inv_mt v0_psum v0_ready s1_psum s1_ready ks_psum
            r_ready v1_psum v1_ready o_psum o_sq oss_psum o_rms ya_ready sv_psum sv_ready
            z_psum z_log z_sp z_masked r_psum r_min att_ready yb_psum yb_ready
            xc_ready lru_log lru_a lru_near lru_var lru_b yc_scan gelu_ready yc_ready gates_ready
            up_psum merged_ready mix_psum ln_var ln_rstd x1_ready x1T_psum x1T_ready rt_psum
            rt_copied rtT_psum sm_in sm_exp mask_ready pos_psum rounds_ready
            pick_ready pick_gate_ready gathered xg_ready xgT_psum xgT_ready w1_done w3_done w2_done
            slots_moved h_silu h_ready hT_psum hT_ready y_ready scattered seeded y_final
            dve_order act_order pool_order""".split()}
        slot_loaded = [sem(f"slot_loaded_{i}") for i in range(RING)]

        block = ctx.enter_context(nc.Block())

        def in_order(eng, order):
            count = {}

            def step(ins, name=order, n=1):
                count[name] = count.get(name, 0) + n
                ins.then_inc(S[name], n)
                eng.wait_ge(S[name], count[name])
            return step

        LRU_UNITS = {24: ("ga", 0), 25: ("ga", 2), 26: ("gx", 0), 27: ("gx", 2)}
        n_dense = [n for n in range(N_UNIT + 4) if n not in LRU_UNITS]

        def unit(u):
            if u in LRU_UNITS:
                kind, c = LRU_UNITS[u]
                return kind, (lr if kind == "ga" else li), c, None
            n = n_dense.index(u)
            name, col = PIECES[n // 2]
            first = 2 * (n % 2)
            if name == "gate":
                return name, gates, col // P + first, n
            return name, raw[name], first, n

        N_ALL = N_UNIT + 4
        N_DENSE = N_PROJ + N_UP + 2
        w_up = [w_up_dn, w_up_sb, w_up_lru]

        @block.sync
        def _(sp):
            sp.dma_start(xin[:], x[0].rearrange("(c p) d -> p c d", p=P)).then_inc(S["x_in"], 16)
            for n in range(N_DENSE):
                s = n % DENSE_SLOTS
                m = n - DENSE_SLOTS
                if 0 <= m < N_PROJ:
                    sp.wait_ge(S["unit_psum"], n_dense[2 * m + 1] + 1)
                elif m >= N_PROJ:
                    sp.wait_ge(S["up_psum"], KD)
                dst = ring[:, s, :]
                if n < N_PROJ:
                    name, col = PIECES[n]
                    w = w_merge if name == "gate" else w_in
                    sp.dma_start(dst.rearrange("p (k n) -> p k n", k=KD),
                                 w[0, :, col:col + 512].rearrange("(p k) n -> p k n", k=KD)
                                 ).then_inc(slot_loaded[s], 16)
                elif n < N_PROJ + N_UP:
                    sp.dma_start(dst.rearrange("p (k n) -> p k n", k=4),
                                 w_up[n - N_PROJ][0].rearrange("(k p) n -> p k n", p=P)
                                 ).then_inc(slot_loaded[s], 16)
                else:
                    h = n - N_PROJ - N_UP
                    sp.dma_start(dst.rearrange("p (k n) -> p k n", k=KD),
                                 w_out[0, :, h * 512:(h + 1) * 512].rearrange("(k p) n -> p k n", p=P)
                                 ).then_inc(slot_loaded[s], 16)

            def expert_load(slot, pair):
                w = (moe_w1, moe_w3, moe_w2)[slot // 2]
                k = KF if slot >= 4 else KD
                src = w[0].rearrange("(a b) (p k) n -> a b p (k n)", b=2, k=k)
                sp.dma_start(ring[:, slot, :], src[pair, slot % 2]).then_inc(slot_loaded[slot], 16)

            expert_load(2, 0)
            sp.wait_ge(S["merged_ready"], KD)
            for slot in (3, 4, 5):
                expert_load(slot, 0)
            sp.wait_ge(S["mix_psum"], TC)
            for slot in (0, 1):
                expert_load(slot, 0)

            def pair_loads(pair, used):
                for slot, done in enumerate(("w1_done", "w1_done", "w3_done", "w3_done",
                                             "w2_done", "w2_done")):
                    sp.wait_ge(S[done], used)
                    expert_load(slot, pair)

            with sp.Fori(1, PAIRS) as p:
                pair_loads(p, p)
            sp.wait_ge(S["rounds_ready"], 1)
            n_rounds = sp.value_load(rounds_i[0:1, 0:1], min_val=1, max_val=T // SLOTS)
            with sp.If(n_rounds > 1):
                with sp.Fori(1, n_rounds) as r:
                    with sp.Fori(0, PAIRS) as p:
                        pair_loads(p, r * PAIRS + p)
            sp.wait_ge(S["y_final"], 1)
            sp.dma_start(out[0].rearrange("(c p) d -> p c d", p=P), xin[:]).then_inc(S["out_stored"], 16)
            sp.wait_ge(S["out_stored"], 16)

        @block.gpsimd
        def _(pool):
            step = in_order(pool, "pool_order")
            nc.gpsimd.memset(rows[:], 0.0)
            step(nc.gpsimd.memset(w_bd[:], 0.0), "bd_zeroed")
            nc.gpsimd.memset(ones[:], 1.0)
            nc.gpsimd.memset(negones[:], -1.0)
            nc.gpsimd.memset(ident[:], 0.0)
            nc.gpsimd.memset(alpha_ident[:], 0.0)
            nc.gpsimd.memset(past_bias[:], 0.0)
            nc.gpsimd.memset(eps_ln, LN_EPS)
            nc.gpsimd.memset(eps_rms, RMS_EPS)
            nc.gpsimd.memset(level1T[:], 0.0)
            nc.gpsimd.memset(before[:], 1.0)
            step(nc.gpsimd.memset(level[:], 0.0))
            for m, fill in ((ident, 1.0), (alpha_ident, ALPHA)):
                nc.gpsimd.affine_select(out=m[:], in_=m[:], compare_op=ALU.not_equal, fill=fill,
                                        base=0, pattern=[[-1, P]], channel_multiplier=1)
            for m, src, op, up in ((upper, ones, ALU.is_ge, 1), (strict, ones, ALU.is_gt, 1),
                                   (lower, ones, ALU.is_gt, -1), (negtri, negones, ALU.is_ge, -1)):
                nc.gpsimd.affine_select(out=m[:], in_=src[:], compare_op=op, fill=0.0, base=0,
                                        pattern=[[up, P]], channel_multiplier=-up)
            for n in (0, 2):
                nc.gpsimd.affine_select(out=past_bias[:, n, :], in_=past_bias[:, n, :],
                                        compare_op=ALU.is_gt, fill=-1e30, base=0,
                                        pattern=[[1, P]], channel_multiplier=-1)
            nc.gpsimd.affine_select(out=before[:], in_=before[:], compare_op=ALU.is_gt, fill=0.0,
                                    base=0, pattern=[[1, PER_GROUP], [-1, PER_GROUP]],
                                    channel_multiplier=0)
            nc.gpsimd.iota(slot_ids[:], pattern=[[1, SLOTS]], base=0, channel_multiplier=0,
                           allow_small_or_imprecise_dtypes=True)

            def left_half(n, size):
                return level[:, n, :].rearrange("p (b a s) -> p b a s", a=2, s=size)[:, :, 0, :]

            for n, size in enumerate([1] + LEVELS):
                nc.gpsimd.affine_select(
                    out=left_half(n, size), in_=ones[:, 0:P // 2].rearrange("p (b s) -> p b s", s=size),
                    compare_op=ALU.is_ge, fill=0.0, base=-size,
                    pattern=[[-2 * size, P // (2 * size)], [0, size]], channel_multiplier=1)
            right1 = level1T[:].rearrange("p (b a) -> p b a", a=2)[:, :, 1]
            step(nc.gpsimd.affine_select(out=right1, in_=ones[:, 0:P // 2], compare_op=ALU.not_equal,
                                         fill=0.0, base=0, pattern=[[-2, P // 2]],
                                         channel_multiplier=1))
            step(nc.gpsimd.tensor_tensor(right1, ones[:, 0:P // 2], right1, ALU.subtract))
            for n, size in enumerate([1] + LEVELS):
                end = nc.gpsimd.affine_select(
                    out=left_half(n, size), in_=left_half(n, size), compare_op=ALU.is_ge, fill=0.0,
                    base=2 * size - 1, pattern=[[2 * size, P // (2 * size)], [0, size]],
                    channel_multiplier=-1)
            step(end, "consts")

            pool.wait_ge(S["silu_done"], 6)
            for n in range(2):
                src = flat(qk[:, 2 * n:2 * n + 2])
                step(nc.gpsimd.tensor_tensor(norms[:, n, :], src, src, ALU.mult), "sq_ready")
            pool.wait_ge(S["dec_ready"], 1)
            d8 = dec.rearrange("p c h t -> p (c h) t")
            dT8 = decT.rearrange("p c h t -> p (c h) t")
            step(nc.gpsimd.tensor_tensor(d8, d8, bc(lower[:], 1, 8), ALU.mult), "dec_masked")
            step(nc.gpsimd.tensor_tensor(dT8, dT8, bc(upper[:], 1, 8), ALU.mult), "dec_masked")
            for h in range(SB_H):
                pool.wait_ge(S["z_sp"], h + 1)
                diag = zs[:, h, :].rearrange("p (a t) -> p a t", t=P)[:, 0:3:2, :]
                step(nc.gpsimd.tensor_tensor(diag, diag, bc(strict[:], 1, 2), ALU.mult), "z_masked")
            pool.wait_ge(S["yb_psum"], 1)
            pool.wait_ge(S["yc_ready"], 1)
            for n, w in enumerate((ln1_g, ln1_b, ln2_g, ln2_b)):
                pool.dma_start(ln_gb[:, n, :], w[0].partition_broadcast(P)).then_inc(S["ln_in"], 16)

        @block.scalar
        def _(act):
            step = in_order(act, "act_order")

            act.wait_ge(S["bd_zeroed"], 1)
            for first, n, src in ((C_DNW, 48, dn_conv_w[0].rearrange("w (c p) -> w c p", p=P)),
                                  (C_LW, 16, lru_conv_w[0].rearrange("w (c p) -> w c p", p=P)),
                                  (C_LCB, 4, lru_conv_b[0].rearrange("(c p) -> c p", p=P)),
                                  (C_BA, 4, lru_b_a[0].rearrange("(c p) -> c p", p=P)),
                                  (C_BX, 4, lru_b_x[0].rearrange("(c p) -> c p", p=P)),
                                  (C_LAM, 4, lru_lambda[0].rearrange("(c p) -> c p", p=P)),
                                  (C_BM, 24, b_merge[0].rearrange("(c p) -> c p", p=P)),
                                  (C_NW, 1, dn_norm_w)):
                if len(src.shape) == 3:
                    src = src.rearrange("w c p -> (w c) p")
                act.dma_start(rows[first:first + n, :], src).then_inc(S["rows_in"], 16)
            act.dma_start(w_ba[:], w_in[0, :, BA0:BA0 + 8].rearrange("(p k) n -> p k n", k=KD)
                          ).then_inc(S["small_in"], 16)
            act.dma_start(w_rt[:], w_router.rearrange("(p k) n -> p k n", k=KD)
                          ).then_inc(S["small_in"], 16)
            act.dma_start(heads4[:, 0, :], dn_a_log[0].partition_broadcast(P)).then_inc(S["small_in"], 16)
            act.dma_start(heads4[:, 1, :], dn_dt_bias[0].partition_broadcast(P)).then_inc(S["small_in"], 16)
            act.dma_start(b_rt[:], b_router.partition_broadcast(P)).then_inc(S["small_in"], 16)
            for n, w in enumerate((lru_w_a, lru_w_x)):
                for half in range(2):
                    o = 64 * half
                    act.dma_start(w_bd[o:o + 64, n, :, o:o + 64],
                                  w[0].rearrange("(c h) i o -> h i c o", h=2)[half]
                                  ).then_inc(S["bd_in"], 16)

            act.wait_ge(S["xT_psum"], 1)
            for b in (0, 2):
                nc.scalar.activation(flat(xT[:, 2 * b:2 * b + 2, :]), bank(b), ACT.Copy
                                     ).then_inc(S["xT_ready"], 1)

            def read_unit(u):
                kind, dst, c, _ = unit(u)
                act.wait_ge(S["unit_psum"], u + 1)
                if kind in ("sv", "lx", "ly"):
                    act.wait_ge(S["conv_done"], 6)
                if kind in ("gate", "ga", "gx"):
                    act.wait_ge(S["cols_ready"], 1)
                    b = {"gate": C_BM, "ga": C_BA, "gx": C_BX}[kind] + c
                    for j in range(2):
                        ins = nc.scalar.activation(dst[:, c + j, :], bank(u % 3)[:, j * T:(j + 1) * T],
                                                   ACT.Identity, bias=cols[:, b + j:b + j + 1])
                else:
                    ins = nc.scalar.activation(flat(dst[:, c:c + 2, :]), bank(u % 3), ACT.Copy,
                                               scale=SB_D ** -0.5 if kind == "sq" else 1.0)
                step(ins, "unit_read")

            def silu(v):
                act.wait_ge(S["conv_done"], v + 1)
                kind, c = v // 2, 2 * (v % 2)
                t = vc[:, c:c + 2, :] if kind == 2 else qk[:, c:c + 2, 1 - kind, :]
                step(nc.scalar.activation(t, t, ACT.Silu), "silu_done")

            read_unit(0)
            act.wait_ge(S["ba_psum"], 1)
            step(nc.scalar.activation(tinyT[0:8, :], ps[0:8, 7, 0:T], ACT.Copy), "ba_copied")
            for u in range(1, 6):
                read_unit(u)
                silu(u - 1)
            silu(5)
            read_unit(6)
            read_unit(7)
            step(nc.scalar.activation(flat(raw["z"]), flat(raw["z"]), ACT.Silu), "z_silu")
            act.wait_ge(S["g_abs"], 1)
            step(nc.scalar.activation(beta.rearrange("p (c h) -> p c h", c=TC),
                                      bank(7)[:, 256:272].rearrange("p (c e) -> p c e", c=TC)[:, :, 0:4],
                                      ACT.Sigmoid))
            nc.scalar.preload_act_table_set("natural_log_exp_and_others")
            step(nc.scalar.activation(ea, heads4[:, 0, :], ACT.Exp))
            step(nc.scalar.activation(e12, e12, ACT.Exp, scale=-1.0), "g_exp")
            act.wait_ge(S["gc_ready"], 1)
            step(nc.scalar.activation(eg, gc, ACT.Exp))
            act.wait_ge(S["diff_ready"], 1)
            step(nc.scalar.activation(eG1, heads(4), ACT.Exp))
            step(nc.scalar.activation(kds[:, 0:4], kds[:, 0:4], ACT.Exp))
            step(nc.scalar.activation(flat(dec), flat(dec), ACT.Exp, scale=-1.0))
            step(nc.scalar.activation(flat(decT), flat(decT), ACT.Exp), "dec_ready")
            read_unit(8)
            for n in range(2):
                act.wait_ge(S["ss_psum"], n + 1)
                for b in range(2):
                    step(nc.scalar.activation(norms[:, n, b * 512:(b + 1) * 512],
                                              bank((5, 3)[n] + b), ACT.Ln, bias=eps_rms))
                step(nc.scalar.activation(norms[:, n, :], norms[:, n, :], ACT.Exp, scale=-0.5),
                     "rn_ready")
            for u in (9, 10, 11):
                read_unit(u)
            act.wait_ge(S["at_psum"], 1)
            for c in range(TC):
                step(nc.scalar.activation(flat(AT[:, c]), bank(3 + c), ACT.Copy), "at_ready")
            read_unit(12)
            for n in range(len(LEVELS)):
                read_unit(13 + n)
                for c in range(TC):
                    act.wait_ge(S["inv_t"], TC * n + c + 1)
                    step(nc.scalar.activation(flat(MT[:, c]), bank(3 + 2 * c), ACT.Copy), "inv_mt")
            act.wait_ge(S["s1_psum"], 1)
            step(nc.scalar.activation(flat(S1), bank(4), ACT.Copy), "s1_ready")
            act.wait_ge(S["o_psum"], 1)
            for b in range(2):
                step(nc.scalar.activation(norms[:, 0, b * 512:(b + 1) * 512], bank(5 + b), ACT.Square),
                     "o_sq")
            act.wait_ge(S["oss_psum"], 1)
            for b in range(2):
                step(nc.scalar.activation(norms[:, 1, b * 512:(b + 1) * 512], bank(3 + b), ACT.Ln,
                                          bias=eps_rms, scale=1.0 / P))
            step(nc.scalar.activation(norms[:, 1, :], norms[:, 1, :], ACT.Exp, scale=-0.5), "o_rms")
            read_unit(19)
            act.wait_ge(S["sv_psum"], 1)
            for c in range(TC):
                step(nc.scalar.activation(vS[:, c, :], bank(3 + c), ACT.Copy), "sv_ready")

            for k in range(SB_H + 2):
                if k < SB_H:
                    act.wait_ge(S["z_psum"], k + 1)
                    step(nc.scalar.activation(zs[:, k, :], bank(3 + k % 3)[:, 0:T + P], ACT.Abs))
                    step(nc.scalar.activation(zs[:, k, :], zs[:, k, :], ACT.Exp, scale=-1.0))
                    step(nc.scalar.activation(zs[:, k, :], zs[:, k, :], ACT.Ln, bias=1.0), "z_log")
                if k >= 2:
                    act.wait_ge(S["r_min"], k - 1)
                    step(nc.scalar.activation(att[:, k - 2, :], att[:, k - 2, :], ACT.Exp), "att_ready")
                if k < SB_H:
                    read_unit(20 + k)
            for b in range(2):
                act.wait_ge(S["yb_psum"], 1)
                step(nc.scalar.activation(flat(yT[:, 1, 2 * b:2 * b + 2, :]), bank(6 + b), ACT.Copy),
                     "yb_ready")
            lrf, lif = flat(lr), flat(li)
            step(nc.scalar.activation(lrf, lrf, ACT.Exp, scale=-1.0))
            step(nc.scalar.activation(lif, lif, ACT.Exp, scale=-1.0), "lru_log")
            act.wait_ge(S["lru_near"], 1)
            step(nc.scalar.activation(flat(la), lrf, ACT.Exp))
            step(nc.scalar.activation(far, lrf, ACT.Exp, scale=2.0))
            step(nc.scalar.activation(lq, lw, ACT.Exp), "lru_a")
            for u in range(28, N_ALL):
                read_unit(u)
            act.wait_ge(S["lru_var"], 1)
            step(nc.scalar.activation(far, far, ACT.Sqrt), "lru_b")
            step(nc.scalar.activation(flat(raw["ly"]), flat(raw["ly"]), ACT.Gelu_apprx_tanh),
                 "gelu_ready")
            step(nc.scalar.activation(flat(gates), flat(gates), ACT.Sigmoid), "gates_ready")

            nc.scalar.preload_act_table_set("natural_log_exp_and_others")

            def inv_std(n):
                act.wait_ge(S["ln_var"], n + 1)
                step(nc.scalar.activation(rstd, mv[:, 1:2], ACT.Ln, bias=eps_ln))
                step(nc.scalar.activation(rstd, rstd, ACT.Exp, scale=-0.5), "ln_rstd")

            for c in range(TC):
                inv_std(c)
            act.wait_ge(S["x1T_psum"], 1)
            for b in (0, 2):
                nc.scalar.activation(flat(xT[:, 2 * b:2 * b + 2, :]), bank(4 + b), ACT.Copy
                                     ).then_inc(S["x1T_ready"], 1)
            act.wait_ge(S["rt_psum"], 1)
            step(nc.scalar.activation(tinyT[:], ps[0:N_EXP, 4, 0:T], ACT.Copy), "rt_copied")
            act.wait_ge(S["sm_in"], 1)
            step(nc.scalar.activation(score, score, ACT.Exp), "sm_exp")

            def read_gather(n):
                act.wait_ge(S["gathered"], n)
                nc.scalar.activation(xg[:, 0:512], bank(6), ACT.Copy).then_inc(S["xg_ready"], 1)

            def read_gatherT(n):
                act.wait_ge(S["xgT_psum"], n)
                nc.scalar.activation(flat(xgT[:, 0:4, :]), bank(6), ACT.Copy).then_inc(S["xgT_ready"], 1)

            nc.scalar.preload_act_table(ACT.Silu)
            read_gather(1)
            read_gatherT(1)
            act.wait_ge(S["rounds_ready"], 1)
            n_rounds = act.value_load(rounds_i[0:1, 0:1], min_val=1, max_val=T // SLOTS)
            with act.Fori(0, n_rounds) as r:
                with act.Fori(0, PAIRS) as p:
                    i = r * PAIRS + p
                    act.wait_ge(S["w1_done"], i + 1)
                    nc.scalar.activation(gS, bank(4), ACT.Silu).then_inc(S["h_silu"], 1)
                    read_gather(i + 2)
                    read_gatherT(i + 2)
                    act.wait_ge(S["w2_done"], i + 1)
                    nc.scalar.activation(yS[:, 0:512], bank(4), ACT.Copy).then_inc(S["y_ready"], 1)
            nc.scalar.preload_act_table_set("natural_log_exp_and_others")
            for c in range(TC):
                inv_std(TC + c)

        @block.tensor
        def _(pe):
            mm = nc.tensor.matmul

            def tr(dst, src):
                k = src.shape[0]
                return nc.tensor.transpose(dst, src, ident[0:k, 0:k])

            pe.wait_ge(S["consts"], 1)
            pe.wait_ge(S["rows_in"], 16 * 8)
            tr(bank(7)[:, 384:512], rows[:]).then_inc(S["rows_psum"], 1)
            pe.wait_ge(S["x_in"], 16)
            for k in range(KD):
                for c in range(TC):
                    last = tr(bank(k // 2)[:, (k % 2) * T + c * P:(k % 2) * T + (c + 1) * P],
                              xin[:, c, k:D:KD])
            last.then_inc(S["xT_psum"], 1)
            pe.wait_ge(S["xT_ready"], 4)
            pe.wait_ge(S["small_in"], 16 * 5)
            for k in range(KD):
                last = mm(ps[0:8, 7, 0:T], w_ba[:, k, :], xT[:, k, :], start=(k == 0), stop=(k == KD - 1))
            last.then_inc(S["ba_psum"], 1)

            def run_unit(u):
                kind, _, c, n = unit(u)
                if u >= 3:
                    pe.wait_ge(S["unit_read"], u - 2)
                if n is None:
                    pe.wait_ge(S["xc_ready"], 4)
                    pe.wait_ge(S["bd_in"], 16 * 4)
                    for j in range(2):
                        last = mm(bank(u % 3)[:, j * T:(j + 1) * T],
                                  w_bd[:, 0 if kind == "ga" else 1, c + j, :], xc[:, c + j, :],
                                  start=True, stop=True)
                else:
                    s = (n // 2) % DENSE_SLOTS
                    pe.wait_ge(slot_loaded[s], 16 * (n // 2 // DENSE_SLOTS + 1))
                    w = ring[:, s, :].rearrange("p (k n) -> p k n", k=KD)
                    for j in range(2):
                        o = (2 * (n % 2) + j) * P
                        for k in range(KD):
                            last = mm(bank(u % 3)[:, j * T:(j + 1) * T], w[:, k, o:o + P], xT[:, k, :],
                                      start=(k == 0), stop=(k == KD - 1))
                last.then_inc(S["unit_psum"], 1)

            run_unit(0)
            pe.wait_ge(S["ba_copied"], 1)
            for c in range(TC):
                last = tr(bank(7)[:, 256 + 8 * c:264 + 8 * c], tinyT[0:8, c * P:(c + 1) * P])
            last.then_inc(S["ba_tok"], 1)
            for u in range(1, 8):
                run_unit(u)

            pe.wait_ge(S["g_ready"], 1)
            for c in range(TC):
                mm(bank(7)[:, 272 + 4 * c:276 + 4 * c], upper[:], g[:, 4 * c:4 * c + 4],
                   start=True, stop=True)
            for c in range(TC):
                for h in range(DN_H):
                    last = mm(heads(3 + c)[:, h, :],
                              g[:, 4 * c + h:4 * c + h + 1].broadcast_to([P, P]), upper[:],
                              start=True, stop=True)
            last.then_inc(S["gb_psum"], 1)
            run_unit(8)

            for n in range(2):
                pe.wait_ge(S["sq_ready"], n + 1)
                if n == 1:
                    pe.wait_ge(S["dec_ready"], 1)
                for b in range(2):
                    last = mm(bank((5, 3)[n] + b), ones[:], norms[:, n, b * 512:(b + 1) * 512],
                              start=True, stop=True)
                last.then_inc(S["ss_psum"], 1)
            run_unit(9)

            pe.wait_ge(S["qk_ready"], 1)
            for h in range(DN_H):
                tr(heads(3)[:, h, :], qk[:, h, 0, 0:P])
            for c in range(TC):
                for h in range(DN_H):
                    last = tr(heads(5 + c)[:, h, :], vc[:, h, c * P:(c + 1) * P])
            last.then_inc(S["tok_psum"], 1)
            run_unit(10)

            pe.wait_ge(S["tok_ready"], 1)
            for c in range(TC):
                for h in range(DN_H):
                    last = mm(bank(3 + 2 * c + h // 2).rearrange("p (a b t) -> p a b t", a=2, b=2)[:, h % 2],
                              qk[:, h, 0, c * P:(c + 1) * P], qk[:, h, :, c * P:(c + 1) * P],
                              start=True, stop=True)
            last.then_inc(S["kk_psum"], 1)
            run_unit(11)
            pe.wait_ge(S["a_ready"], 1)
            for c in range(TC):
                for h in range(DN_H):
                    last = tr(heads(3 + c)[:, h, :], Amat[:, c, h, :])
            last.then_inc(S["at_psum"], 1)
            run_unit(12)

            pe.wait_ge(S["at_ready"], TC)
            for n in range(len(LEVELS)):
                for c in range(TC):
                    pe.wait_ge(S["inv_m"], TC * n + c + 1)
                    if n:
                        pe.wait_ge(S["inv_mt"], TC * (n - 1) + c + 1)
                    for h in range(DN_H):
                        last = mm(heads(3 + 2 * c)[:, h, :], AT[:, c, h, :], M[:, c, h, :],
                                  start=True, stop=True)
                    last.then_inc(S["inv_x"], 1)
                for c in range(TC):
                    pe.wait_ge(S["inv_xs"], TC * n + c + 1)
                    for h in range(DN_H):
                        last = mm(heads(4 + 2 * c)[:, h, :], MT[:, c, h, :], XS[:, c, h, :],
                                  start=True, stop=True)
                    last.then_inc(S["inv_z"], 1)
                run_unit(13 + n)
                for c in range(TC):
                    pe.wait_ge(S["inv_m"], TC * (n + 1) + c + 1)
                    for h in range(DN_H):
                        last = tr(heads(3 + 2 * c)[:, h, :], M[:, c, h, :])
                    last.then_inc(S["inv_t"], 1)

            pe.wait_ge(S["inv_mt"], TC * len(LEVELS))
            for h in range(DN_H):
                last = mm(heads(3)[:, h, :], MT[:, 0, h, :], vb[:, 0, h, :], start=True, stop=True)
            last.then_inc(S["v0_psum"], 1)
            pe.wait_ge(S["v0_ready"], 1)
            for h in range(DN_H):
                last = mm(heads(4)[:, h, :], kdec[:, h, :], V0[:, h, :], start=True, stop=True)
            last.then_inc(S["s1_psum"], 1)

            def o_part(c, h):
                return bank(5 + h // 2).rearrange("p (a c t) -> p a c t", a=2, c=TC)[:, h % 2, c, :]

            for h in range(DN_H):
                mm(o_part(0, h), V0[:, h, :], QKT[:, 0, h, :], start=True, stop=True)
            pe.wait_ge(S["s1_ready"], 1)
            for h in range(DN_H):
                last = mm(heads(3)[:, h, :], qk[:, h, 0, P:T], S1[:, h, :], start=True, stop=True)
            last.then_inc(S["ks_psum"], 1)
            pe.wait_ge(S["r_ready"], 1)
            for h in range(DN_H):
                last = mm(heads(4)[:, h, :], MT[:, 1, h, :], R[:, h, :], start=True, stop=True)
            last.then_inc(S["v1_psum"], 1)
            pe.wait_ge(S["v1_ready"], 1)
            for h in range(DN_H):
                mm(o_part(1, h), S1[:, h, :], qe[:, h, :], start=True, stop=False)
                last = mm(o_part(1, h), V1[:, h, :], QKT[:, 1, h, :], start=False, stop=True)
            last.then_inc(S["o_psum"], 1)
            run_unit(19)
            pe.wait_ge(S["o_sq"], 2)
            for b in range(2):
                last = mm(bank(3 + b), ones[:], norms[:, 0, b * 512:(b + 1) * 512], start=True, stop=True)
            last.then_inc(S["oss_psum"], 1)

            pe.wait_ge(S["o_rms"], 1)
            for c in range(TC):
                for j in range(4):
                    last = tr(heads(3 + c)[:, j, :], raw["sv"][:, j, c * P:(c + 1) * P])
            last.then_inc(S["sv_psum"], 1)
            pe.wait_ge(S["sv_ready"], TC)
            pe.wait_ge(S["ya_ready"], 1)

            for k in range(SB_H + 2):
                if k < SB_H:
                    if k >= 3:
                        pe.wait_ge(S["r_min"], k - 2)
                    o = SB_D * (k % 2)
                    kt, qt = raw["sk"][o:o + SB_D, k // 2, :], raw["sq"][o:o + SB_D, k // 2, :]
                    zb = bank(3 + k % 3)
                    mm(zb[:, 0:T], kt[:, 0:P], qt, start=True, stop=True, skip_group_check=True)
                    mm(zb[:, T:T + P], kt[:, P:T], qt[:, P:T], start=False, stop=True,
                       skip_group_check=True).then_inc(S["z_psum"], 1)
                    run_unit(20 + k)
                if 1 <= k <= SB_H:
                    h = k - 1
                    pe.wait_ge(S["z_masked"], h + 1)
                    zb = bank(3 + h % 3)
                    mm(zb[:, 0:T + P], negtri[:], zs[:, h, :], start=False, stop=True,
                       skip_group_check=True)
                    mm(zb[:, P:T], negones[:], zs[:, h, T:T + P], start=False, stop=True,
                       skip_group_check=True).then_inc(S["r_psum"], 1)
                if k >= 2:
                    h = k - 2
                    pe.wait_ge(S["att_ready"], h + 1)
                    o = SB_D * (h % 2)
                    yb = ps[o:o + SB_D, 6 + h // 4, (h // 2 % 2) * T:(h // 2 % 2 + 1) * T]
                    mm(yb, vS[:, 0, h * SB_D:(h + 1) * SB_D], att[:, h, 0:T], start=True, stop=False,
                       skip_group_check=True)
                    last = mm(yb[:, P:T], vS[:, 1, h * SB_D:(h + 1) * SB_D], att[:, h, T:T + P],
                              start=False, stop=True, skip_group_check=True)
            last.then_inc(S["yb_psum"], 1)
            for u in range(28, N_ALL):
                run_unit(u)

            for n in range(N_UP):
                pe.wait_ge(slot_loaded[(N_PROJ + n) % DENSE_SLOTS],
                           16 * ((N_PROJ + n) // DENSE_SLOTS + 1))
            pe.wait_ge(S["ya_ready"], 1)
            pe.wait_ge(S["yb_ready"], 2)
            pe.wait_ge(S["yc_ready"], 1)
            for m in range(KD):
                if m >= 2:
                    pe.wait_ge(S["merged_ready"], m - 1)
                for n in range(N_UP):
                    w = ring[:, (N_PROJ + n) % DENSE_SLOTS, :].rearrange("p (k n) -> p k n", k=4)
                    ub = bank(3 + 2 * (m % 2) + n // 2)[:, (n % 2) * T:(n % 2 + 1) * T]
                    for k in range(4):
                        last = mm(ub, w[:, k, m * P:(m + 1) * P], yT[:, n, k, :],
                                  start=(k == 0), stop=(k == 3))
                last.then_inc(S["up_psum"], 1)

            pe.wait_ge(S["merged_ready"], KD)
            pe.wait_ge(S["unit_read"], N_ALL)
            for n in range(2):
                p = N_PROJ + N_UP + n
                pe.wait_ge(slot_loaded[p % DENSE_SLOTS], 16 * (p // DENSE_SLOTS + 1))
            for c in range(TC):
                for n in range(2):
                    w = ring[:, (N_PROJ + N_UP + n) % DENSE_SLOTS, :].rearrange("p (k n) -> p k n", k=KD)
                    for k in range(KD):
                        last = mm(bank(2 * c + n), merged[:, k, c * P:(c + 1) * P], w[:, k, :],
                                  start=(k == 0), stop=(k == KD - 1))
                last.then_inc(S["mix_psum"], 1)

            for c in range(TC):
                pe.wait_ge(S["x1_ready"], c + 1)
                for k in range(KD):
                    last = tr(bank(4 + k // 2)[:, (k % 2) * T + c * P:(k % 2) * T + (c + 1) * P],
                              x1[:, c, k:D:KD])
            last.then_inc(S["x1T_psum"], 1)
            pe.wait_ge(S["x1T_ready"], 4)
            for k in range(KD):
                last = mm(ps[0:N_EXP, 4, 0:T], w_rt[:, k, :], xT[:, k, :], start=(k == 0), stop=(k == KD - 1))
            last.then_inc(S["rt_psum"], 1)
            for c in range(TC):
                for n in range(2):
                    mm(bank(2 * c + n), alpha_ident[:], x1[:, c, n * 512:(n + 1) * 512],
                       start=True, stop=False, skip_group_check=True)
            pe.wait_ge(S["rt_copied"], 1)
            for c in range(TC):
                last = tr(bank(5)[:, N_EXP * c:N_EXP * (c + 1)], tinyT[:, c * P:(c + 1) * P])
            last.then_inc(S["rtT_psum"], 1)
            pe.wait_ge(S["mask_ready"], 1)
            mc = [mask[:, N_EXP * c:N_EXP * (c + 1)] for c in range(TC)]
            mm(bank(6)[:, 0:16], strict[:], mc[0], start=True, stop=True)
            mm(bank(6)[:, 16:32], ones[:], mc[0], start=True, stop=False)
            mm(bank(6)[:, 16:32], strict[:], mc[1], start=False, stop=True)
            mm(bank(6)[:, 32:48], ones[:], mc[0], start=True, stop=False)
            mm(bank(6)[:, 32:48], ones[:], mc[1], start=False, stop=True).then_inc(S["pos_psum"], 1)

            def gather(n):
                pe.wait_ge(S["pick_ready"], n)
                for half in range(2):
                    for c in range(TC):
                        last = mm(bank(6 + half), pick[:, c, :], x1[:, c, half * 512:(half + 1) * 512],
                                  start=(c == 0), stop=(c == TC - 1))
                last.then_inc(S["gathered"], 1)

            def gather_transpose(n):
                pe.wait_ge(S["xg_ready"], 2 * n)
                for k in range(KD):
                    last = tr(heads(6 + k // 4)[:, k % 4, :], xg[:, k:D:KD])
                last.then_inc(S["xgT_psum"], 1)

            gather(1)
            gather_transpose(1)
            pe.wait_ge(S["rounds_ready"], 1)
            n_rounds = pe.value_load(rounds_i[0:1, 0:1], min_val=1, max_val=T // SLOTS)
            before_moe = [16 * len([n for n in range(N_DENSE) if n % DENSE_SLOTS == s])
                          if s < DENSE_SLOTS else 0 for s in range(RING)]

            def two_experts(dst, lhsT, slot, cols_, steps):
                for k in range(steps):
                    for e in range(2):
                        w = ring[:, slot + e, :].rearrange("p (k n) -> p k n", k=steps)
                        last = mm(dst[e * SLOTS:(e + 1) * SLOTS, :], lhsT[:, k, e * SLOTS:(e + 1) * SLOTS],
                                  w[:, k, cols_:cols_ + 512], start=(k == 0), stop=(k == steps - 1))
                return last

            with pe.Fori(0, n_rounds) as r:
                with pe.Fori(0, PAIRS) as p:
                    i = r * PAIRS + p
                    pe.wait_ge(S["xgT_ready"], 2 * i + 2)
                    for s in (0, 1):
                        pe.wait_ge(slot_loaded[s], 16 * i + 16 + before_moe[s])
                    two_experts(bank(4), xgT, 0, 0, KD).then_inc(S["w1_done"], 1)
                    for s in (2, 3):
                        pe.wait_ge(slot_loaded[s], 16 * i + 16 + before_moe[s])
                    two_experts(bank(5), xgT, 2, 0, KD).then_inc(S["w3_done"], 1)
                    gather(i + 2)
                    pe.wait_ge(S["h_ready"], i + 1)
                    for k in range(KF):
                        tr(heads(4)[:, k, :], hS[:, k:FF:KF])
                    pe.wait_ge(S["pick_gate_ready"], i + 1)
                    for c in range(TC):
                        last = tr(heads(5)[:, c, :], pick_gate[:, c, :])
                    last.then_inc(S["hT_psum"], 1)
                    gather_transpose(i + 2)
                    pe.wait_ge(S["hT_ready"], i + 1)
                    for s in (4, 5):
                        pe.wait_ge(slot_loaded[s], 16 * i + 16 + before_moe[s])
                    for half in range(2):
                        last = two_experts(bank(4 + half), hT, 4, half * 512, KF)
                    last.then_inc(S["w2_done"], 1)
                    pe.wait_ge(S["y_ready"], 2 * i + 2)
                    for c in range(TC):
                        for half in range(2):
                            last = mm(bank(2 * c + half), pick_gateT[:, c, :],
                                      yS[:, half * 512:(half + 1) * 512], start=False, stop=False,
                                      skip_group_check=True)
                    last.then_inc(S["scattered"], 1)

        @block.vector
        def _(dve):
            step = in_order(dve, "dve_order")
            tt, ts, stt = nc.vector.tensor_tensor, nc.vector.tensor_scalar, nc.vector.scalar_tensor_tensor
            copy = nc.vector.tensor_copy

            dve.wait_ge(S["rows_psum"], 1)
            step(copy(cols[:], bank(7)[:, 384:512]), "cols_ready")
            dve.wait_ge(S["xT_psum"], 1)
            for b in (1, 3):
                copy(flat(xT[:, 2 * b:2 * b + 2, :]), bank(b)).then_inc(S["xT_ready"], 1)

            def conv(dst, src, w0, stride, bias=None):
                def w(tap):
                    return cols[:, w0 + tap * stride:w0 + tap * stride + 1]
                if bias is None:
                    step(ts(dst, src, w(TAPS - 1), None, ALU.mult))
                else:
                    step(ts(dst, src, w(TAPS - 1), bias, ALU.mult, ALU.add))
                for back in range(1, TAPS):
                    last = stt(dst[:, back:T], src[:, 0:T - back], w(TAPS - 1 - back), dst[:, back:T],
                               ALU.mult, ALU.add)
                    if back < TAPS - 1:
                        step(last)
                return last

            def conv_unit(v):
                dve.wait_ge(S["unit_read"], v + 1)
                kind, c = v // 2, 2 * (v % 2)
                for j in range(2):
                    dst = vc[:, c + j, :] if kind == 2 else qk[:, c + j, 1 - kind, :]
                    src = raw[("q", "k", "v")[kind]][:, c + j, :]
                    last = conv(dst, src, C_DNW + 4 * kind + c + j, 12)
                    step(last) if j == 0 else step(last, "conv_done")

            conv_unit(0)
            dve.wait_ge(S["ba_tok"], 1)
            dve.wait_ge(S["small_in"], 16 * 5)
            tok8 = bank(7)[:, 256:272].rearrange("p (c e) -> p c e", c=TC)
            step(tt(v12[:, 0:8].rearrange("p (c h) -> p c h", c=TC), tok8[:, :, 4:8],
                    bc(heads4[:, 1, :], 1, TC), ALU.add))
            step(ts(v12[:, 8:12], cols[:, C_LAM:C_LAM + 4], -1.0, None, ALU.mult))
            step(ts(m12, v12, 0.0, None, ALU.max))
            step(stt(e12, v12, -1.0, v12, ALU.mult, ALU.max), "g_abs")
            for v in range(1, 6):
                conv_unit(v)
            dve.wait_ge(S["g_exp"], 1)
            step(ts(z12, e12, 2.0, None, ALU.add))
            step(nc.vector.reciprocal(z12, z12))
            step(tt(z12, z12, e12, ALU.mult))
            step(tt(e12, z12, z12, ALU.mult))
            step(ts(q12, e12, 1.0 / 17, None, ALU.mult))
            for n in (15, 13, 11, 9, 7, 5, 3):
                step(stt(q12, q12, 1.0 / n, e12, ALU.add, ALU.mult))
            step(stt(q12, q12, 1.0, z12, ALU.add, ALU.mult))
            step(stt(sp12, q12, 2.0, m12, ALU.mult, ALU.add))
            step(ts(n8, sp12[:, 8:12], -LRU_C, None, ALU.mult))
            step(stt(g.rearrange("p (c h) -> p c h", c=TC), sp12[:, 0:8].rearrange("p (c h) -> p c h", c=TC),
                     -1.0, bc(ea, 1, TC), ALU.mult, ALU.mult), "g_ready")
            dve.wait_ge(S["gb_psum"], 1)
            step(copy(gc, bank(7)[:, 272:280]), "gc_ready")
            for c in range(TC):
                for h in range(DN_H):
                    gcol = gc[:, 4 * c + h:4 * c + h + 1]
                    ts(dec[:, c, h, :], heads(3 + c)[:, h, :], gcol, 0.0, ALU.subtract, ALU.max)
                    ts(decT[:, c, h, :], heads(3 + c)[:, h, :], gcol, 0.0, ALU.subtract, ALU.min)
            step(tt(kds[:, 0:4], heads(3)[:, :, P - 1], gc[:, 0:4], ALU.subtract), "diff_ready")
            dve.wait_ge(S["z_silu"], 1)
            step(ts(flat(raw["z"]), flat(raw["z"]), cols[:, C_NW:C_NW + 1], None, ALU.mult))
            for n in range(2):
                dve.wait_ge(S["rn_ready"], n + 1)
                rn = norms[:, n, :].rearrange("p (h b t) -> p h b t", h=2, b=2)
                for b, scale in ((0, 1.0), (1, P ** -0.5)):
                    t = qk[:, 2 * n:2 * n + 2, b, :]
                    last = stt(t, t, scale, rn[:, :, b, :], ALU.mult, ALU.mult)
            step(last, "qk_ready")
            dve.wait_ge(S["tok_psum"], 1)
            dve.wait_ge(S["dec_ready"], 1)
            for c in range(TC):
                for h in range(DN_H):
                    ts(vb[:, c, h, :], heads(5 + c)[:, h, :], beta[:, 4 * c + h:4 * c + h + 1], None, ALU.mult)
            for h in range(DN_H):
                last = ts(kdec[:, h, :], heads(3)[:, h, :], kds[:, h:h + 1], None, ALU.mult)
            step(last, "tok_ready")
            step(stt(negbeg, beta[:, 4:8], -1.0, eg[:, 4:8], ALU.mult, ALU.mult))
            dve.wait_ge(S["kk_psum"], 1)
            dve.wait_ge(S["dec_masked"], 2)

            def pair_bank(b):
                return bank(b).rearrange("p (a b t) -> p a b t", a=2, b=2)

            for c in range(TC):
                for h in range(DN_H):
                    stt(Amat[:, c, h, :], pair_bank(3 + 2 * c + h // 2)[:, h % 2, 0, :],
                        beta[:, 4 * c + h:4 * c + h + 1], dec[:, c, h, :], ALU.mult, ALU.mult)
                for hp in range(2):
                    last = tt(QKT[:, c, 2 * hp:2 * hp + 2, :], pair_bank(3 + 2 * c + hp)[:, :, 1, :],
                              decT[:, c, 2 * hp:2 * hp + 2, :], ALU.mult)
            step(last, "a_ready")

            def all8(m):
                return m.rearrange("p c h t -> p (c h) t")

            step(tt(all8(M), all8(Amat), bc(level[:, 0, :], 1, 8), ALU.mult))
            for c in range(TC):
                step(tt(M[:, c], bc(ident[:], 1, 4), M[:, c], ALU.subtract), "inv_m")
            dve.wait_ge(S["at_ready"], TC)
            step(tt(all8(MT), all8(AT), bc(level1T[:], 1, 8), ALU.mult))
            step(tt(all8(MT), bc(ident[:], 1, 8), all8(MT), ALU.subtract))
            step(tt(qe, qk[:, :, 1, P:T], eG1, ALU.mult))
            for n in range(len(LEVELS)):
                for c in range(TC):
                    dve.wait_ge(S["inv_x"], TC * n + c + 1)
                    step(tt(XS[:, c], heads(3 + 2 * c), bc(level[:, n + 1, :], 1, 4), ALU.mult), "inv_xs")
                for c in range(TC):
                    dve.wait_ge(S["inv_z"], TC * n + c + 1)
                    step(tt(M[:, c], M[:, c], heads(4 + 2 * c), ALU.subtract), "inv_m")
            dve.wait_ge(S["v0_psum"], 1)
            step(copy(flat(V0), bank(3)), "v0_ready")
            dve.wait_ge(S["ks_psum"], 1)
            for h in range(DN_H):
                last = stt(R[:, h, :], heads(3)[:, h, :], negbeg[:, h:h + 1], vb[:, 1, h, :],
                           ALU.mult, ALU.add)
            step(last, "r_ready")
            dve.wait_ge(S["v1_psum"], 1)
            step(copy(flat(V1), bank(4)), "v1_ready")
            dve.wait_ge(S["o_rms"], 1)
            for b in range(2):
                ya = flat(yT[:, 0, 2 * b:2 * b + 2, :])
                step(tt(ya, bank(5 + b), norms[:, 1, b * 512:(b + 1) * 512], ALU.mult))
                last = tt(ya, ya, flat(raw["z"][:, 2 * b:2 * b + 2, :]), ALU.mult)
                step(last) if b == 0 else step(last, "ya_ready")

            for k in range(SB_H + 2):
                if k < 4:
                    dve.wait_ge(S["unit_read"], 18)
                    last = conv(xc[:, k, :], raw["lx"][:, k, :], C_LW + k, 4,
                                cols[:, C_LCB + k:C_LCB + k + 1])
                    step(last, "xc_ready")
                if k >= 2:
                    h = k - 2
                    dve.wait_ge(S["r_psum"], h + 1)
                    step(stt(att[:, h, :], bank(3 + h % 3)[:, 0:T + P], 0.0, flat(past_bias[:]),
                             ALU.min, ALU.add), "r_min")
                if k < SB_H:
                    dve.wait_ge(S["z_log"], k + 1)
                    step(stt(zs[:, k, :], bank(3 + k % 3)[:, 0:T + P], 0.0, zs[:, k, :],
                             ALU.max, ALU.add), "z_sp")

            dve.wait_ge(S["lru_log"], 1)
            for t in (flat(lr), flat(li)):
                step(ts(t, t, 1.0, None, ALU.add))
                step(nc.vector.reciprocal(t, t))
            for c in range(LRU_CH):
                last = ts(lr[:, c, :], lr[:, c, :], n8[:, c:c + 1], None, ALU.mult)
            step(last)
            step(ts(lw, flat(lr), 2.0, -1.0, ALU.mult, ALU.max), "lru_near")
            step(tt(flat(li), flat(li), flat(xc), ALU.mult))
            dve.wait_ge(S["lru_a"], 1)
            step(tt(far, lq, far, ALU.subtract))
            step(ts(lw, lw, 0.25, None, ALU.mult))
            step(ts(lq, lw, 1.0 / 720, None, ALU.mult))
            for coef in (1.0 / 120, 1.0 / 24, 1.0 / 6, 0.5, 1.0):
                step(stt(lq, lq, coef, lw, ALU.add, ALU.mult))
            step(stt(lw, lq, 2.0, lq, ALU.add, ALU.mult))
            step(stt(lq, lw, 2.0, lw, ALU.add, ALU.mult))
            step(tt(far, far, lq, ALU.subtract))
            step(ts(far, far, 0.0, None, ALU.max), "lru_var")
            dve.wait_ge(S["lru_b"], 1)
            step(tt(flat(li), flat(li), far, ALU.mult))
            for c in range(LRU_CH):
                last = nc.vector.tensor_tensor_scan(lr[:, c, :], la[:, c, :], li[:, c, :], 0.0,
                                                    ALU.mult, ALU.add)
            step(last)
            dve.wait_ge(S["gelu_ready"], 1)
            step(tt(flat(yT[:, 2]), flat(lr), flat(raw["ly"]), ALU.mult), "yc_ready")

            dve.wait_ge(S["gates_ready"], 1)
            gb = gates.rearrange("p (n m) t -> p n m t", n=3)
            prod = tmp[:, 0, 0:768].rearrange("p (n t) -> p n t", n=3)
            for m in range(KD):
                dve.wait_ge(S["up_psum"], m + 1)
                b = 3 + 2 * (m % 2)
                tt(prod[:, 0:2, :], bank(b).rearrange("p (n t) -> p n t", n=2), gb[:, 0:2, m, :], ALU.mult)
                step(tt(prod[:, 2, :], bank(b + 1)[:, 0:T], gb[:, 2, m, :], ALU.mult))
                step(tt(prod[:, 0, :], prod[:, 0, :], prod[:, 1, :], ALU.add))
                step(tt(merged[:, m, :], prod[:, 0, :], prod[:, 2, :], ALU.add), "merged_ready")

            def layer_norm(t, gb0, name):
                for n in range(2):
                    nc.vector.bn_stats(stats[:, 6 * n:6 * n + 6], t[:, n * 512:(n + 1) * 512])
                step(copy(rnd[:, 0:1], eps_ln))
                step(nc.vector.bn_aggr(mv, stats), "ln_var")
                ln_count[0] += 1
                dve.wait_ge(S["ln_rstd"], ln_count[0])
                step(ts(t, t, mv[:, 0:1], rstd, ALU.subtract, ALU.mult))
                step(tt(t, t, ln_gb[:, gb0, :], ALU.mult))
                return tt(t, t, ln_gb[:, gb0 + 1, :], ALU.add)

            ln_count = [0]
            dve.wait_ge(S["ln_in"], 16 * 4)
            for c in range(TC):
                dve.wait_ge(S["mix_psum"], c + 1)
                for n in range(2):
                    part = slice(n * 512, (n + 1) * 512)
                    last = stt(x1[:, c, part], xin[:, c, part], ALPHA, bank(2 * c + n), ALU.mult, ALU.add)
                step(last)
                step(layer_norm(x1[:, c, :], 0, "x1"), "x1_ready")
            dve.wait_ge(S["x1T_psum"], 1)
            for b in (1, 3):
                copy(flat(xT[:, 2 * b:2 * b + 2, :]), bank(4 + b)).then_inc(S["x1T_ready"], 1)

            dve.wait_ge(S["rtT_psum"], 1)
            l3, s3 = (t.rearrange("p (c e) -> p c e", c=TC) for t in (logit, score))
            step(copy(logit, bank(5)[:, 0:32]))
            step(nc.vector.tensor_reduce(mx, l3, AX_X, ALU.max))
            step(tt(s3, l3, bc(mx, 2, N_EXP), ALU.subtract), "sm_in")
            dve.wait_ge(S["sm_exp"], 1)
            step(nc.vector.tensor_reduce(sume, s3, AX_X, ALU.add))
            step(nc.vector.reciprocal(sume, sume))
            step(tt(s3, s3, bc(sume, 2, N_EXP), ALU.mult))
            step(tt(sel.rearrange("p (c e) -> p c e", c=TC), s3, bc(b_rt[:], 1, TC), ALU.add))

            def ranks(dst, vals, n):
                v = vals.rearrange("p (g e) -> p g e", e=PER_GROUP)
                other, own = bc(v, 2, PER_GROUP), bc(v, 3, PER_GROUP)
                c1, c2 = (t[:, 0:16 * n].rearrange("p (g a b) -> p g a b", a=4, b=4) for t in (cmp1, cmp2))
                step(tt(c1, other, own, ALU.is_equal))
                step(tt(c1, c1, bc(before[:], 1, n), ALU.mult))
                step(tt(c2, other, own, ALU.is_gt))
                step(tt(c1, c1, c2, ALU.add))
                step(nc.vector.tensor_reduce(dst, c1.rearrange("p g a b -> p (g a) b"), AX_X, ALU.add))

            ranks(chosen, sel, 8)
            step(ts(chosen, chosen, 1.5, None, ALU.is_lt))
            step(tt(tk, sel, chosen, ALU.mult))
            step(nc.vector.tensor_reduce(gsum, tk.rearrange("p (g e) -> p g e", e=4), AX_X, ALU.add))
            ranks(gsel, gsum, 2)
            step(ts(gsel, gsel, 0.5, None, ALU.is_lt))
            step(tt(mask.rearrange("p (g e) -> p g e", e=4), chosen.rearrange("p (g e) -> p g e", e=4),
                    bc(gsel, 2, 4), ALU.mult), "mask_ready")
            step(tt(tk, score, mask, ALU.mult))
            tk3 = tk.rearrange("p (c e) -> p c e", c=TC)
            step(nc.vector.tensor_reduce(sume, tk3, AX_X, ALU.add))
            step(nc.vector.reciprocal(sume, sume))
            step(tt(gate[:, :, 0:N_EXP], tk3, bc(sume, 2, N_EXP), ALU.mult))
            step(copy(gate[:, :, N_EXP:], gate[:, :, 0:2]))
            dve.wait_ge(S["pos_psum"], 1)
            m3 = mask.rearrange("p (c e) -> p c e", c=TC)
            step(stt(posx[:, :, 0:N_EXP], bank(6)[:, 0:32].rearrange("p (c e) -> p c e", c=TC), 1024.0, m3,
                     ALU.add, ALU.mult))
            step(ts(posx[:, :, 0:N_EXP], posx[:, :, 0:N_EXP], -1024.0, None, ALU.add))
            step(ts(posx[:, :, N_EXP:], posx[:, :, 0:2], -float(SLOTS), None, ALU.add))
            step(nc.vector.tensor_reduce(cnt, bank(6)[:, 32:48], AX_X, ALU.max))
            for n in range(1, T // SLOTS):
                step(ts(rnd[:, n:n + 1], cnt, float(n * SLOTS), None, ALU.is_gt))
            step(nc.vector.tensor_reduce(rnd[:, 0:1], rnd[:, 1:4], AX_X, ALU.add))
            step(ts(rounds_i[:], rnd[:, 0:1], 1.0, None, ALU.add), "rounds_ready")

            def pick_pair(first):
                tt(pick.rearrange("p c (e s) -> p c e s", e=2),
                   bc(bc(slot_ids[:], 1, 2), 1, TC),
                   bc(posx[:, :, first:first + 2], 3, SLOTS), ALU.is_equal).then_inc(S["pick_ready"], 1)

            def read_gather(n):
                dve.wait_ge(S["gathered"], n)
                copy(xg[:, 512:1024], bank(7)).then_inc(S["xg_ready"], 1)

            def read_gatherT(n):
                dve.wait_ge(S["xgT_psum"], n)
                copy(flat(xgT[:, 4:8, :]), bank(7)).then_inc(S["xgT_ready"], 1)

            pick_pair(0)
            read_gather(1)
            read_gatherT(1)
            n_rounds = dve.value_load(rounds_i[0:1, 0:1], min_val=1, max_val=T // SLOTS)
            with dve.Fori(0, n_rounds) as r:
                with dve.Fori(0, PAIRS) as p:
                    i = r * PAIRS + p
                    dve.wait_ge(S["pick_ready"], i + 1)
                    tt(pick_gate.rearrange("p c (e s) -> p c e s", e=2),
                       pick.rearrange("p c (e s) -> p c e s", e=2),
                       bc(gate[:, :, bass.ds(2 * p, 2)], 3, SLOTS), ALU.mult
                       ).then_inc(S["pick_gate_ready"], 1)
                    dve.wait_ge(S["pick_gate_ready"], i + 1)
                    tt(pick.rearrange("p c (e s) -> p c e s", e=2),
                       bc(bc(slot_ids[:], 1, 2), 1, TC),
                       bc(posx[:, :, bass.ds(2 * p + 2, 2)], 3, SLOTS), ALU.is_equal
                       ).then_inc(S["pick_ready"], 1)
                    dve.wait_ge(S["h_silu"], i + 1)
                    dve.wait_ge(S["w3_done"], i + 1)
                    tt(hS, gS, bank(5), ALU.mult).then_inc(S["h_ready"], 1)
                    read_gather(i + 2)
                    dve.wait_ge(S["hT_psum"], i + 1)
                    copy(flat(hT), bank(4))
                    copy(flat(pick_gateT), bank(5)[:, 0:256]).then_inc(S["hT_ready"], 1)
                    read_gatherT(i + 2)
                    dve.wait_ge(S["w2_done"], i + 1)
                    copy(yS[:, 512:1024], bank(5)).then_inc(S["y_ready"], 1)
                dve.wait_ge(S["pick_ready"], r * PAIRS + PAIRS + 1)
                ts(posx[:, :, 0:N_EXP], posx[:, :, 0:N_EXP], -float(SLOTS), None, ALU.add
                   ).then_inc(S["slots_moved"], 1)
                dve.wait_ge(S["slots_moved"], 2 * r + 1)
                ts(posx[:, :, N_EXP:], posx[:, :, 0:2], -float(SLOTS), None, ALU.add
                   ).then_inc(S["slots_moved"], 1)
                dve.wait_ge(S["slots_moved"], 2 * r + 2)

            dve.wait_ge(S["scattered"], n_rounds * PAIRS)
            for c in range(TC):
                for n in range(2):
                    last = copy(xin[:, c, n * 512:(n + 1) * 512], bank(2 * c + n))
                step(last)
                last = layer_norm(xin[:, c, :], 2, "y")
                step(last) if c == 0 else step(last, "y_final")


_INS = ['x', 'w_in', 'dn_conv_w', 'dn_a_log', 'dn_dt_bias', 'dn_norm_w', 'lru_conv_w', 'lru_conv_b',
        'lru_w_a', 'lru_b_a', 'lru_w_x', 'lru_b_x', 'lru_lambda', 'w_up_dn', 'w_up_sb', 'w_up_lru',
        'w_merge', 'b_merge', 'w_out', 'ln1_g', 'ln1_b', 'w_router', 'b_router', 'moe_w1', 'moe_w3',
        'moe_w2', 'ln2_g', 'ln2_b']
_OUTS = [((1, 256, 1024), 'float32')]


def kernel(**inputs):
    import numpy as _np
    import concourse.bacc as _bacc
    from concourse import mybir as _mybir
    from concourse.bass_utils import run_bass_kernel_spmd as _run

    nc = _bacc.Bacc("TRN2", target_bir_lowering=False, num_devices=1)
    arrays, args = {}, []
    for name in _INS:
        a = _np.ascontiguousarray(inputs[name])
        arrays[f"in_{name}_dram"] = a
        args.append(nc.dram_tensor(f"in_{name}_dram", a.shape, _mybir.dt.from_np(a.dtype),
                                   kind="ExternalInput").ap())
    for i, (shape, dtype) in enumerate(_OUTS):
        dt = _mybir.dt.from_np(_np.dtype(dtype))
        args.append(nc.dram_tensor(f"out_{i}_dram", shape, dt, kind="ExternalOutput").ap())
    hybrid_layer(nc, *args)
    r = _run(nc, [arrays], core_ids=[0])
    return r.results[0]["out_0_dram"]
```

```python
from contextlib import ExitStack

import concourse.bass as bass
from concourse import mybir

F32 = mybir.dt.float32
F32R = mybir.dt.float32r
I32 = mybir.dt.int32
ALU = mybir.AluOpType
ACT = mybir.ActivationFunctionType
AX_X = mybir.AxisListType.X

P = 128
D = 1024
T = 256
TC = T // P
KD = D // P
DN_H = 4
SB_H = 8
SB_D = 64
LRU_CH = 4
LRU_C = 8.0
TAPS = 4
N_EXP = 16
GROUPS = 4
PER_GROUP = N_EXP // GROUPS
FF = 512
KF = FF // P
SLOTS = 64
PAIRS = N_EXP // 2
ALPHA = 2.0 ** 0.25
LN_EPS = 1e-5
RMS_EPS = 1e-6
N_UP = 3

SLOT = 4096
DENSE_SLOTS = 3
RING = 6
UNIT = 2048
RAW_SLOTS = 4
HI_SLOTS = 2

C_DNW, C_LW, C_LCB, C_BA, C_BX, C_LAM, C_BM, C_NW = 0, 48, 64, 68, 72, 76, 80, 104
N_ROWS = 105

Q0, K0, V0, Z0, BA0 = 0, 512, 1024, 1536, 2048
SQ0, SK0, SV0, LX0, LY0 = 2056, 2568, 3080, 3592, 4104
PIECES = [("q", Q0), ("k", K0), ("v", V0), ("z", Z0), ("sq", SQ0), ("sk", SK0), ("sv", SV0),
          ("lx", LX0), ("ly", LY0)] + [("gate", 512 * n) for n in range(6)]
N_PROJ = len(PIECES)
N_UNIT = 2 * N_PROJ
N_UPS = 2 * N_UP
N_OUTS = 4
LEVELS = [2, 4, 8, 16, 32, 64]


def hybrid_layer(nc: bass.Bass, x, w_in, dn_conv_w, dn_a_log, dn_dt_bias, dn_norm_w, lru_conv_w,
                 lru_conv_b, lru_w_a, lru_b_a, lru_w_x, lru_b_x, lru_lambda, w_up_dn, w_up_sb,
                 w_up_lru, w_merge, b_merge, w_out, ln1_g, ln1_b, w_router, b_router, moe_w1,
                 moe_w3, moe_w2, ln2_g, ln2_b, out):
    with ExitStack() as ctx:
        def sb(name, shape, dt=F32):
            return ctx.enter_context(nc.sbuf_tensor(name, shape, dt))

        def sem(name):
            return ctx.enter_context(nc.semaphore(name))

        def flat(ap):
            names = "abcd"[:len(ap.shape) - 1]
            return ap.rearrange(f"p {' '.join(names)} -> p ({' '.join(names)})")

        def bc(ap, axis, n):
            a = ap.unsqueeze(axis)
            shape = list(a.shape)
            shape[axis] = n
            return a.broadcast_to(shape)

        def again(name, shape, off, dt=F32R):
            return nc.alloc_sbuf_tensor_at(name, shape, dt, offset=off)

        def here():
            return (nc.sbuf_base + 31) // 32 * 32

        ring_at = here()
        ring = sb("ring", [P, RING, SLOT])
        w_lo = again("w_lo", [P, RAW_SLOTS, UNIT], ring_at)
        w_hi = again("w_hi", [P, HI_SLOTS, UNIT], ring_at + 2 * SLOT * 4)
        held = again("held", [P, 6, 1024], ring_at + DENSE_SLOTS * SLOT * 4)
        y_hi = [held[:, n, :].rearrange("p (k t) -> p k t", t=T) for n in (3, 4, 1)]
        xh = sb("xh", [P, KD, T], F32R)
        xl = sb("xl", [P, KD, T], F32R)
        y_at = here()
        yT = sb("yT", [P, 3, 4, T])
        y_lo = again("y_lo", [P, 3, 4, T], y_at)
        pick_at = y_at + 4 * 2 * 1024
        pick_r = again("pick_r", [P, TC, P], pick_at)
        pickT = again("pickT", [P, TC, P], pick_at + 4 * TC * P)
        vc_at = here()
        vc = sb("vc", [P, DN_H, T])
        y_slot_hi = again("y_slot_hi", [P, D], vc_at)
        hold = flat(ring[:, DENSE_SLOTS:RING, :])
        raw = {}
        for n, name in enumerate(("q", "k", "v", "z", "sq", "sk")):
            raw[name] = hold[:, n * 1024:(n + 1) * 1024].rearrange("p (c t) -> p c t", c=4)
        raw["sv"], raw["lx"], raw["ly"] = raw["q"], raw["k"], raw["v"]
        vS = hold[:, 0:1024].rearrange("p (c n) -> p c n", c=TC)
        gates = hold[:, 6144:12288].rearrange("p (c t) -> p c t", c=24)
        xin = sb("xin", [P, TC, D])
        qk = sb("qk", [P, DN_H, 2, T])
        dn = sb("dn", [P, 8, 1024])
        tmp_at = here()
        tmp = sb("tmp", [P, 3, 1024])
        y_slot_lo = again("y_slot_lo", [P, D], tmp_at + 4 * 1024)
        small = sb("small", [P, 512])
        ident = sb("ident", [P, P])
        alpha_ident = sb("alpha_ident", [P, P])
        upper = sb("upper", [P, P])
        strict = sb("strict", [P, P])
        lower = sb("lower", [P, P])
        negtri = sb("negtri", [P, P])
        ones = sb("ones", [P, P])
        negones = sb("negones", [P, P])
        past_bias = sb("past_bias", [P, 3, P])
        level = sb("level", [P, 1 + len(LEVELS), P])
        level1T = sb("level1T", [P, P])
        slot_ids = sb("slot_ids", [P, SLOTS])
        before = sb("before", [P, PER_GROUP, PER_GROUP])
        rows = sb("rows", [P, P])
        cols = sb("cols", [P, P])
        w_ba = sb("w_ba", [P, KD, 8])
        ba_hi = sb("ba_hi", [P, KD, 8], F32R)
        ba_lo = sb("ba_lo", [P, KD, 8], F32R)
        w_rt = sb("w_rt", [P, KD, N_EXP])
        w_bd = sb("w_bd", [P, 2, LRU_CH, P])
        eps = sb("eps", [P, 2])
        eps_ln, eps_rms = eps[:, 0:1], eps[:, 1:2]
        heads4 = sb("heads4", [P, 2, 4])
        b_rt = sb("b_rt", [P, N_EXP])
        rounds_i = sb("rounds_i", [P, 1], I32)
        tinyT = sb("tinyT", [N_EXP, T])

        def dn4(n):
            return dn[:, n, :].rearrange("p (c h t) -> p c h t", c=TC, h=DN_H)

        def dnh(n, half):
            return dn[:, n, half * 512:(half + 1) * 512].rearrange("p (h t) -> p h t", h=DN_H)

        vb = dn4(0)
        kdec, V0 = dnh(1, 0), dnh(1, 1)
        dec = dn4(2)
        R, V1 = dnh(2, 0), dnh(2, 1)
        AT, M, MT, XS, QKT = (dn4(n) for n in range(3, 8))
        decT = XS
        Amat = flat(vc[:]).rearrange("p (c h t) -> p c h t", c=TC, h=DN_H)
        qe = flat(vc[:])[:, 0:512].rearrange("p (h t) -> p h t", h=DN_H)
        norms = tmp[:, 0:2, :]
        eG1 = tmp[:, 2, 0:512].rearrange("p (h t) -> p h t", h=DN_H)
        S1 = tmp[:, 2, 512:1024].rearrange("p (h t) -> p h t", h=DN_H)
        zs = flat(dn[:, 0:3, :]).rearrange("p (h n) -> p h n", h=SB_H)
        att = flat(dn[:, 3:6, :]).rearrange("p (h n) -> p h n", h=SB_H)
        xc = flat(qk[:, 0:2]).rearrange("p (c t) -> p c t", c=4)
        lr = flat(qk[:, 2:4]).rearrange("p (c t) -> p c t", c=4)
        li = vc[:]
        la = dn[:, 6, :].rearrange("p (c t) -> p c t", c=4)
        far = dn[:, 7, :]
        lw, lq = tmp[:, 0, :], tmp[:, 1, :]
        merged = flat(dn[:, 0:2, :]).rearrange("p (m t) -> p m t", t=T)
        x1 = dn[:, 2:4, :]
        ln_gb = dn[:, 4:8, :]
        xg = flat(qk[:])[:, 0:1024]
        xgT = flat(qk[:])[:, 1024:2048].rearrange("p (k s) -> p k s", k=KD)
        x1T = flat(qk[:]).rearrange("p (k t) -> p k t", t=T)
        x1h, x1l = (flat(m[:]).rearrange("p (c d) -> p c d", c=TC) for m in (xh, xl))
        yflat = flat(yT[:])
        hS, gS = yflat[:, 0:512], yflat[:, 512:1024]
        hT = yflat[:, 1024:1536].rearrange("p (k s) -> p k s", k=KF)
        pick_gate = yflat[:, 1536:1792].rearrange("p (c s) -> p c s", c=TC)
        pick = pick_r[:].bitcast(F32)

        def sm(a, n):
            return small[:, a:a + n]

        v12, e12, z12, q12, sp12, m12 = (sm(12 * i, 12) for i in range(6))
        beta, g, gc, eg, kds = (sm(72 + 8 * i, 8) for i in range(5))
        ea, n8, negbeg = sm(112, 4), sm(116, 4), sm(120, 4)
        stats = sm(124, 12)
        mv = sm(136, 2)
        rstd = sm(138, 1)
        logit, score, sel, chosen, mask, tk = (sm(140 + 32 * i, 32) for i in range(6))
        mx, sume = sm(332, 2), sm(334, 2)
        gsum, gsel = sm(336, 8), sm(344, 8)
        posx = sm(352, 36).rearrange("p (c e) -> p c e", c=TC)
        gate = sm(388, 36).rearrange("p (c e) -> p c e", c=TC)
        cnt, rnd, slot_gate = sm(424, 1), sm(425, 4), sm(429, 1)
        shift = sm(430, 1)
        cmp1, cmp2 = tmp[:, 0, 0:128], tmp[:, 0, 128:256]

        ps = ctx.enter_context(nc.psum_tensor("ps", [P, 8, 512], F32))

        def bank(b):
            return ps[:, b, :]

        def heads(b):
            return bank(b).rearrange("p (h t) -> p h t", h=4)

        S = {n: sem(n) for n in """x_in rows_in small_in bd_in bd_zeroed ln_in out_stored consts
            xT_psum rows_psum ident_ready xh_ready xl_ready hi_ready lo_first lo_ready ba_hi_ready ba_split
            cols_ready ba_psum ba_copied ba_tok
            unit_psum unit_read conv_done silu_done z_silu
            g_abs g_exp g_ready gb_psum gc_ready diff_ready dec_ready dec_masked sq_ready ss_psum y_split x1h_ready x1_split
            rn_ready qk_ready tok_psum tok_ready kk_psum a_ready at_psum at_ready
            inv_x inv_xs inv_z inv_m inv_t inv_mt v0_psum v0_ready s1_psum s1_ready ks_psum
            r_ready v1_psum v1_ready o_psum o_sq oss_psum o_rms ya_ready sv_psum sv_ready slot_gate_ready y_lo_ready
            z_psum z_log z_sp z_masked r_psum r_min att_ready yb_psum yb_ready
            xc_ready lru_gate lru_a lru_near lru_var lru_b yc_scan gelu_ready yc_ready gates_ready
            up_psum merged_ready mix_psum ln_var ln_rstd ln_shift y_norm x1_ready x1T_psum x1T_ready_act
            x1T_ready_dve rt_psum sm_in sm_exp mask_ready pos_psum rounds_ready
            pick_ready pick_gate_ready gathered xg_ready xgT_psum xgT_ready w1_done w3_done w2_done
            slots_moved h_silu h_ready hT_psum hT_ready y_ready scattered y_final
            dve_order act_order pool_order""".split()}
        unit_loaded = [sem(f"unit_loaded_{i}") for i in range(RAW_SLOTS)]
        slot_loaded = [sem(f"slot_loaded_{i}") for i in range(RING)]

        block = ctx.enter_context(nc.Block())

        def in_order(eng, order):
            count = {}

            def step(ins, name=order, n=1):
                count[name] = count.get(name, 0) + n
                ins.then_inc(S[name], n)
                eng.wait_ge(S[name], count[name])
            return step

        LRU_UNITS = {26: ("ga", 0), 27: ("ga", 2), 28: ("gx", 0), 29: ("gx", 2)}
        n_dense = [n for n in range(N_UNIT + 4) if n not in LRU_UNITS]

        def unit(u):
            if u in LRU_UNITS:
                kind, c = LRU_UNITS[u]
                return kind, (lr if kind == "ga" else li), c, None
            n = n_dense.index(u)
            name, col = PIECES[n // 2]
            first = 2 * (n % 2)
            if name == "gate":
                return name, gates, col // P + first, n
            return name, raw[name], first, n

        N_ALL = N_UNIT + 4
        w_up = [w_up_dn, w_up_sb, w_up_lru]
        UP0, OUT0 = N_UNIT, N_UNIT + N_UPS
        N_DENSE = OUT0 + N_OUTS

        def raw_unit(n):
            return ring[:, n % RAW_SLOTS // 2, n % 2 * UNIT:(n % 2 + 1) * UNIT]

        def wait_used(eng, n):
            if n < UP0:
                eng.wait_ge(S["unit_psum"], n_dense[n] + 1)
            else:
                eng.wait_ge(S["up_psum"], n - UP0 + 1)

        def wait_unit_loaded(eng, n):
            eng.wait_ge(unit_loaded[n % RAW_SLOTS], 16 * (n // RAW_SLOTS + 1))

        @block.sync
        def _(sp):
            sp.dma_start(xin[:], x[0].rearrange("(c p) d -> p c d", p=P)).then_inc(S["x_in"], 16)
            for n in range(N_DENSE):
                if n >= RAW_SLOTS:
                    wait_used(sp, n - RAW_SLOTS)
                dst = raw_unit(n)
                if n < UP0:
                    name, col = PIECES[n // 2]
                    col += 256 * (n % 2)
                    w = w_merge if name == "gate" else w_in
                    src = w[0, :, col:col + 256].rearrange("(p k) n -> p k n", k=KD)
                elif n < OUT0:
                    o = (n - UP0) % 2 * 512
                    src = w_up[(n - UP0) // 2][0, :, o:o + 512].rearrange("(k p) n -> p k n", p=P)
                else:
                    k, o = (n - OUT0) // 2 * 4, (n - OUT0) % 2 * 512
                    src = w_out[0, k * P:(k + 4) * P, o:o + 512].rearrange("(k p) n -> p k n", p=P)
                if n == 1:
                    sp.wait_ge(S["x_in"], 16)
                sp.dma_start(dst.rearrange("p (k n) -> p k n", k=src.shape[1]), src
                             ).then_inc(unit_loaded[n % RAW_SLOTS], 16)

            def expert_load(slot, pair):
                w = (moe_w1, moe_w3, moe_w2)[slot // 2]
                k = KF if slot >= 4 else KD
                src = w[0].rearrange("(a b) (p k) n -> a b p (k n)", b=2, k=k)
                sp.dma_start(ring[:, slot, :], src[pair, slot % 2]).then_inc(slot_loaded[slot], 16)

            sp.wait_ge(S["up_psum"], N_UPS)
            expert_load(2, 0)
            sp.wait_ge(S["merged_ready"], N_UPS)
            for slot in (3, 4, 5):
                expert_load(slot, 0)
            sp.wait_ge(S["mix_psum"], TC)
            for slot in (0, 1):
                expert_load(slot, 0)

            def pair_loads(pair, used):
                for slot, done in enumerate(("w1_done", "w1_done", "w3_done", "w3_done",
                                             "w2_done", "w2_done")):
                    sp.wait_ge(S[done], used)
                    expert_load(slot, pair)

            with sp.Fori(1, PAIRS) as p:
                pair_loads(p, p)
            sp.wait_ge(S["rounds_ready"], 1)
            n_rounds = sp.value_load(rounds_i[0:1, 0:1], min_val=1, max_val=T // SLOTS)
            with sp.If(n_rounds > 1):
                with sp.Fori(1, n_rounds) as r:
                    with sp.Fori(0, PAIRS) as p:
                        pair_loads(p, r * PAIRS + p)
            for c in range(TC):
                sp.wait_ge(S["y_final"], c + 1)
                sp.dma_start(out[0, c * P:(c + 1) * P, :], xin[:, c, :]).then_inc(S["out_stored"], 16)
            sp.wait_ge(S["out_stored"], 16 * TC)

        LO_FIRST = 2

        @block.gpsimd
        def _(pool):
            step = in_order(pool, "pool_order")
            step(nc.gpsimd.memset(ident[:], 0.0))
            step(nc.gpsimd.affine_select(out=ident[:], in_=ident[:], compare_op=ALU.not_equal, fill=1.0,
                                         base=0, pattern=[[-1, P]], channel_multiplier=1), "ident_ready")
            step(nc.gpsimd.memset(w_bd[:], 0.0), "bd_zeroed")
            nc.gpsimd.memset(ones[:], 1.0)
            nc.gpsimd.memset(negones[:], -1.0)
            nc.gpsimd.memset(alpha_ident[:], 0.0)
            nc.gpsimd.memset(past_bias[:], 0.0)
            nc.gpsimd.memset(eps_ln, LN_EPS)
            nc.gpsimd.memset(eps_rms, RMS_EPS)
            nc.gpsimd.memset(level1T[:], 0.0)
            nc.gpsimd.memset(before[:], 1.0)
            step(nc.gpsimd.memset(level[:], 0.0))
            nc.gpsimd.affine_select(out=alpha_ident[:], in_=alpha_ident[:], compare_op=ALU.not_equal,
                                    fill=ALPHA, base=0, pattern=[[-1, P]], channel_multiplier=1)
            for m, src, op, up in ((upper, ones, ALU.is_ge, 1), (strict, ones, ALU.is_gt, 1),
                                   (lower, ones, ALU.is_gt, -1), (negtri, negones, ALU.is_ge, -1)):
                nc.gpsimd.affine_select(out=m[:], in_=src[:], compare_op=op, fill=0.0, base=0,
                                        pattern=[[up, P]], channel_multiplier=-up)
            for n in (0, 2):
                nc.gpsimd.affine_select(out=past_bias[:, n, :], in_=past_bias[:, n, :],
                                        compare_op=ALU.is_gt, fill=-1e30, base=0,
                                        pattern=[[1, P]], channel_multiplier=-1)
            nc.gpsimd.affine_select(out=before[:], in_=before[:], compare_op=ALU.is_gt, fill=0.0,
                                    base=0, pattern=[[1, PER_GROUP], [-1, PER_GROUP]],
                                    channel_multiplier=0)
            nc.gpsimd.iota(slot_ids[:], pattern=[[1, SLOTS]], base=0, channel_multiplier=0,
                           allow_small_or_imprecise_dtypes=True)

            def left_half(n, size):
                return level[:, n, :].rearrange("p (b a s) -> p b a s", a=2, s=size)[:, :, 0, :]

            for n, size in enumerate([1] + LEVELS):
                nc.gpsimd.affine_select(
                    out=left_half(n, size), in_=ones[:, 0:P // 2].rearrange("p (b s) -> p b s", s=size),
                    compare_op=ALU.is_ge, fill=0.0, base=-size,
                    pattern=[[-2 * size, P // (2 * size)], [0, size]], channel_multiplier=1)
            right1 = level1T[:].rearrange("p (b a) -> p b a", a=2)[:, :, 1]
            step(nc.gpsimd.affine_select(out=right1, in_=ones[:, 0:P // 2], compare_op=ALU.not_equal,
                                         fill=0.0, base=0, pattern=[[-2, P // 2]],
                                         channel_multiplier=1))
            step(nc.gpsimd.tensor_tensor(right1, ones[:, 0:P // 2], right1, ALU.subtract))
            for n, size in enumerate([1] + LEVELS):
                end = nc.gpsimd.affine_select(
                    out=left_half(n, size), in_=left_half(n, size), compare_op=ALU.is_ge, fill=0.0,
                    base=2 * size - 1, pattern=[[2 * size, P // (2 * size)], [0, size]],
                    channel_multiplier=-1)
            step(end, "consts")

            def split_lo(n):
                pool.wait_ge(S["hi_ready"], n + 1)
                step(nc.gpsimd.tensor_tensor(w_lo[:, n % RAW_SLOTS, :], raw_unit(n),
                                             w_hi[:, n % HI_SLOTS, :].bitcast(F32), ALU.subtract), "lo_ready")

            for n in range(LO_FIRST, 10):
                split_lo(n)
            pool.wait_ge(S["dec_ready"], 1)
            d8 = dec.rearrange("p c h t -> p (c h) t")
            dT8 = decT.rearrange("p c h t -> p (c h) t")
            step(nc.gpsimd.tensor_tensor(d8, d8, bc(lower[:], 1, 8), ALU.mult), "dec_masked")
            step(nc.gpsimd.tensor_tensor(dT8, dT8, bc(upper[:], 1, 8), ALU.mult), "dec_masked")
            for n in range(10, OUT0):
                split_lo(n)
            pool.wait_ge(S["yb_psum"], 1)
            pool.wait_ge(S["yc_ready"], 1)
            for n, w in enumerate((ln1_g, ln1_b, ln2_g, ln2_b)):
                pool.dma_start(ln_gb[:, n, :], w[0].partition_broadcast(P)).then_inc(S["ln_in"], 16)
            for c in range(TC):
                pool.wait_ge(S["x1h_ready"], c + 1)
                step(nc.gpsimd.tensor_tensor(x1l[:, c, :], x1[:, c, :], x1h[:, c, :].bitcast(F32),
                                             ALU.subtract), "x1_split")

        @block.scalar
        def _(act):
            step = in_order(act, "act_order")

            for first, n, src in ((C_DNW, 48, dn_conv_w[0].rearrange("w (c p) -> w c p", p=P)),
                                  (C_LW, 16, lru_conv_w[0].rearrange("w (c p) -> w c p", p=P)),
                                  (C_LCB, 4, lru_conv_b[0].rearrange("(c p) -> c p", p=P)),
                                  (C_BA, 4, lru_b_a[0].rearrange("(c p) -> c p", p=P)),
                                  (C_BX, 4, lru_b_x[0].rearrange("(c p) -> c p", p=P)),
                                  (C_LAM, 4, lru_lambda[0].rearrange("(c p) -> c p", p=P)),
                                  (C_BM, 24, b_merge[0].rearrange("(c p) -> c p", p=P)),
                                  (C_NW, 1, dn_norm_w)):
                if len(src.shape) == 3:
                    src = src.rearrange("w c p -> (w c) p")
                act.dma_start(rows[first:first + n, :], src).then_inc(S["rows_in"], 16)
            act.dma_start(w_ba[:], w_in[0, :, BA0:BA0 + 8].rearrange("(p k) n -> p k n", k=KD)
                          ).then_inc(S["small_in"], 16)
            act.dma_start(w_rt[:], w_router.rearrange("(p k) n -> p k n", k=KD)
                          ).then_inc(S["small_in"], 16)
            act.dma_start(heads4[:, 0, :], dn_a_log[0].partition_broadcast(P)).then_inc(S["small_in"], 16)
            act.dma_start(heads4[:, 1, :], dn_dt_bias[0].partition_broadcast(P)).then_inc(S["small_in"], 16)
            act.dma_start(b_rt[:], b_router.partition_broadcast(P)).then_inc(S["small_in"], 16)
            def split_hi(n):
                if n >= UP0 + HI_SLOTS:
                    wait_used(act, n - HI_SLOTS)
                wait_unit_loaded(act, n)
                nc.scalar.activation(w_hi[:, n % HI_SLOTS, :], raw_unit(n), ACT.Copy
                                     ).then_inc(S["hi_ready"], 1)

            for b in range(4):
                act.wait_ge(S["xT_psum"], b + 1)
                nc.scalar.activation(flat(xh[:, 2 * b:2 * b + 2, :]), bank(b), ACT.Copy
                                     ).then_inc(S["xh_ready"], 1)
            split_hi(0)
            act.wait_ge(S["small_in"], 16 * 5)
            nc.scalar.activation(ba_hi[:], w_ba[:], ACT.Copy).then_inc(S["ba_hi_ready"], 1)
            split_hi(1)

            act.wait_ge(S["bd_zeroed"], 1)
            for n, w in enumerate((lru_w_a, lru_w_x)):
                for half in range(2):
                    o = 64 * half
                    act.dma_start(w_bd[o:o + 64, n, :, o:o + 64],
                                  w[0].rearrange("(c h) i o -> h i c o", h=2)[half]
                                  ).then_inc(S["bd_in"], 16)

            def read_unit(u):
                kind, dst, c, n = unit(u)
                act.wait_ge(S["unit_psum"], u + 1)
                if kind in ("sv", "lx", "ly"):
                    act.wait_ge(S["conv_done"], 6)
                if kind in ("gate", "ga", "gx"):
                    act.wait_ge(S["cols_ready"], 1)
                    b = {"gate": C_BM, "ga": C_BA, "gx": C_BX}[kind] + c
                    for j in range(2):
                        ins = nc.scalar.activation(dst[:, c + j, :], bank(u % 3)[:, j * T:(j + 1) * T],
                                                   ACT.Identity, bias=cols[:, b + j:b + j + 1])
                else:
                    ins = nc.scalar.activation(flat(dst[:, c:c + 2, :]), bank(u % 3), ACT.Copy,
                                               scale=SB_D ** -0.5 if kind == "sq" else 1.0)
                step(ins, "unit_read")
                if n is not None:
                    split_hi(n + HI_SLOTS)

            def silu(v):
                act.wait_ge(S["conv_done"], v + 1)
                kind, c = v // 2, 2 * (v % 2)
                t = vc[:, c:c + 2, :] if kind == 2 else qk[:, c:c + 2, 1 - kind, :]
                step(nc.scalar.activation(t, t, ACT.Silu), "silu_done")

            read_unit(0)
            act.wait_ge(S["g_abs"], 1)
            step(nc.scalar.activation(beta.rearrange("p (c h) -> p c h", c=TC),
                                      bank(7)[:, 256:272].rearrange("p (c e) -> p c e", c=TC)[:, :, 0:4],
                                      ACT.Exp, scale=-1.0))
            step(nc.scalar.activation(ea, heads4[:, 0, :], ACT.Exp))
            step(nc.scalar.activation(e12, e12, ACT.Exp, scale=-1.0), "g_exp")
            for u in range(1, 6):
                read_unit(u)
                silu(u - 1)
            silu(5)
            for n in range(2):
                step(nc.scalar.activation(norms[:, n, :], flat(qk[:, 2 * n:2 * n + 2]), ACT.Square),
                     "sq_ready")
            read_unit(6)
            read_unit(7)
            step(nc.scalar.activation(flat(raw["z"]), flat(raw["z"]), ACT.Silu), "z_silu")
            nc.scalar.preload_act_table_set("natural_log_exp_and_others")
            act.wait_ge(S["gc_ready"], 1)
            step(nc.scalar.activation(eg, gc, ACT.Exp))
            act.wait_ge(S["diff_ready"], 1)
            step(nc.scalar.activation(eG1, heads(4), ACT.Exp))
            step(nc.scalar.activation(kds[:, 0:4], kds[:, 0:4], ACT.Exp))
            step(nc.scalar.activation(flat(dec), flat(dec), ACT.Exp, scale=-1.0))
            step(nc.scalar.activation(flat(decT), flat(decT), ACT.Exp), "dec_ready")
            read_unit(8)
            for n in range(2):
                act.wait_ge(S["ss_psum"], n + 1)
                for b in range(2):
                    step(nc.scalar.activation(norms[:, n, b * 512:(b + 1) * 512],
                                              bank((5, 3)[n] + b), ACT.Ln, bias=eps_rms))
                step(nc.scalar.activation(norms[:, n, :], norms[:, n, :], ACT.Exp, scale=-0.5),
                     "rn_ready")
            for u in (9, 10, 11):
                read_unit(u)
            act.wait_ge(S["at_psum"], 1)
            for c in range(TC):
                step(nc.scalar.activation(flat(AT[:, c]), bank(3 + c), ACT.Copy), "at_ready")
            read_unit(12)
            for n in range(len(LEVELS)):
                for c in range(TC):
                    act.wait_ge(S["inv_t"], TC * n + c + 1)
                    step(nc.scalar.activation(flat(MT[:, c]), bank(3 + 2 * c), ACT.Copy), "inv_mt")
                read_unit(13 + n)
            act.wait_ge(S["s1_psum"], 1)
            step(nc.scalar.activation(flat(S1), bank(4), ACT.Copy), "s1_ready")
            act.wait_ge(S["o_psum"], 1)
            for b in range(2):
                step(nc.scalar.activation(norms[:, 0, b * 512:(b + 1) * 512], bank(5 + b), ACT.Square),
                     "o_sq")
            act.wait_ge(S["oss_psum"], 1)
            for b in range(2):
                step(nc.scalar.activation(norms[:, 1, b * 512:(b + 1) * 512], bank(3 + b), ACT.Ln,
                                          bias=eps_rms, scale=1.0 / P))
            step(nc.scalar.activation(norms[:, 1, :], norms[:, 1, :], ACT.Exp, scale=-0.5), "o_rms")
            read_unit(19)
            read_unit(20)
            act.wait_ge(S["sv_psum"], 1)
            for c in range(TC):
                step(nc.scalar.activation(vS[:, c, :], bank(3 + c), ACT.Copy), "sv_ready")
            read_unit(21)

            for k in range(SB_H + 2):
                if k < SB_H:
                    act.wait_ge(S["z_psum"], k + 1)
                    step(nc.scalar.activation(zs[:, k, :], bank(3 + k % 3)[:, 0:T + P], ACT.Abs))
                    step(nc.scalar.activation(zs[:, k, :], zs[:, k, :], ACT.Exp, scale=-1.0))
                    step(nc.scalar.activation(zs[:, k, :], zs[:, k, :], ACT.Ln, bias=1.0), "z_log")
                if k >= 2:
                    act.wait_ge(S["r_min"], k - 1)
                    step(nc.scalar.activation(att[:, k - 2, :], att[:, k - 2, :], ACT.Exp), "att_ready")
                if k < SB_H:
                    read_unit(22 + k)
            for b in range(2):
                act.wait_ge(S["yb_psum"], 1)
                step(nc.scalar.activation(flat(y_hi[1][:, 2 * b:2 * b + 2, :]), bank(6 + b), ACT.Copy),
                     "yb_ready")
            lrf = flat(lr)
            for t in (lrf, flat(li)):
                step(nc.scalar.activation(t, t, ACT.Exp, scale=-1.0))
                step(nc.scalar.activation(t, t, ACT.Ln, bias=1.0))
                step(nc.scalar.activation(t, t, ACT.Exp, scale=-1.0), "lru_gate")
            read_unit(30)
            act.wait_ge(S["lru_near"], 1)
            step(nc.scalar.activation(flat(la), lrf, ACT.Exp))
            step(nc.scalar.activation(far, lrf, ACT.Exp, scale=2.0))
            step(nc.scalar.activation(lq, lw, ACT.Exp), "lru_a")
            read_unit(31)
            step(nc.scalar.activation(flat(raw["ly"]), flat(raw["ly"]), ACT.Gelu_apprx_tanh),
                 "gelu_ready")
            read_unit(32)
            read_unit(33)
            for n in range(N_UP):
                o = n * 8 * T
                part = flat(gates)[:, o:o + 8 * T]
                step(nc.scalar.activation(part, part, ACT.Sigmoid), "gates_ready")
            split_hi(UP0 + 2)
            act.wait_ge(S["lru_var"], 1)
            step(nc.scalar.activation(far, far, ACT.Sqrt), "lru_b")
            for n in range(UP0 + 3, OUT0):
                split_hi(n)

            nc.scalar.preload_act_table_set("natural_log_exp_and_others")

            def inv_std(n):
                act.wait_ge(S["ln_var"], n + 1)
                step(nc.scalar.activation(rstd, mv[:, 1:2], ACT.Ln, bias=eps_ln))
                step(nc.scalar.activation(rstd, rstd, ACT.Exp, scale=-0.5), "ln_rstd")

            for c in range(TC):
                inv_std(c)
            for c in range(TC):
                act.wait_ge(S["x1T_psum"], 2 * c + 1)
                nc.scalar.activation(x1T[:, 0:4, c * P:(c + 1) * P], heads(4 + 2 * c), ACT.Copy
                                     ).then_inc(S["x1T_ready_act"], 1)
            for c in range(TC):
                nc.scalar.activation(x1h[:, c, :], x1[:, c, :], ACT.Copy).then_inc(S["x1h_ready"], 1)
            act.wait_ge(S["sm_in"], 1)
            step(nc.scalar.activation(score, score, ACT.Exp), "sm_exp")

            def read_gather(n):
                act.wait_ge(S["gathered"], n)
                nc.scalar.activation(xg[:, 0:512], bank(6), ACT.Copy).then_inc(S["xg_ready"], 1)

            def read_gatherT(n):
                act.wait_ge(S["xgT_psum"], n)
                nc.scalar.activation(flat(xgT[:, 0:4, :]), bank(6), ACT.Copy).then_inc(S["xgT_ready"], 1)

            nc.scalar.preload_act_table(ACT.Silu)
            read_gather(1)
            read_gatherT(1)
            act.wait_ge(S["rounds_ready"], 1)
            n_rounds = act.value_load(rounds_i[0:1, 0:1], min_val=1, max_val=T // SLOTS)
            with act.Fori(0, n_rounds) as r:
                with act.Fori(0, PAIRS) as p:
                    i = r * PAIRS + p
                    act.wait_ge(S["w1_done"], i + 1)
                    nc.scalar.activation(gS, bank(4), ACT.Silu).then_inc(S["h_silu"], 1)
                    read_gather(i + 2)
                    read_gatherT(i + 2)
                    act.wait_ge(S["w2_done"], i + 1)
                    act.wait_ge(S["slot_gate_ready"], i + 1)
                    for half in range(2):
                        nc.scalar.activation(y_slot_hi[:, half * 512:(half + 1) * 512], bank(4 + half),
                                             ACT.Copy, scale=slot_gate).then_inc(S["y_ready"], 1)
            nc.scalar.preload_act_table_set("natural_log_exp_and_others")
            for c in range(TC):
                inv_std(TC + c)
                act.wait_ge(S["ln_shift"], c + 1)
                for n in range(2):
                    nc.scalar.activation(xin[:, c, n * 512:(n + 1) * 512], bank(2 * c + n), ACT.Identity,
                                         bias=shift, scale=rstd).then_inc(S["y_norm"], 1)

        @block.tensor
        def _(pe):
            mm = nc.tensor.matmul

            def tr(dst, src):
                k = src.shape[0]
                return nc.tensor.transpose(dst, src, ident[0:k, 0:k])

            pe.wait_ge(S["ident_ready"], 1)
            pe.wait_ge(S["x_in"], 16)
            for k in range(KD):
                for c in range(TC):
                    last = tr(bank(k // 2)[:, (k % 2) * T + c * P:(k % 2) * T + (c + 1) * P],
                              xin[:, c, k:D:KD])
                if k % 2:
                    last.then_inc(S["xT_psum"], 1)
            pe.wait_ge(S["xh_ready"], 4)
            pe.wait_ge(S["xl_ready"], 4)

            def wait_lo(n):
                if n < LO_FIRST:
                    pe.wait_ge(S["lo_first"], n + 1)
                else:
                    pe.wait_ge(S["lo_ready"], n - LO_FIRST + 1)

            def split_products(n, dst, w_cols, ks, x_hi, x_lo, N_cols=T):
                wh, wl = (t.rearrange("p (k n) -> p k n", k=ks)
                          for t in (w_hi[:, n % HI_SLOTS, :], w_lo[:, n % RAW_SLOTS, :]))
                pe.wait_ge(S["hi_ready"], n + 1)
                for j, o in enumerate(w_cols):
                    for k in range(ks):
                        for rhs in (x_hi, x_lo):
                            mm(dst[j], wh[:, k, o:o + P], rhs[:, k, :],
                               start=(k == 0 and rhs is x_hi and j % 2 == 0), stop=False,
                               skip_group_check=True)
                wait_lo(n)
                for j, o in enumerate(w_cols):
                    for k in range(ks):
                        last = mm(dst[j], wl[:, k, o:o + P], x_hi[:, k, :], start=False,
                                  stop=(k == ks - 1), skip_group_check=True)
                return last

            def run_unit(u):
                kind, _, c, n = unit(u)
                if u >= 3:
                    pe.wait_ge(S["unit_read"], u - 2)
                if n is None:
                    pe.wait_ge(S["xc_ready"], 4)
                    pe.wait_ge(S["bd_in"], 16 * 4)
                    for j in range(2):
                        last = mm(bank(u % 3)[:, j * T:(j + 1) * T],
                                  w_bd[:, 0 if kind == "ga" else 1, c + j, :], xc[:, c + j, :],
                                  start=True, stop=True)
                else:
                    last = split_products(n, [bank(u % 3)[:, j * T:(j + 1) * T] for j in range(2)],
                                          (0, P), KD, xh, xl)
                last.then_inc(S["unit_psum"], 1)

            run_unit(0)
            pe.wait_ge(S["rows_in"], 16 * 8)
            tr(bank(6)[:, 0:N_ROWS], rows[0:N_ROWS, :]).then_inc(S["rows_psum"], 1)
            pe.wait_ge(S["ba_split"], 1)
            for c in range(TC):
                t = slice(c * P, (c + 1) * P)
                for k in range(KD):
                    for n, (a, b) in enumerate(((xh, ba_hi), (xh, ba_lo), (xl, ba_hi))):
                        last = mm(bank(7)[:, 256 + 8 * c:264 + 8 * c], a[:, k, t], b[:, k, :],
                                  start=(k == 0 and n == 0), stop=(k == KD - 1 and n == 2))
            last.then_inc(S["ba_tok"], 1)
            for u in range(1, 5):
                run_unit(u)

            pe.wait_ge(S["consts"], 1)
            pe.wait_ge(S["g_ready"], 1)
            for c in range(TC):
                mm(bank(7)[:, 272 + 4 * c:276 + 4 * c], upper[:], g[:, 4 * c:4 * c + 4],
                   start=True, stop=True)
            for c in range(TC):
                for h in range(DN_H):
                    last = mm(heads(3 + c)[:, h, :],
                              g[:, 4 * c + h:4 * c + h + 1].broadcast_to([P, P]), upper[:],
                              start=True, stop=True)
            last.then_inc(S["gb_psum"], 1)
            for u in range(5, 9):
                run_unit(u)

            for n in range(2):
                pe.wait_ge(S["sq_ready"], n + 1)
                if n == 1:
                    pe.wait_ge(S["dec_ready"], 1)
                for b in range(2):
                    last = mm(bank((5, 3)[n] + b), ones[:], norms[:, n, b * 512:(b + 1) * 512],
                              start=True, stop=True)
                last.then_inc(S["ss_psum"], 1)
            run_unit(9)

            pe.wait_ge(S["qk_ready"], 1)
            for h in range(DN_H):
                tr(heads(3)[:, h, :], qk[:, h, 0, 0:P])
            for c in range(TC):
                for h in range(DN_H):
                    last = tr(heads(5 + c)[:, h, :], vc[:, h, c * P:(c + 1) * P])
            last.then_inc(S["tok_psum"], 1)
            run_unit(10)

            pe.wait_ge(S["tok_ready"], 1)
            for c in range(TC):
                for h in range(DN_H):
                    last = mm(bank(3 + 2 * c + h // 2).rearrange("p (a b t) -> p a b t", a=2, b=2)[:, h % 2],
                              qk[:, h, 0, c * P:(c + 1) * P], qk[:, h, :, c * P:(c + 1) * P],
                              start=True, stop=True)
            last.then_inc(S["kk_psum"], 1)
            run_unit(11)
            pe.wait_ge(S["a_ready"], 1)
            for c in range(TC):
                for h in range(DN_H):
                    last = tr(heads(3 + c)[:, h, :], Amat[:, c, h, :])
            last.then_inc(S["at_psum"], 1)
            run_unit(12)

            pe.wait_ge(S["at_ready"], TC)
            for n in range(len(LEVELS)):
                for c in range(TC):
                    pe.wait_ge(S["inv_m"], TC * n + c + 1)
                    if n:
                        pe.wait_ge(S["inv_mt"], TC * (n - 1) + c + 1)
                    for h in range(DN_H):
                        last = mm(heads(3 + 2 * c)[:, h, :], AT[:, c, h, :], M[:, c, h, :],
                                  start=True, stop=True)
                    last.then_inc(S["inv_x"], 1)
                for c in range(TC):
                    pe.wait_ge(S["inv_xs"], TC * n + c + 1)
                    for h in range(DN_H):
                        last = mm(heads(4 + 2 * c)[:, h, :], MT[:, c, h, :], XS[:, c, h, :],
                                  start=True, stop=True)
                    last.then_inc(S["inv_z"], 1)
                run_unit(13 + n)
                for c in range(TC):
                    pe.wait_ge(S["inv_m"], TC * (n + 1) + c + 1)
                    for h in range(DN_H):
                        last = tr(heads(3 + 2 * c)[:, h, :], M[:, c, h, :])
                    last.then_inc(S["inv_t"], 1)

            pe.wait_ge(S["inv_mt"], TC * len(LEVELS))
            for h in range(DN_H):
                last = mm(heads(3)[:, h, :], MT[:, 0, h, :], vb[:, 0, h, :], start=True, stop=True)
            last.then_inc(S["v0_psum"], 1)
            pe.wait_ge(S["v0_ready"], 1)
            for h in range(DN_H):
                last = mm(heads(4)[:, h, :], kdec[:, h, :], V0[:, h, :], start=True, stop=True)
            last.then_inc(S["s1_psum"], 1)

            def o_part(c, h):
                return bank(5 + h // 2).rearrange("p (a c t) -> p a c t", a=2, c=TC)[:, h % 2, c, :]

            for h in range(DN_H):
                mm(o_part(0, h), V0[:, h, :], QKT[:, 0, h, :], start=True, stop=True)
            pe.wait_ge(S["s1_ready"], 1)
            for h in range(DN_H):
                last = mm(heads(3)[:, h, :], qk[:, h, 0, P:T], S1[:, h, :], start=True, stop=True)
            last.then_inc(S["ks_psum"], 1)
            pe.wait_ge(S["r_ready"], 1)
            for h in range(DN_H):
                last = mm(heads(4)[:, h, :], MT[:, 1, h, :], R[:, h, :], start=True, stop=True)
            last.then_inc(S["v1_psum"], 1)
            pe.wait_ge(S["v1_ready"], 1)
            for h in range(DN_H):
                mm(o_part(1, h), S1[:, h, :], qe[:, h, :], start=True, stop=False)
                last = mm(o_part(1, h), V1[:, h, :], QKT[:, 1, h, :], start=False, stop=True)
            last.then_inc(S["o_psum"], 1)
            run_unit(19)
            pe.wait_ge(S["o_sq"], 2)
            for b in range(2):
                last = mm(bank(3 + b), ones[:], norms[:, 0, b * 512:(b + 1) * 512], start=True, stop=True)
            last.then_inc(S["oss_psum"], 1)
            run_unit(20)

            pe.wait_ge(S["o_rms"], 1)
            for c in range(TC):
                for j in range(4):
                    last = tr(heads(3 + c)[:, j, :], raw["sv"][:, j, c * P:(c + 1) * P])
            last.then_inc(S["sv_psum"], 1)
            run_unit(21)
            pe.wait_ge(S["sv_ready"], TC)
            pe.wait_ge(S["ya_ready"], 2)

            for k in range(SB_H + 2):
                if k < SB_H:
                    if k >= 3:
                        pe.wait_ge(S["r_min"], k - 2)
                    o = SB_D * (k % 2)
                    kt, qt = raw["sk"][o:o + SB_D, k // 2, :], raw["sq"][o:o + SB_D, k // 2, :]
                    zb = bank(3 + k % 3)
                    mm(zb[:, 0:T], kt[:, 0:P], qt, start=True, stop=True, skip_group_check=True)
                    mm(zb[:, T:T + P], kt[:, P:T], qt[:, P:T], start=False, stop=True,
                       skip_group_check=True).then_inc(S["z_psum"], 1)
                    run_unit(22 + k)
                if 1 <= k <= SB_H:
                    h = k - 1
                    pe.wait_ge(S["z_masked"], h + 1)
                    zb = bank(3 + h % 3)
                    mm(zb[:, 0:T + P], negtri[:], zs[:, h, :], start=False, stop=True,
                       skip_group_check=True)
                    mm(zb[:, P:T], negones[:], zs[:, h, T:T + P], start=False, stop=True,
                       skip_group_check=True).then_inc(S["r_psum"], 1)
                if k >= 2:
                    h = k - 2
                    pe.wait_ge(S["att_ready"], h + 1)
                    o = SB_D * (h % 2)
                    yb = ps[o:o + SB_D, 6 + h // 4, (h // 2 % 2) * T:(h // 2 % 2 + 1) * T]
                    mm(yb, vS[:, 0, h * SB_D:(h + 1) * SB_D], att[:, h, 0:T], start=True, stop=False,
                       skip_group_check=True)
                    last = mm(yb[:, P:T], vS[:, 1, h * SB_D:(h + 1) * SB_D], att[:, h, T:T + P],
                              start=False, stop=True, skip_group_check=True)
            last.then_inc(S["yb_psum"], 1)
            for u in range(30, N_ALL):
                run_unit(u)

            for i in range(N_UPS):
                n = i // 2
                pe.wait_ge(S["y_split"], n + 1)
                if i == 0:
                    pe.wait_ge(S["y_split"], 2)
                if i >= 2:
                    pe.wait_ge(S["merged_ready"], i - 1)
                ub = [bank(3 + 2 * (i % 2) + j // 2)[:, (j % 2) * T:(j % 2 + 1) * T] for j in range(4)]
                split_products(UP0 + i, ub, [P * j for j in range(4)], 4, y_hi[n], y_lo[:, n]
                               ).then_inc(S["up_psum"], 1)

            pe.wait_ge(S["unit_read"], N_ALL)
            for c in range(TC):
                for u in range(N_OUTS):
                    first, n = u // 2 * 4, u % 2
                    if c == 0:
                        pe.wait_ge(S["merged_ready"], N_UPS - 1 + u // 2)
                        wait_unit_loaded(pe, OUT0 + u)
                    w = raw_unit(OUT0 + u).rearrange("p (k n) -> p k n", k=4)
                    for k in range(4):
                        last = mm(bank(2 * c + n), merged[:, first + k, c * P:(c + 1) * P], w[:, k, :],
                                  start=(first + k == 0), stop=(first + k == KD - 1))
                last.then_inc(S["mix_psum"], 1)

            for c in range(TC):
                pe.wait_ge(S["x1_ready"], c + 1)
                for k in range(KD):
                    last = tr(heads(4 + 2 * c + k // 4)[:, k % 4, :], x1[:, c, k:D:KD])
                    if k % 4 == 3:
                        last.then_inc(S["x1T_psum"], 1)
            for c in range(TC):
                for half in range(2):
                    pe.wait_ge(S["x1T_ready_act"] if half == 0 else S["x1T_ready_dve"], c + 1)
                    for k in range(4 * half, 4 * half + 4):
                        last = mm(bank(4)[:, N_EXP * c:N_EXP * (c + 1)], x1T[:, k, c * P:(c + 1) * P],
                                  w_rt[:, k, :], start=(k == 0), stop=(k == KD - 1))
            last.then_inc(S["rt_psum"], 1)
            for c in range(TC):
                for n in range(2):
                    mm(bank(2 * c + n), alpha_ident[:], x1[:, c, n * 512:(n + 1) * 512],
                       start=True, stop=False, skip_group_check=True)
            pe.wait_ge(S["mask_ready"], 1)
            mc = [mask[:, N_EXP * c:N_EXP * (c + 1)] for c in range(TC)]
            mm(bank(6)[:, 0:16], strict[:], mc[0], start=True, stop=True)
            mm(bank(6)[:, 16:32], ones[:], mc[0], start=True, stop=False)
            mm(bank(6)[:, 16:32], strict[:], mc[1], start=False, stop=True)
            mm(bank(6)[:, 32:48], ones[:], mc[0], start=True, stop=False)
            mm(bank(6)[:, 32:48], ones[:], mc[1], start=False, stop=True).then_inc(S["pos_psum"], 1)

            def gather(n):
                pe.wait_ge(S["pick_ready"], n)
                for half in range(2):
                    for c in range(TC):
                        for part in (x1h, x1l):
                            last = mm(bank(6 + half), pick_r[:, c, :], part[:, c, half * 512:(half + 1) * 512],
                                      start=(c == 0 and part is x1h), stop=(c == TC - 1 and part is x1l))
                last.then_inc(S["gathered"], 1)

            def gather_transpose(n):
                pe.wait_ge(S["xg_ready"], 2 * n)
                for k in range(KD):
                    last = tr(heads(6 + k // 4)[:, k % 4, :], xg[:, k:D:KD])
                last.then_inc(S["xgT_psum"], 1)

            pe.wait_ge(S["x1_split"], TC)
            gather(1)
            gather_transpose(1)
            pe.wait_ge(S["rounds_ready"], 1)
            n_rounds = pe.value_load(rounds_i[0:1, 0:1], min_val=1, max_val=T // SLOTS)
            def two_experts(dst, lhsT, slot, cols_, steps):
                for k in range(steps):
                    for e in range(2):
                        w = ring[:, slot + e, :].rearrange("p (k n) -> p k n", k=steps)
                        last = mm(dst[e * SLOTS:(e + 1) * SLOTS, :], lhsT[:, k, e * SLOTS:(e + 1) * SLOTS],
                                  w[:, k, cols_:cols_ + 512], start=(k == 0), stop=(k == steps - 1))
                return last

            with pe.Fori(0, n_rounds) as r:
                with pe.Fori(0, PAIRS) as p:
                    i = r * PAIRS + p
                    pe.wait_ge(S["xgT_ready"], 2 * i + 2)
                    for s in (0, 1):
                        pe.wait_ge(slot_loaded[s], 16 * i + 16)
                    two_experts(bank(4), xgT, 0, 0, KD).then_inc(S["w1_done"], 1)
                    for s in (2, 3):
                        pe.wait_ge(slot_loaded[s], 16 * i + 16)
                    two_experts(bank(5), xgT, 2, 0, KD).then_inc(S["w3_done"], 1)
                    gather(i + 2)
                    pe.wait_ge(S["h_ready"], i + 1)
                    for k in range(KF):
                        tr(heads(4)[:, k, :], hS[:, k:FF:KF])
                    pe.wait_ge(S["pick_gate_ready"], i + 1)
                    for c in range(TC):
                        last = tr(heads(5)[:, c, :], pick_gate[:, c, :])
                    last.then_inc(S["hT_psum"], 1)
                    gather_transpose(i + 2)
                    pe.wait_ge(S["hT_ready"], i + 1)
                    for s in (4, 5):
                        pe.wait_ge(slot_loaded[s], 16 * i + 16)
                    for half in range(2):
                        if half:
                            pe.wait_ge(S["slot_gate_ready"], i + 1)
                        last = two_experts(bank(4 + half), hT, 4, half * 512, KF)
                    last.then_inc(S["w2_done"], 1)
                    for part, ready in ((y_slot_hi, "y_ready"), (y_slot_lo, "y_lo_ready")):
                        pe.wait_ge(S[ready], 2 * i + 2)
                        for c in range(TC):
                            for half in range(2):
                                last = mm(bank(2 * c + half), pickT[:, c, :],
                                          part[:, half * 512:(half + 1) * 512], start=False, stop=False,
                                          skip_group_check=True)
                    last.then_inc(S["scattered"], 1)

        @block.vector
        def _(dve):
            step = in_order(dve, "dve_order")
            tt, ts, stt = nc.vector.tensor_tensor, nc.vector.tensor_scalar, nc.vector.scalar_tensor_tensor
            copy = nc.vector.tensor_copy

            for b in range(4):
                dve.wait_ge(S["xh_ready"], b + 1)
                part = slice(2 * b, 2 * b + 2)
                tt(flat(xl[:, part, :]), bank(b), flat(xh[:, part, :]).bitcast(F32), ALU.subtract
                   ).then_inc(S["xl_ready"], 1)
            for n in range(LO_FIRST):
                dve.wait_ge(S["hi_ready"], n + 1)
                tt(w_lo[:, n, :], raw_unit(n), w_hi[:, n, :].bitcast(F32), ALU.subtract
                   ).then_inc(S["lo_first"], 1)
                if n == 0:
                    dve.wait_ge(S["ba_hi_ready"], 1)
                    tt(ba_lo[:], w_ba[:], ba_hi[:].bitcast(F32), ALU.subtract).then_inc(S["ba_split"], 1)
            dve.wait_ge(S["rows_psum"], 1)
            step(copy(cols[:, 0:N_ROWS], bank(6)[:, 0:N_ROWS]), "cols_ready")

            def conv(dst, src, w0, stride, bias=None):
                def w(tap):
                    return cols[:, w0 + tap * stride:w0 + tap * stride + 1]
                if bias is None:
                    step(ts(dst, src, w(TAPS - 1), None, ALU.mult))
                else:
                    step(ts(dst, src, w(TAPS - 1), bias, ALU.mult, ALU.add))
                for back in range(1, TAPS):
                    last = stt(dst[:, back:T], src[:, 0:T - back], w(TAPS - 1 - back), dst[:, back:T],
                               ALU.mult, ALU.add)
                    if back < TAPS - 1:
                        step(last)
                return last

            def conv_unit(v):
                dve.wait_ge(S["unit_read"], v + 1)
                kind, c = v // 2, 2 * (v % 2)
                for j in range(2):
                    dst = vc[:, c + j, :] if kind == 2 else qk[:, c + j, 1 - kind, :]
                    src = raw[("q", "k", "v")[kind]][:, c + j, :]
                    last = conv(dst, src, C_DNW + 4 * kind + c + j, 12)
                    step(last) if j == 0 else step(last, "conv_done")

            conv_unit(0)
            dve.wait_ge(S["ba_tok"], 1)
            dve.wait_ge(S["small_in"], 16 * 5)
            tok8 = bank(7)[:, 256:272].rearrange("p (c e) -> p c e", c=TC)
            step(tt(v12[:, 0:8].rearrange("p (c h) -> p c h", c=TC), tok8[:, :, 4:8],
                    bc(heads4[:, 1, :], 1, TC), ALU.add))
            step(ts(v12[:, 8:12], cols[:, C_LAM:C_LAM + 4], -1.0, None, ALU.mult))
            step(ts(m12, v12, 0.0, None, ALU.max))
            step(stt(e12, v12, -1.0, v12, ALU.mult, ALU.max), "g_abs")
            conv_unit(1)
            dve.wait_ge(S["g_exp"], 1)
            step(ts(beta, beta, 1.0, None, ALU.add))
            step(nc.vector.reciprocal(beta, beta))
            step(ts(z12, e12, 2.0, None, ALU.add))
            step(nc.vector.reciprocal(z12, z12))
            step(tt(z12, z12, e12, ALU.mult))
            step(tt(e12, z12, z12, ALU.mult))
            step(ts(q12, e12, 1.0 / 17, None, ALU.mult))
            for n in (15, 13, 11, 9, 7, 5, 3):
                step(stt(q12, q12, 1.0 / n, e12, ALU.add, ALU.mult))
            step(stt(q12, q12, 1.0, z12, ALU.add, ALU.mult))
            step(stt(sp12, q12, 2.0, m12, ALU.mult, ALU.add))
            step(ts(n8, sp12[:, 8:12], -LRU_C, None, ALU.mult))
            step(stt(g.rearrange("p (c h) -> p c h", c=TC), sp12[:, 0:8].rearrange("p (c h) -> p c h", c=TC),
                     -1.0, bc(ea, 1, TC), ALU.mult, ALU.mult), "g_ready")
            conv_unit(2)
            conv_unit(3)
            dve.wait_ge(S["gb_psum"], 1)
            step(copy(gc, bank(7)[:, 272:280]), "gc_ready")
            for c in range(TC):
                for h in range(DN_H):
                    gcol = gc[:, 4 * c + h:4 * c + h + 1]
                    ts(dec[:, c, h, :], heads(3 + c)[:, h, :], gcol, 0.0, ALU.subtract, ALU.max)
                    ts(decT[:, c, h, :], heads(3 + c)[:, h, :], gcol, 0.0, ALU.subtract, ALU.min)
            step(tt(kds[:, 0:4], heads(3)[:, :, P - 1], gc[:, 0:4], ALU.subtract), "diff_ready")
            conv_unit(4)
            conv_unit(5)
            dve.wait_ge(S["z_silu"], 1)
            step(ts(flat(raw["z"]), flat(raw["z"]), cols[:, C_NW:C_NW + 1], None, ALU.mult))
            for n in range(2):
                dve.wait_ge(S["rn_ready"], n + 1)
                rn = norms[:, n, :].rearrange("p (h b t) -> p h b t", h=2, b=2)
                for b, scale in ((0, 1.0), (1, P ** -0.5)):
                    t = qk[:, 2 * n:2 * n + 2, b, :]
                    last = stt(t, t, scale, rn[:, :, b, :], ALU.mult, ALU.mult)
            step(last, "qk_ready")
            dve.wait_ge(S["tok_psum"], 1)
            dve.wait_ge(S["dec_ready"], 1)
            for c in range(TC):
                for h in range(DN_H):
                    ts(vb[:, c, h, :], heads(5 + c)[:, h, :], beta[:, 4 * c + h:4 * c + h + 1], None, ALU.mult)
            for h in range(DN_H):
                last = ts(kdec[:, h, :], heads(3)[:, h, :], kds[:, h:h + 1], None, ALU.mult)
            step(last, "tok_ready")
            step(stt(negbeg, beta[:, 4:8], -1.0, eg[:, 4:8], ALU.mult, ALU.mult))
            dve.wait_ge(S["kk_psum"], 1)
            dve.wait_ge(S["dec_masked"], 2)

            def pair_bank(b):
                return bank(b).rearrange("p (a b t) -> p a b t", a=2, b=2)

            for c in range(TC):
                for h in range(DN_H):
                    stt(Amat[:, c, h, :], pair_bank(3 + 2 * c + h // 2)[:, h % 2, 0, :],
                        beta[:, 4 * c + h:4 * c + h + 1], dec[:, c, h, :], ALU.mult, ALU.mult)
                for hp in range(2):
                    last = tt(QKT[:, c, 2 * hp:2 * hp + 2, :], pair_bank(3 + 2 * c + hp)[:, :, 1, :],
                              decT[:, c, 2 * hp:2 * hp + 2, :], ALU.mult)
            step(last, "a_ready")

            def all8(m):
                return m.rearrange("p c h t -> p (c h) t")

            step(tt(all8(M), all8(Amat), bc(level[:, 0, :], 1, 8), ALU.mult))
            for c in range(TC):
                step(tt(M[:, c], bc(ident[:], 1, 4), M[:, c], ALU.subtract), "inv_m")
            dve.wait_ge(S["at_ready"], TC)
            step(tt(all8(MT), all8(AT), bc(level1T[:], 1, 8), ALU.mult))
            step(tt(all8(MT), bc(ident[:], 1, 8), all8(MT), ALU.subtract))
            step(tt(qe, qk[:, :, 1, P:T], eG1, ALU.mult))
            for n in range(len(LEVELS)):
                for c in range(TC):
                    dve.wait_ge(S["inv_x"], TC * n + c + 1)
                    step(tt(XS[:, c], heads(3 + 2 * c), bc(level[:, n + 1, :], 1, 4), ALU.mult), "inv_xs")
                for c in range(TC):
                    dve.wait_ge(S["inv_z"], TC * n + c + 1)
                    step(tt(M[:, c], M[:, c], heads(4 + 2 * c), ALU.subtract), "inv_m")
            dve.wait_ge(S["v0_psum"], 1)
            step(copy(flat(V0), bank(3)), "v0_ready")
            dve.wait_ge(S["ks_psum"], 1)
            for h in range(DN_H):
                last = stt(R[:, h, :], heads(3)[:, h, :], negbeg[:, h:h + 1], vb[:, 1, h, :],
                           ALU.mult, ALU.add)
            step(last, "r_ready")
            dve.wait_ge(S["v1_psum"], 1)
            step(copy(flat(V1), bank(4)), "v1_ready")
            dve.wait_ge(S["o_rms"], 1)
            for b in range(2):
                ya = flat(yT[:, 0, 2 * b:2 * b + 2, :])
                step(tt(ya, bank(5 + b), norms[:, 1, b * 512:(b + 1) * 512], ALU.mult), "ya_ready")
                step(tt(ya, ya, flat(raw["z"][:, 2 * b:2 * b + 2, :]), ALU.mult))

            def split_y(n):
                y = flat(yT[:, n])
                step(copy(flat(y_hi[n]), y))
                step(tt(flat(y_lo[:, n]), y, flat(y_hi[n]).bitcast(F32), ALU.subtract), "y_split")

            split_y(0)

            for k in range(SB_H + 2):
                if k < 4:
                    dve.wait_ge(S["unit_read"], 18)
                    last = conv(xc[:, k, :], raw["lx"][:, k, :], C_LW + k, 4,
                                cols[:, C_LCB + k:C_LCB + k + 1])
                    step(last, "xc_ready")
                if k >= 2:
                    h = k - 2
                    dve.wait_ge(S["r_psum"], h + 1)
                    step(stt(att[:, h, :], bank(3 + h % 3)[:, 0:T + P], 0.0, flat(past_bias[:]),
                             ALU.min, ALU.add), "r_min")
                if k < SB_H:
                    dve.wait_ge(S["z_log"], k + 1)
                    step(stt(zs[:, k, :], bank(3 + k % 3)[:, 0:T + P], 0.0, zs[:, k, :],
                             ALU.max, ALU.add), "z_sp")
                    diag = zs[:, k, :].rearrange("p (a t) -> p a t", t=P)[:, 0:3:2, :]
                    step(tt(diag, diag, bc(strict[:], 1, 2), ALU.mult), "z_masked")
            for b in range(2):
                dve.wait_ge(S["yb_ready"], b + 1)
                part = slice(2 * b, 2 * b + 2)
                last = tt(flat(y_lo[:, 1, part, :]), bank(6 + b), flat(y_hi[1][:, part, :]).bitcast(F32),
                          ALU.subtract)
                step(last) if b == 0 else step(last, "y_split")

            dve.wait_ge(S["lru_gate"], 1)
            for c in range(LRU_CH):
                last = ts(lr[:, c, :], lr[:, c, :], n8[:, c:c + 1], None, ALU.mult)
            step(last)
            step(ts(lw, flat(lr), 2.0, -1.0, ALU.mult, ALU.max), "lru_near")
            dve.wait_ge(S["lru_gate"], 2)
            step(tt(flat(li), flat(li), flat(xc), ALU.mult))
            dve.wait_ge(S["lru_a"], 1)
            step(tt(far, lq, far, ALU.subtract))
            step(ts(lw, lw, 0.25, None, ALU.mult))
            step(ts(lq, lw, 1.0 / 720, None, ALU.mult))
            for coef in (1.0 / 120, 1.0 / 24, 1.0 / 6, 0.5, 1.0):
                step(stt(lq, lq, coef, lw, ALU.add, ALU.mult))
            step(stt(lw, lq, 2.0, lq, ALU.add, ALU.mult))
            step(stt(lq, lw, 2.0, lw, ALU.add, ALU.mult))
            step(tt(far, far, lq, ALU.subtract))
            step(ts(far, far, 0.0, None, ALU.max), "lru_var")
            def merge(i):
                n, half = i // 2, i % 2
                dve.wait_ge(S["gates_ready"], n + 1)
                dve.wait_ge(S["up_psum"], i + 1)
                b = 3 + 2 * (i % 2)
                o = (n * 8 + half * 4) * T
                prod = tmp[:, 2, :]
                dst = flat(merged)[:, half * 1024:(half + 1) * 1024]
                last = tt(prod if n else dst, flat(ps[:, b:b + 2, :]), flat(gates)[:, o:o + 1024], ALU.mult)
                if n:
                    step(last)
                    last = tt(dst, dst, prod, ALU.add)
                step(last, "merged_ready")

            merge(0)
            dve.wait_ge(S["lru_b"], 1)
            step(tt(flat(li), flat(li), far, ALU.mult))
            for c in range(LRU_CH):
                last = nc.vector.tensor_tensor_scan(lr[:, c, :], la[:, c, :], li[:, c, :], 0.0,
                                                    ALU.mult, ALU.add)
            step(last)
            merge(1)
            dve.wait_ge(S["gelu_ready"], 1)
            step(tt(flat(yT[:, 2]), flat(lr), flat(raw["ly"]), ALU.mult), "yc_ready")
            split_y(2)
            for i in range(2, N_UPS):
                merge(i)


            def layer_norm(t, gb0, name):
                for n in range(2):
                    nc.vector.bn_stats(stats[:, 6 * n:6 * n + 6], t[:, n * 512:(n + 1) * 512])
                step(copy(rnd[:, 0:1], eps_ln))
                step(nc.vector.bn_aggr(mv, stats), "ln_var")
                ln_count[0] += 1
                dve.wait_ge(S["ln_rstd"], ln_count[0])
                step(ts(t, t, mv[:, 0:1], rstd, ALU.subtract, ALU.mult))
                step(tt(t, t, ln_gb[:, gb0, :], ALU.mult))
                return tt(t, t, ln_gb[:, gb0 + 1, :], ALU.add)

            ln_count = [0]
            dve.wait_ge(S["ln_in"], 16 * 4)
            for c in range(TC):
                dve.wait_ge(S["mix_psum"], c + 1)
                for n in range(2):
                    part = slice(n * 512, (n + 1) * 512)
                    last = stt(x1[:, c, part], xin[:, c, part], ALPHA, bank(2 * c + n), ALU.mult, ALU.add)
                step(last)
                step(layer_norm(x1[:, c, :], 0, "x1"), "x1_ready")
            for c in range(TC):
                dve.wait_ge(S["x1T_psum"], 2 * c + 2)
                copy(x1T[:, 4:8, c * P:(c + 1) * P], heads(5 + 2 * c)).then_inc(S["x1T_ready_dve"], 1)

            dve.wait_ge(S["rt_psum"], 1)
            l3, s3 = (t.rearrange("p (c e) -> p c e", c=TC) for t in (logit, score))
            step(copy(logit, bank(4)[:, 0:32]))
            step(nc.vector.tensor_reduce(mx, l3, AX_X, ALU.max))
            step(tt(s3, l3, bc(mx, 2, N_EXP), ALU.subtract), "sm_in")
            dve.wait_ge(S["sm_exp"], 1)
            step(nc.vector.tensor_reduce(sume, s3, AX_X, ALU.add))
            step(nc.vector.reciprocal(sume, sume))
            step(tt(s3, s3, bc(sume, 2, N_EXP), ALU.mult))
            step(tt(sel.rearrange("p (c e) -> p c e", c=TC), s3, bc(b_rt[:], 1, TC), ALU.add))

            def ranks(dst, vals, n):
                v = vals.rearrange("p (g e) -> p g e", e=PER_GROUP)
                other, own = bc(v, 2, PER_GROUP), bc(v, 3, PER_GROUP)
                c1, c2 = (t[:, 0:16 * n].rearrange("p (g a b) -> p g a b", a=4, b=4) for t in (cmp1, cmp2))
                step(tt(c1, other, own, ALU.is_equal))
                step(tt(c1, c1, bc(before[:], 1, n), ALU.mult))
                step(tt(c2, other, own, ALU.is_gt))
                step(tt(c1, c1, c2, ALU.add))
                step(nc.vector.tensor_reduce(dst, c1.rearrange("p g a b -> p (g a) b"), AX_X, ALU.add))

            ranks(chosen, sel, 8)
            step(ts(chosen, chosen, 1.5, None, ALU.is_lt))
            step(tt(tk, sel, chosen, ALU.mult))
            step(nc.vector.tensor_reduce(gsum, tk.rearrange("p (g e) -> p g e", e=4), AX_X, ALU.add))
            ranks(gsel, gsum, 2)
            step(ts(gsel, gsel, 0.5, None, ALU.is_lt))
            step(tt(mask.rearrange("p (g e) -> p g e", e=4), chosen.rearrange("p (g e) -> p g e", e=4),
                    bc(gsel, 2, 4), ALU.mult), "mask_ready")
            step(tt(tk, score, mask, ALU.mult))
            tk3 = tk.rearrange("p (c e) -> p c e", c=TC)
            step(nc.vector.tensor_reduce(sume, tk3, AX_X, ALU.add))
            step(nc.vector.reciprocal(sume, sume))
            step(tt(gate[:, :, 0:N_EXP], tk3, bc(sume, 2, N_EXP), ALU.mult))
            step(copy(gate[:, :, N_EXP:], gate[:, :, 0:2]))
            dve.wait_ge(S["pos_psum"], 1)
            m3 = mask.rearrange("p (c e) -> p c e", c=TC)
            step(stt(posx[:, :, 0:N_EXP], bank(6)[:, 0:32].rearrange("p (c e) -> p c e", c=TC), 1024.0, m3,
                     ALU.add, ALU.mult))
            step(ts(posx[:, :, 0:N_EXP], posx[:, :, 0:N_EXP], -1024.0, None, ALU.add))
            step(ts(posx[:, :, N_EXP:], posx[:, :, 0:2], -float(SLOTS), None, ALU.add))
            step(nc.vector.tensor_reduce(cnt, bank(6)[:, 32:48], AX_X, ALU.max))
            for n in range(1, T // SLOTS):
                step(ts(rnd[:, n:n + 1], cnt, float(n * SLOTS), None, ALU.is_gt))
            step(nc.vector.tensor_reduce(rnd[:, 0:1], rnd[:, 1:4], AX_X, ALU.add))
            step(ts(rounds_i[:], rnd[:, 0:1], 1.0, None, ALU.add), "rounds_ready")

            def pick_pair(first):
                tt(pick_r[:].rearrange("p c (e s) -> p c e s", e=2),
                   bc(bc(slot_ids[:], 1, 2), 1, TC),
                   bc(posx[:, :, first:first + 2], 3, SLOTS), ALU.is_equal).then_inc(S["pick_ready"], 1)

            def read_gather(n):
                dve.wait_ge(S["gathered"], n)
                copy(xg[:, 512:1024], bank(7)).then_inc(S["xg_ready"], 1)

            def read_gatherT(n):
                dve.wait_ge(S["xgT_psum"], n)
                copy(flat(xgT[:, 4:8, :]), bank(7)).then_inc(S["xgT_ready"], 1)

            pick_pair(0)
            read_gather(1)
            read_gatherT(1)
            n_rounds = dve.value_load(rounds_i[0:1, 0:1], min_val=1, max_val=T // SLOTS)
            with dve.Fori(0, n_rounds) as r:
                with dve.Fori(0, PAIRS) as p:
                    i = r * PAIRS + p
                    dve.wait_ge(S["pick_ready"], i + 1)
                    tt(pick_gate.rearrange("p c (e s) -> p c e s", e=2),
                       pick.rearrange("p c (e s) -> p c e s", e=2),
                       bc(gate[:, :, bass.ds(2 * p, 2)], 3, SLOTS), ALU.mult
                       ).then_inc(S["pick_gate_ready"], 1)
                    dve.wait_ge(S["pick_gate_ready"], i + 1)
                    tt(pick_r[:].rearrange("p c (e s) -> p c e s", e=2),
                       bc(bc(slot_ids[:], 1, 2), 1, TC),
                       bc(posx[:, :, bass.ds(2 * p + 2, 2)], 3, SLOTS), ALU.is_equal
                       ).then_inc(S["pick_ready"], 1)
                    dve.wait_ge(S["h_silu"], i + 1)
                    dve.wait_ge(S["w3_done"], i + 1)
                    tt(hS, gS, bank(5), ALU.mult).then_inc(S["h_ready"], 1)
                    read_gather(i + 2)
                    dve.wait_ge(S["hT_psum"], i + 1)
                    copy(flat(hT), bank(4)).then_inc(S["hT_ready"], 1)
                    ts(flat(pickT[:]), bank(5)[:, 0:256], 0.0, None, ALU.is_gt)
                    nc.vector.tensor_reduce(slot_gate, bank(5)[:, 0:256], AX_X, ALU.add
                                            ).then_inc(S["slot_gate_ready"], 1)
                    read_gatherT(i + 2)
                    for half in range(2):
                        dve.wait_ge(S["y_ready"], 2 * i + 1 + half)
                        part = slice(half * 512, (half + 1) * 512)
                        stt(y_slot_lo[:, part], bank(4 + half), slot_gate, y_slot_hi[:, part].bitcast(F32),
                            ALU.mult, ALU.subtract).then_inc(S["y_lo_ready"], 1)
                dve.wait_ge(S["pick_ready"], r * PAIRS + PAIRS + 1)
                ts(posx[:, :, 0:N_EXP], posx[:, :, 0:N_EXP], -float(SLOTS), None, ALU.add
                   ).then_inc(S["slots_moved"], 1)
                dve.wait_ge(S["slots_moved"], 2 * r + 1)
                ts(posx[:, :, N_EXP:], posx[:, :, 0:2], -float(SLOTS), None, ALU.add
                   ).then_inc(S["slots_moved"], 1)
                dve.wait_ge(S["slots_moved"], 2 * r + 2)

            dve.wait_ge(S["scattered"], n_rounds * PAIRS)
            for c in range(TC):
                for n in range(2):
                    nc.vector.bn_stats(stats[:, 6 * n:6 * n + 6], bank(2 * c + n))
                step(copy(rnd[:, 0:1], eps_ln))
                step(nc.vector.bn_aggr(mv, stats), "ln_var")
                dve.wait_ge(S["ln_rstd"], TC + c + 1)
                step(stt(shift, mv[:, 0:1], -1.0, rstd, ALU.mult, ALU.mult), "ln_shift")
                for n in range(2):
                    part = slice(n * 512, (n + 1) * 512)
                    dve.wait_ge(S["y_norm"], 2 * c + n + 1)
                    last = tt(xin[:, c, part], xin[:, c, part], ln_gb[:, 2, part], ALU.mult)
                step(last)
                step(tt(xin[:, c, :], xin[:, c, :], ln_gb[:, 3, :], ALU.add), "y_final")


_INS = ['x', 'w_in', 'dn_conv_w', 'dn_a_log', 'dn_dt_bias', 'dn_norm_w', 'lru_conv_w', 'lru_conv_b',
        'lru_w_a', 'lru_b_a', 'lru_w_x', 'lru_b_x', 'lru_lambda', 'w_up_dn', 'w_up_sb', 'w_up_lru',
        'w_merge', 'b_merge', 'w_out', 'ln1_g', 'ln1_b', 'w_router', 'b_router', 'moe_w1', 'moe_w3',
        'moe_w2', 'ln2_g', 'ln2_b']
_OUTS = [((1, 256, 1024), 'float32')]


def kernel(**inputs):
    import numpy as _np
    import concourse.bacc as _bacc
    from concourse import mybir as _mybir
    from concourse.bass_utils import run_bass_kernel_spmd as _run

    nc = _bacc.Bacc("TRN2", target_bir_lowering=False, num_devices=1)
    arrays, args = {}, []
    for name in _INS:
        a = _np.ascontiguousarray(inputs[name])
        arrays[f"in_{name}_dram"] = a
        args.append(nc.dram_tensor(f"in_{name}_dram", a.shape, _mybir.dt.from_np(a.dtype),
                                   kind="ExternalInput").ap())
    for i, (shape, dtype) in enumerate(_OUTS):
        dt = _mybir.dt.from_np(_np.dtype(dtype))
        args.append(nc.dram_tensor(f"out_{i}_dram", shape, dt, kind="ExternalOutput").ap())
    hybrid_layer(nc, *args)
    r = _run(nc, [arrays], core_ids=[0])
    return r.results[0]["out_0_dram"]
```

```python
from contextlib import ExitStack

import concourse.bass as bass
from concourse import mybir

F32 = mybir.dt.float32
F32R = mybir.dt.float32r
I32 = mybir.dt.int32
ALU = mybir.AluOpType
ACT = mybir.ActivationFunctionType
AX_X = mybir.AxisListType.X

P = 128
D = 1024
T = 256
TC = T // P
KD = D // P
DN_H = 4
SB_H = 8
SB_D = 64
LRU_CH = 4
LRU_C = 8.0
TAPS = 4
N_EXP = 16
GROUPS = 4
PER_GROUP = N_EXP // GROUPS
FF = 512
KF = FF // P
SLOTS = 64
SLOT_BASE = 1024
PAIRS = N_EXP // 2
ALPHA = 2.0 ** 0.25
LN_EPS = 1e-5
RMS_EPS = 1e-6
N_UP = 3

SLOT = 4096
DENSE_SLOTS = 3
RING = 6
UNIT = 2048
RAW_SLOTS = 4
HI_SLOTS = 2

C_DNW, C_LW, C_LCB, C_BA, C_BX, C_LAM, C_BM, C_NW = 0, 48, 64, 68, 72, 76, 80, 104
N_ROWS = 105

Q0, K0, V0, Z0, BA0 = 0, 512, 1024, 1536, 2048
SQ0, SK0, SV0, LX0, LY0 = 2056, 2568, 3080, 3592, 4104
PIECES = [("q", Q0), ("k", K0), ("v", V0), ("z", Z0), ("sq", SQ0), ("sk", SK0), ("sv", SV0),
          ("lx", LX0), ("ly", LY0)] + [("gate", 512 * n) for n in range(6)]
N_PROJ = len(PIECES)
N_UNIT = 2 * N_PROJ
N_UPS = 2 * N_UP
N_OUTS = 4
LEVELS = [2, 4, 8, 16, 32, 64]


def hybrid_layer(nc: bass.Bass, x, w_in, dn_conv_w, dn_a_log, dn_dt_bias, dn_norm_w, lru_conv_w,
                 lru_conv_b, lru_w_a, lru_b_a, lru_w_x, lru_b_x, lru_lambda, w_up_dn, w_up_sb,
                 w_up_lru, w_merge, b_merge, w_out, ln1_g, ln1_b, w_router, b_router, moe_w1,
                 moe_w3, moe_w2, ln2_g, ln2_b, out):
    with ExitStack() as ctx:
        def sb(name, shape, dt=F32):
            return ctx.enter_context(nc.sbuf_tensor(name, shape, dt))

        def sem(name):
            return ctx.enter_context(nc.semaphore(name))

        def flat(ap):
            names = "abcd"[:len(ap.shape) - 1]
            return ap.rearrange(f"p {' '.join(names)} -> p ({' '.join(names)})")

        def bc(ap, axis, n):
            a = ap.unsqueeze(axis)
            shape = list(a.shape)
            shape[axis] = n
            return a.broadcast_to(shape)

        def again(name, shape, off, dt=F32R):
            return nc.alloc_sbuf_tensor_at(name, shape, dt, offset=off)

        def here():
            return (nc.sbuf_base + 31) // 32 * 32

        ring_at = here()
        ring = sb("ring", [P, RING, SLOT])
        w_lo = again("w_lo", [P, RAW_SLOTS, UNIT], ring_at)
        w_hi = again("w_hi", [P, HI_SLOTS, UNIT], ring_at + 2 * SLOT * 4)
        held = again("held", [P, 6, 1024], ring_at + DENSE_SLOTS * SLOT * 4)
        y_hi = [held[:, n, :].rearrange("p (k t) -> p k t", t=T) for n in (3, 4, 5)]
        xh = sb("xh", [P, KD, T], F32R)
        xl = sb("xl", [P, KD, T], F32R)
        y_at = here()
        yT = sb("yT", [P, 3, 4, T])
        y_lo = again("y_lo", [P, 3, 4, T], y_at)
        pick_at = y_at + 4 * 2 * 1024
        pick_r = again("pick_r", [P, TC, P], pick_at)
        pickT = again("pickT", [P, TC, P], pick_at + 4 * TC * P)
        vc_at = here()
        vc = sb("vc", [P, DN_H, T])
        y_slot_hi = again("y_slot_hi", [P, D], vc_at)
        hold = flat(ring[:, DENSE_SLOTS:RING, :])
        raw = {}
        for n, name in enumerate(("q", "k", "v", "z", "sq", "sk")):
            raw[name] = hold[:, n * 1024:(n + 1) * 1024].rearrange("p (c t) -> p c t", c=4)
        raw["sv"], raw["lx"], raw["ly"] = raw["q"], raw["k"], raw["v"]
        vS = hold[:, 0:1024].rearrange("p (c n) -> p c n", c=TC)
        gates = hold[:, 6144:12288].rearrange("p (c t) -> p c t", c=24)
        xin = sb("xin", [P, TC, D])
        qk_at = here()
        qk = sb("qk", [P, DN_H, 2, T])
        dn_at = here()
        dn = sb("dn", [P, 8, 1024])
        tmp_at = here()
        tmp4 = sb("tmp4", [P, 4, 1024])
        tmp = tmp4[:, 0:3, :]
        w_bd = tmp4[:, 3, :].rearrange("p (n c o) -> p n c o", n=2, c=LRU_CH)
        out_hi = [again(f"out_hi_{n}", [P, UNIT], at)[:] for n, at in enumerate((qk_at, tmp_at, y_at, dn_at))]
        small = sb("small", [P, 512])
        ident = sb("ident", [P, P])
        alpha_ident = sb("alpha_ident", [P, P])
        upper = sb("upper", [P, P])
        strict = sb("strict", [P, P])
        lower = sb("lower", [P, P])
        negtri = sb("negtri", [P, P])
        ones = sb("ones", [P, P])
        negones = sb("negones", [P, P])
        past_bias = sb("past_bias", [P, 3, P])
        levels_at = here()
        levels = sb("levels", [P, 2 + len(LEVELS), P])
        level, level1T = levels[:, 0:1 + len(LEVELS), :], levels[:, 1 + len(LEVELS), :]
        y_slot_lo = again("y_slot_lo", [P, D], levels_at)
        slot_ids = sb("slot_ids", [P, SLOTS])
        before = sb("before", [P, PER_GROUP, PER_GROUP])
        rows = sb("rows", [P, P])
        cols = sb("cols", [P, P])
        w_ba = sb("w_ba", [P, KD, 8])
        ba_hi = sb("ba_hi", [P, KD, 8], F32R)
        ba_lo = sb("ba_lo", [P, KD, 8], F32R)
        w_rt = sb("w_rt", [P, KD, N_EXP])
        eps = sb("eps", [P, 2])
        eps_ln, eps_rms = eps[:, 0:1], eps[:, 1:2]
        heads4 = sb("heads4", [P, 2, 4])
        b_rt = sb("b_rt", [P, N_EXP])
        rounds_i = sb("rounds_i", [P, 1], I32)
        tinyT = sb("tinyT", [8, T])

        def dn4(n):
            return dn[:, n, :].rearrange("p (c h t) -> p c h t", c=TC, h=DN_H)

        def dnh(n, half):
            return dn[:, n, half * 512:(half + 1) * 512].rearrange("p (h t) -> p h t", h=DN_H)

        vb = dn4(0)
        kdec, V0 = dnh(1, 0), dnh(1, 1)
        dec = dn4(2)
        R, V1 = dnh(2, 0), dnh(2, 1)
        AT, M, MT, XS, QKT = (dn4(n) for n in range(3, 8))
        decT = XS
        Amat = flat(vc[:]).rearrange("p (c h t) -> p c h t", c=TC, h=DN_H)
        qe = flat(vc[:])[:, 0:512].rearrange("p (h t) -> p h t", h=DN_H)
        norms = tmp[:, 0:2, :]
        eG1 = tmp[:, 2, 0:512].rearrange("p (h t) -> p h t", h=DN_H)
        S1 = tmp[:, 2, 512:1024].rearrange("p (h t) -> p h t", h=DN_H)
        zs = flat(dn[:, 0:3, :]).rearrange("p (h n) -> p h n", h=SB_H)
        att = flat(dn[:, 3:6, :]).rearrange("p (h n) -> p h n", h=SB_H)
        xc = flat(qk[:, 0:2]).rearrange("p (c t) -> p c t", c=4)
        lr = flat(qk[:, 2:4]).rearrange("p (c t) -> p c t", c=4)
        li = vc[:]
        la = dn[:, 6, :].rearrange("p (c t) -> p c t", c=4)
        far = dn[:, 7, :]
        lq = tmp[:, 1, :]
        merged = flat(dn[:, 0:2, :]).rearrange("p (m t) -> p m t", t=T)
        x1 = dn[:, 2:4, :]
        ln_gb = dn[:, 4:8, :]
        xg = flat(qk[:])[:, 0:1024]
        xgT = flat(qk[:])[:, 1024:2048].rearrange("p (k s) -> p k s", k=KD)
        y_out = ring[:, 0, 0:TC * D].rearrange("p (c d) -> p c d", c=TC)
        x1T = flat(qk[:]).rearrange("p (k t) -> p k t", t=T)
        x1h, x1l = (flat(m[:]).rearrange("p (c d) -> p c d", c=TC) for m in (xh, xl))
        yflat = flat(yT[:])
        hS, gS = yflat[:, 0:512], yflat[:, 512:1024]
        hT = yflat[:, 1024:1536].rearrange("p (k s) -> p k s", k=KF)
        pick_gate = yflat[:, 1536:1792].rearrange("p (c s) -> p c s", c=TC)
        pick = pick_r[:].bitcast(F32)

        def sm(a, n):
            return small[:, a:a + n]

        v12, e12, z12, q12, sp12, m12 = (sm(12 * i, 12) for i in range(6))
        beta, g, gc, eg, kds = (sm(72 + 8 * i, 8) for i in range(5))
        ea, n8, negbeg = sm(112, 4), sm(116, 4), sm(120, 4)
        stats = sm(124, 12)
        mv = sm(136, 2)
        rstd = sm(138, 1)
        score, sel, chosen, mask, tk = (sm(172 + 32 * i, 32) for i in range(5))
        mx, sume = sm(332, 2), sm(334, 2)
        gsum, gsel = sm(336, 8), sm(344, 8)
        posx = sm(352, 36).rearrange("p (c e) -> p c e", c=TC)
        gate = sm(388, 36).rearrange("p (c e) -> p c e", c=TC)
        cnt, rnd, slot_gate = sm(424, 1), sm(425, 4), sm(429, 1)
        stats2 = sm(432, 24).rearrange("p (c n) -> p c n", c=TC)
        mv2 = sm(456, 4).rearrange("p (c n) -> p c n", c=TC)
        rstd2 = sm(460, 2)
        cmp1, cmp2 = tmp[:, 2, 0:128], tmp[:, 2, 128:256]

        ps = ctx.enter_context(nc.psum_tensor("ps", [P, 8, 512], F32))

        def bank(b):
            return ps[:, b, :]

        def heads(b):
            return bank(b).rearrange("p (h t) -> p h t", h=4)

        S = {n: sem(n) for n in """x_in_0 x_in_1 rows_in small_in bd_in bd_zeroed ln_in ln2_in out_stored consts
            xT_psum rows_psum ident_ready xh_ready xl_ready hi_ready lo_first lo_ready ba_hi_ready ba_split
            cols_ready ba_psum ba_copied ba_tok
            unit_psum unit_read conv_done silu_done z_silu
            g_abs g_exp g_ready gb_psum gc_ready diff_ready dec_ready dec_masked sq_ready ss_psum y_split x1h_ready x1_split
            rn_ready qk_ready tok_psum tok_ready kk_psum a_ready at_psum at_ready
            inv_x inv_xs inv_z inv_m inv_t inv_mt v0_psum v0_ready s1_psum s1_ready ks_psum
            r_ready v1_psum v1_ready o_psum o_sq oss_psum o_rms ya_ready sv_psum sv_ready slot_gate_ready y_lo_ready
            z_psum z_log z_sp z_masked r_psum r_min att_ready yb_psum yb_ready
            xc_ready lru_gate lru_log_a lru_a lru_var lru_b gelu_ready yc_ready gates_ready
            up_psum merged_ready merged_split mix_psum ln_var ln_rstd x1_ready x1T_psum x1T_ready x1T_last rt_psum sm_in sm_exp mask_ready pos_psum rounds_ready
            pick_ready pick_gate_ready gathered xg_ready xgT_psum xgT_ready w1_done w3_done w2_done
            slots_moved h_silu h_ready hT_psum hT_ready y_ready scattered seeded y_final
            dve_order act_order pool_order""".split()}
        unit_loaded = [sem(f"unit_loaded_{i}") for i in range(RAW_SLOTS)]
        expert_loaded = {(m, e, half): sem(f"{m}_loaded_{e}_{half}")
                         for m in ("w1a", "w1b", "w3a", "w3b", "w2") for e in range(2) for half in range(2)}

        block = ctx.enter_context(nc.Block())

        def in_order(eng, order):
            count = {}

            def step(ins, name=order, n=1):
                count[name] = count.get(name, 0) + n
                ins.then_inc(S[name], n)
                eng.wait_ge(S[name], count[name])
            return step

        LRU_UNITS = {25: ("ga", 0), 26: ("ga", 2), 28: ("gx", 0), 29: ("gx", 2)}
        TURN_UNITS = [(22,), (23,), (24, 25, 26), (27, 28, 29), (30,), (31,), (32,), (33,)]
        n_dense = [n for n in range(N_UNIT + 4) if n not in LRU_UNITS]

        def unit(u):
            if u in LRU_UNITS:
                kind, c = LRU_UNITS[u]
                return kind, (lr if kind == "ga" else li), c, None
            n = n_dense.index(u)
            name, col = PIECES[n // 2]
            first = 2 * (n % 2)
            if name == "gate":
                return name, gates, col // P + first, n
            return name, raw[name], first, n

        N_ALL = N_UNIT + 4
        w_up = [w_up_dn, w_up_sb, w_up_lru]
        UP0, OUT0 = N_UNIT, N_UNIT + N_UPS
        N_DENSE = OUT0 + N_OUTS

        def raw_unit(n):
            return ring[:, n % RAW_SLOTS // 2, n % 2 * UNIT:(n % 2 + 1) * UNIT]

        def hi_place(n):
            return w_hi[:, n % HI_SLOTS, :] if n < OUT0 else out_hi[n - OUT0]

        def expert_place(m, e, half):
            if m == "w1b":
                return ((flat(xin[:]), flat(tmp4[:, 0:2, :])),
                        (flat(dn[:, 0:2, :]), flat(dn[:, 2:4, :])))[e][half]
            if m == "w3b" and e == 0:
                return (flat(dn[:, 4:6, :]), flat(tmp4[:, 2:4, :]))[half]
            slot = {"w1a": 0, "w3a": 2, "w3b": 2, "w2": 4}[m] + e
            return ring[:, slot, half * UNIT:(half + 1) * UNIT]

        def wait_used(eng, n):
            if n < UP0:
                eng.wait_ge(S["unit_psum"], n_dense[n] + 1)
            else:
                eng.wait_ge(S["up_psum"], n - UP0 + 1)

        def wait_unit_loaded(eng, n):
            eng.wait_ge(unit_loaded[n % RAW_SLOTS], 16 * (n // RAW_SLOTS + 1))

        @block.sync
        def _(sp):
            for c in range(TC):
                sp.dma_start(xin[:, c, :], x[0, c * P:(c + 1) * P, :]).then_inc(S[f"x_in_{c}"], 16)
            def load_half(m, e, half, pair=0):
                w, k = {"w1": (moe_w1, KD), "w3": (moe_w3, KD), "w2": (moe_w2, KF)}[m[:2]]
                src = w[0].rearrange("(a b) (p k) n -> a b p (k n)", b=2, k=k)
                o = half * UNIT
                sp.dma_start(expert_place(m, e, half), src[pair, e][:, o:o + UNIT]
                             ).then_inc(expert_loaded[m, e, half], 16)

            def load_vectors():
                for first, n, src in ((C_DNW, 48, dn_conv_w[0].rearrange("w (c p) -> w c p", p=P)),
                                      (C_LW, 16, lru_conv_w[0].rearrange("w (c p) -> w c p", p=P)),
                                      (C_LCB, 4, lru_conv_b[0].rearrange("(c p) -> c p", p=P)),
                                      (C_BA, 4, lru_b_a[0].rearrange("(c p) -> c p", p=P)),
                                      (C_BX, 4, lru_b_x[0].rearrange("(c p) -> c p", p=P)),
                                      (C_LAM, 4, lru_lambda[0].rearrange("(c p) -> c p", p=P)),
                                      (C_BM, 24, b_merge[0].rearrange("(c p) -> c p", p=P)),
                                      (C_NW, 1, dn_norm_w)):
                    if len(src.shape) == 3:
                        src = src.rearrange("w c p -> (w c) p")
                    sp.dma_start(rows[first:first + n, :], src).then_inc(S["rows_in"], 16)

            def load_small():
                sp.dma_start(w_ba[:], w_in[0, :, BA0:BA0 + 8].rearrange("(p k) n -> p k n", k=KD)
                              ).then_inc(S["small_in"], 16)
                sp.dma_start(w_rt[:], w_router.rearrange("(p k) n -> p k n", k=KD)
                              ).then_inc(S["small_in"], 16)
                sp.dma_start(heads4[:, 0, :], dn_a_log[0].partition_broadcast(P)).then_inc(S["small_in"], 16)
                sp.dma_start(heads4[:, 1, :], dn_dt_bias[0].partition_broadcast(P)).then_inc(S["small_in"], 16)
                sp.dma_start(b_rt[:], b_router.partition_broadcast(P)).then_inc(S["small_in"], 16)

            for n in range(N_DENSE):
                if n >= RAW_SLOTS:
                    wait_used(sp, n - RAW_SLOTS)
                dst = raw_unit(n)
                if n < UP0:
                    name, col = PIECES[n // 2]
                    col += 256 * (n % 2)
                    w = w_merge if name == "gate" else w_in
                    src = w[0, :, col:col + 256].rearrange("(p k) n -> p k n", k=KD)
                elif n < OUT0:
                    o = (n - UP0) % 2 * 512
                    src = w_up[(n - UP0) // 2][0, :, o:o + 512].rearrange("(k p) n -> p k n", p=P)
                else:
                    k, o = (n - OUT0) // 2 * 4, (n - OUT0) % 2 * 512
                    src = w_out[0, k * P:(k + 4) * P, o:o + 512].rearrange("(k p) n -> p k n", p=P)
                if n == 1:
                    load_vectors()
                if n == 2:
                    load_small()
                sp.dma_start(dst.rearrange("p (k n) -> p k n", k=src.shape[1]), src
                             ).then_inc(unit_loaded[n % RAW_SLOTS], 16)
                if n == UP0 + 3:
                    sp.wait_ge(S["yb_psum"], 1)
                    load_half("w3a", 1, 0)
                if n == UP0 + 5:
                    sp.wait_ge(S["merged_ready"], 2)
                    load_half("w2", 0, 1)
                if n == OUT0 + 1:
                    sp.wait_ge(S["merged_ready"], 4)
                    load_half("w2", 1, 0)
                if n == OUT0 + 2:
                    sp.wait_ge(S["yc_ready"], 1)
                    load_half("w3a", 1, 1)
                if n == OUT0 + 3:
                    sp.wait_ge(S["up_psum"], N_UPS)
                    load_half("w2", 0, 0)
                    for half in range(2):
                        load_half("w3a", 0, half)
                    sp.wait_ge(S["merged_ready"], N_UPS)
                    load_half("w2", 1, 1)

            def expert_load(m, pair, used=None):
                for half in range(2):
                    if used is not None:
                        sp.wait_ge(S[f"{m[:2]}_done"], 2 * used - 1 + half)
                    for e in range(2):
                        load_half(m, e, half, pair)

            sp.wait_ge(S["mix_psum"], 2 * TC)
            expert_load("w1a", 0)
            sp.wait_ge(S["x1_ready"], TC)
            for half in range(2):
                load_half("w1b", 0, half, 1)
            load_half("w3b", 0, 0, 1)
            sp.wait_ge(S["mask_ready"], 1)
            load_half("w3b", 0, 1, 1)
            sp.wait_ge(S["x1_split"], TC)
            sp.wait_ge(S["seeded"], 1)
            for half in range(2):
                load_half("w1b", 1, half, 1)

            def pair_loads(odd, pair, used):
                expert_load("w1b" if odd else "w1a", pair, used - 1)
                expert_load("w3b" if odd else "w3a", pair, used)
                expert_load("w2", pair, used)

            expert_load("w1a", 2, 1)
            for half in range(2):
                sp.wait_ge(S["w3_done"], 1 + half)
                load_half("w3b", 1, half, 1)
            expert_load("w2", 1, 1)
            expert_load("w1b", 3, 2)
            expert_load("w3a", 2, 2)
            expert_load("w2", 2, 2)
            expert_load("w3b", 3, 3)
            expert_load("w2", 3, 3)
            with sp.Fori(2, PAIRS // 2) as p2:
                pair_loads(0, 2 * p2, 2 * p2)
                pair_loads(1, 2 * p2 + 1, 2 * p2 + 1)
            sp.wait_ge(S["rounds_ready"], 1)
            n_rounds = sp.value_load(rounds_i[0:1, 0:1], min_val=1, max_val=T // SLOTS)
            with sp.If(n_rounds > 1):
                with sp.Fori(1, n_rounds) as r:
                    with sp.Fori(0, PAIRS // 2) as p2:
                        pair_loads(0, 2 * p2, r * PAIRS + 2 * p2)
                        pair_loads(1, 2 * p2 + 1, r * PAIRS + 2 * p2 + 1)
            for c in range(TC):
                sp.wait_ge(S["y_final"], c + 1)
                sp.dma_start(out[0, c * P:(c + 1) * P, :], y_out[:, c, :]).then_inc(S["out_stored"], 16)
            sp.wait_ge(S["out_stored"], 16 * TC)

        LO_FIRST = 2

        @block.gpsimd
        def _(pool):
            step = in_order(pool, "pool_order")
            step(nc.gpsimd.memset(ident[:], 0.0))
            step(nc.gpsimd.affine_select(out=ident[:], in_=ident[:], compare_op=ALU.not_equal, fill=1.0,
                                         base=0, pattern=[[-1, P]], channel_multiplier=1), "ident_ready")
            step(nc.gpsimd.memset(tmp4[:, 3, :], 0.0), "bd_zeroed")
            nc.gpsimd.memset(ones[:], 1.0)
            nc.gpsimd.memset(negones[:], -1.0)
            nc.gpsimd.memset(alpha_ident[:], 0.0)
            nc.gpsimd.memset(past_bias[:], 0.0)
            nc.gpsimd.memset(eps_ln, LN_EPS)
            nc.gpsimd.memset(eps_rms, RMS_EPS)
            nc.gpsimd.memset(level1T, 0.0)
            nc.gpsimd.memset(before[:], 1.0)
            step(nc.gpsimd.memset(level, 0.0))
            nc.gpsimd.affine_select(out=alpha_ident[:], in_=alpha_ident[:], compare_op=ALU.not_equal,
                                    fill=ALPHA, base=0, pattern=[[-1, P]], channel_multiplier=1)
            for m, src, op, up in ((upper, ones, ALU.is_ge, 1), (strict, ones, ALU.is_gt, 1),
                                   (lower, ones, ALU.is_gt, -1), (negtri, negones, ALU.is_ge, -1)):
                nc.gpsimd.affine_select(out=m[:], in_=src[:], compare_op=op, fill=0.0, base=0,
                                        pattern=[[up, P]], channel_multiplier=-up)
            for n in (0, 2):
                nc.gpsimd.affine_select(out=past_bias[:, n, :], in_=past_bias[:, n, :],
                                        compare_op=ALU.is_gt, fill=-1e30, base=0,
                                        pattern=[[1, P]], channel_multiplier=-1)
            nc.gpsimd.affine_select(out=before[:], in_=before[:], compare_op=ALU.is_gt, fill=0.0,
                                    base=0, pattern=[[1, PER_GROUP], [-1, PER_GROUP]],
                                    channel_multiplier=0)
            nc.gpsimd.iota(slot_ids[:], pattern=[[1, SLOTS]], base=SLOT_BASE, channel_multiplier=0,
                           allow_small_or_imprecise_dtypes=True)

            def left_half(n, size):
                return level[:, n, :].rearrange("p (b a s) -> p b a s", a=2, s=size)[:, :, 0, :]

            for n, size in enumerate([1] + LEVELS):
                nc.gpsimd.affine_select(
                    out=left_half(n, size), in_=ones[:, 0:P // 2].rearrange("p (b s) -> p b s", s=size),
                    compare_op=ALU.is_ge, fill=0.0, base=-size,
                    pattern=[[-2 * size, P // (2 * size)], [0, size]], channel_multiplier=1)
            right1 = level1T.rearrange("p (b a) -> p b a", a=2)[:, :, 1]
            step(nc.gpsimd.affine_select(out=right1, in_=ones[:, 0:P // 2], compare_op=ALU.not_equal,
                                         fill=0.0, base=0, pattern=[[-2, P // 2]],
                                         channel_multiplier=1))
            step(nc.gpsimd.tensor_tensor(right1, ones[:, 0:P // 2], right1, ALU.subtract))
            for n, size in enumerate([1] + LEVELS):
                end = nc.gpsimd.affine_select(
                    out=left_half(n, size), in_=left_half(n, size), compare_op=ALU.is_ge, fill=0.0,
                    base=2 * size - 1, pattern=[[2 * size, P // (2 * size)], [0, size]],
                    channel_multiplier=-1)
            step(end, "consts")

            def split_lo(n):
                pool.wait_ge(S["hi_ready"], n + 1)
                step(nc.gpsimd.tensor_tensor(w_lo[:, n % RAW_SLOTS, :], raw_unit(n),
                                             hi_place(n).bitcast(F32), ALU.subtract), "lo_ready")

            for n in range(LO_FIRST, 10):
                split_lo(n)
            pool.wait_ge(S["dec_ready"], 1)
            d8 = dec.rearrange("p c h t -> p (c h) t")
            dT8 = decT.rearrange("p c h t -> p (c h) t")
            step(nc.gpsimd.tensor_tensor(d8, d8, bc(lower[:], 1, 8), ALU.mult), "dec_masked")
            step(nc.gpsimd.tensor_tensor(dT8, dT8, bc(upper[:], 1, 8), ALU.mult), "dec_masked")
            for n in range(10, UP0 + 2):
                split_lo(n)
            pool.wait_ge(S["yb_psum"], 1)
            for n, w in ((0, ln1_g), (1, ln1_b)):
                pool.dma_start(ln_gb[:, n, :], w[0].partition_broadcast(P)).then_inc(S["ln_in"], 16)
            for n in range(UP0 + 2, N_DENSE):
                split_lo(n)
            pool.wait_ge(S["yc_ready"], 1)
            for n, w in ((2, ln2_g), (3, ln2_b)):
                pool.dma_start(ln_gb[:, n, :], w[0].partition_broadcast(P)).then_inc(S["ln2_in"], 16)
            for c in range(TC):
                pool.wait_ge(S["x1h_ready"], c + 1)
                step(nc.gpsimd.tensor_tensor(x1l[:, c, :], x1[:, c, :], x1h[:, c, :].bitcast(F32),
                                             ALU.subtract), "x1_split")
        @block.scalar
        def _(act):
            step = in_order(act, "act_order")

            def split_hi(n):
                if UP0 + HI_SLOTS <= n < OUT0:
                    wait_used(act, n - HI_SLOTS)
                wait_unit_loaded(act, n)
                nc.scalar.activation(hi_place(n), raw_unit(n), ACT.Copy
                                     ).then_inc(S["hi_ready"], 1)

            for b in range(4):
                act.wait_ge(S["xT_psum"], b + 1)
                nc.scalar.activation(flat(xh[:, 2 * b:2 * b + 2, :]), bank(b), ACT.Copy
                                     ).then_inc(S["xh_ready"], 1)
            split_hi(0)
            act.wait_ge(S["small_in"], 16 * 5)
            nc.scalar.activation(ba_hi[:], w_ba[:], ACT.Copy).then_inc(S["ba_hi_ready"], 1)
            split_hi(1)

            act.wait_ge(S["bd_zeroed"], 1)
            for n, w in enumerate((lru_w_a, lru_w_x)):
                for half in range(2):
                    o = 64 * half
                    act.dma_start(w_bd[o:o + 64, n, :, o:o + 64],
                                  w[0].rearrange("(c h) i o -> h i c o", h=2)[half]
                                  ).then_inc(S["bd_in"], 16)

            def read_unit(u):
                kind, dst, c, n = unit(u)
                act.wait_ge(S["unit_psum"], u + 1)
                if kind in ("sv", "lx", "ly"):
                    act.wait_ge(S["conv_done"], 6)
                if kind in ("gate", "ga", "gx"):
                    act.wait_ge(S["cols_ready"], 1)
                    b = {"gate": C_BM, "ga": C_BA, "gx": C_BX}[kind] + c
                    for j in range(2):
                        ins = nc.scalar.activation(dst[:, c + j, :], bank(u % 3)[:, j * T:(j + 1) * T],
                                                   ACT.Identity, bias=cols[:, b + j:b + j + 1])
                else:
                    ins = nc.scalar.activation(flat(dst[:, c:c + 2, :]), bank(u % 3), ACT.Copy,
                                               scale=SB_D ** -0.5 if kind == "sq" else 1.0)
                step(ins, "unit_read")
                if n is not None:
                    split_hi(n + HI_SLOTS)

            def silu(v):
                act.wait_ge(S["conv_done"], v + 1)
                kind, c = v // 2, 2 * (v % 2)
                t = vc[:, c:c + 2, :] if kind == 2 else qk[:, c:c + 2, 1 - kind, :]
                step(nc.scalar.activation(t, t, ACT.Silu), "silu_done")

            read_unit(0)
            act.wait_ge(S["ba_psum"], 1)
            step(nc.scalar.activation(tinyT[0:8, :], ps[0:8, 7, 0:T], ACT.Copy), "ba_copied")
            read_unit(1)
            act.wait_ge(S["g_abs"], 1)
            step(nc.scalar.activation(beta.rearrange("p (c h) -> p c h", c=TC),
                                      bank(7)[:, 256:272].rearrange("p (c e) -> p c e", c=TC)[:, :, 0:4],
                                      ACT.Exp, scale=-1.0))
            step(nc.scalar.activation(ea, heads4[:, 0, :], ACT.Exp))
            step(nc.scalar.activation(e12, e12, ACT.Exp, scale=-1.0), "g_exp")
            silu(0)
            for u in range(2, 6):
                read_unit(u)
                silu(u - 1)
            read_unit(6)
            silu(5)
            for n in range(2):
                step(nc.scalar.activation(norms[:, n, :], flat(qk[:, 2 * n:2 * n + 2]), ACT.Square),
                     "sq_ready")
            read_unit(7)
            step(nc.scalar.activation(flat(raw["z"]), flat(raw["z"]), ACT.Silu), "z_silu")
            nc.scalar.preload_act_table_set("natural_log_exp_and_others")
            act.wait_ge(S["gc_ready"], 1)
            step(nc.scalar.activation(eg, gc, ACT.Exp))
            act.wait_ge(S["diff_ready"], 1)
            step(nc.scalar.activation(eG1, heads(4), ACT.Exp))
            step(nc.scalar.activation(kds[:, 0:4], kds[:, 0:4], ACT.Exp))
            step(nc.scalar.activation(flat(dec), flat(dec), ACT.Exp, scale=-1.0))
            step(nc.scalar.activation(flat(decT), flat(decT), ACT.Exp), "dec_ready")
            read_unit(8)
            for n in range(2):
                act.wait_ge(S["ss_psum"], n + 1)
                for b in range(2):
                    step(nc.scalar.activation(norms[:, n, b * 512:(b + 1) * 512],
                                              bank((5, 3)[n] + b), ACT.Ln, bias=eps_rms))
                step(nc.scalar.activation(norms[:, n, :], norms[:, n, :], ACT.Exp, scale=-0.5),
                     "rn_ready")
            for u in (9, 10, 11):
                read_unit(u)
            act.wait_ge(S["at_psum"], 1)
            for c in range(TC):
                step(nc.scalar.activation(flat(AT[:, c]), bank(3 + c), ACT.Copy), "at_ready")
            read_unit(12)
            for n in range(len(LEVELS)):
                for c in range(TC):
                    act.wait_ge(S["inv_t"], TC * n + c + 1)
                    step(nc.scalar.activation(flat(MT[:, c]), bank(3 + 2 * c), ACT.Copy), "inv_mt")
                if n == len(LEVELS) - 1:
                    step(nc.scalar.activation(flat(raw["ly"]), flat(raw["ly"]), ACT.Gelu_apprx_tanh),
                         "gelu_ready")
                    nc.scalar.preload_act_table_set("natural_log_exp_and_others")
                read_unit(13 + n)
            act.wait_ge(S["s1_psum"], 1)
            step(nc.scalar.activation(flat(S1), bank(4), ACT.Copy), "s1_ready")
            read_unit(19)
            act.wait_ge(S["o_psum"], 1)
            for b in range(2):
                step(nc.scalar.activation(norms[:, 0, b * 512:(b + 1) * 512], bank(5 + b), ACT.Square),
                     "o_sq")
            act.wait_ge(S["oss_psum"], 1)
            for b in range(2):
                step(nc.scalar.activation(norms[:, 1, b * 512:(b + 1) * 512], bank(3 + b), ACT.Ln,
                                          bias=eps_rms, scale=1.0 / P))
            step(nc.scalar.activation(norms[:, 1, :], norms[:, 1, :], ACT.Exp, scale=-0.5), "o_rms")
            read_unit(20)
            act.wait_ge(S["sv_psum"], 1)
            for c in range(TC):
                step(nc.scalar.activation(vS[:, c, :], bank(3 + c), ACT.Copy), "sv_ready")
            read_unit(21)

            lrf, lif = flat(lr), flat(li)
            for k in range(SB_H + 2):
                if k < SB_H:
                    act.wait_ge(S["z_psum"], k + 1)
                    step(nc.scalar.activation(zs[:, k, :], bank(3 + k % 3)[:, 0:T + P], ACT.Abs))
                    step(nc.scalar.activation(zs[:, k, :], zs[:, k, :], ACT.Exp, scale=-1.0))
                    step(nc.scalar.activation(zs[:, k, :], zs[:, k, :], ACT.Ln, bias=1.0), "z_log")
                if k >= 2:
                    act.wait_ge(S["r_min"], k - 1)
                    step(nc.scalar.activation(att[:, k - 2, :], att[:, k - 2, :], ACT.Exp), "att_ready")
                if k < SB_H:
                    for u in TURN_UNITS[k]:
                        read_unit(u)
                if k == 4:
                    step(nc.scalar.activation(lrf, lrf, ACT.Exp, scale=-1.0))
                    step(nc.scalar.activation(lrf, lrf, ACT.Ln, bias=1.0))
                elif k == 5:
                    step(nc.scalar.activation(lrf, lrf, ACT.Exp, scale=-1.0), "lru_gate")
                    step(nc.scalar.activation(lif, lif, ACT.Exp, scale=-1.0))
                elif k == 6:
                    step(nc.scalar.activation(lif, lif, ACT.Ln, bias=1.0))
                    step(nc.scalar.activation(lif, lif, ACT.Exp, scale=-1.0), "lru_gate")
            for b in range(2):
                act.wait_ge(S["yb_psum"], 1)
                step(nc.scalar.activation(flat(y_hi[1][:, 2 * b:2 * b + 2, :]), bank(6 + b), ACT.Copy),
                     "yb_ready")
            act.wait_ge(S["lru_log_a"], 1)
            step(nc.scalar.activation(far, lrf, ACT.Exp, scale=2.0))
            step(nc.scalar.activation(flat(la), lrf, ACT.Exp))
            step(nc.scalar.activation(lq, lrf, ACT.Tanh), "lru_a")

            def gate_sigmoid(n):
                part = flat(gates)[:, n * 8 * T:(n + 1) * 8 * T]
                step(nc.scalar.activation(part, part, ACT.Sigmoid), "gates_ready")

            gate_sigmoid(0)
            split_hi(UP0 + 2)
            act.wait_ge(S["lru_var"], 1)
            step(nc.scalar.activation(far, far, ACT.Sqrt, scale=-1.0), "lru_b")
            split_hi(UP0 + 3)
            gate_sigmoid(1)
            split_hi(UP0 + 4)
            gate_sigmoid(2)
            split_hi(UP0 + 5)
            act.wait_ge(S["y_split"], 3)
            split_hi(OUT0)
            split_hi(OUT0 + 1)
            act.wait_ge(S["up_psum"], N_UPS)
            split_hi(OUT0 + 2)
            act.wait_ge(S["merged_split"], 2)
            split_hi(OUT0 + 3)

            nc.scalar.preload_act_table_set("natural_log_exp_and_others")

            def inv_std(n):
                act.wait_ge(S["ln_var"], n + 1)
                step(nc.scalar.activation(rstd, mv[:, 1:2], ACT.Ln, bias=eps_ln))
                step(nc.scalar.activation(rstd, rstd, ACT.Exp, scale=-0.5), "ln_rstd")

            inv_std(0)
            for n in range(3):
                if n == 2:
                    inv_std(1)
                act.wait_ge(S["x1T_psum"], n + 1)
                nc.scalar.activation(x1T[:, n % 2 * 4:n % 2 * 4 + 4, n // 2 * P:(n // 2 + 1) * P],
                                     heads(4 + n), ACT.Copy).then_inc(S["x1T_ready"], 1)
            for c in range(TC):
                nc.scalar.activation(x1h[:, c, :], x1[:, c, :], ACT.Copy).then_inc(S["x1h_ready"], 1)
            act.wait_ge(S["sm_in"], 1)
            step(nc.scalar.activation(score, score, ACT.Exp), "sm_exp")

            def read_gather(n):
                act.wait_ge(S["gathered"], n)
                nc.scalar.activation(xg[:, 0:512], bank(6), ACT.Copy).then_inc(S["xg_ready"], 1)

            def read_gatherT(n):
                act.wait_ge(S["xgT_psum"], n)
                nc.scalar.activation(flat(xgT[:, 0:4, :]), bank(6), ACT.Copy).then_inc(S["xgT_ready"], 1)

            nc.scalar.preload_act_table(ACT.Silu)
            read_gather(1)
            read_gatherT(1)
            act.wait_ge(S["rounds_ready"], 1)
            n_rounds = act.value_load(rounds_i[0:1, 0:1], min_val=1, max_val=T // SLOTS)
            with act.Fori(0, n_rounds) as r:
                with act.Fori(0, PAIRS) as p:
                    i = r * PAIRS + p
                    act.wait_ge(S["w1_done"], 2 * i + 2)
                    nc.scalar.activation(gS, bank(4), ACT.Silu).then_inc(S["h_silu"], 1)
                    read_gather(i + 2)
                    read_gatherT(i + 2)
                    act.wait_ge(S["w2_done"], 2 * i + 2)
                    act.wait_ge(S["slot_gate_ready"], i + 1)
                    for half in range(2):
                        nc.scalar.activation(y_slot_hi[:, half * 512:(half + 1) * 512], bank(4 + half),
                                             ACT.Copy, scale=slot_gate).then_inc(S["y_ready"], 1)
            nc.scalar.preload_act_table_set("natural_log_exp_and_others")
            act.wait_ge(S["ln_var"], TC + 1)
            step(nc.scalar.activation(rstd2, mv2[:, :, 1], ACT.Ln, bias=eps_ln))
            step(nc.scalar.activation(rstd2, rstd2, ACT.Exp, scale=-0.5), "ln_rstd")
        @block.tensor
        def _(pe):
            mm = nc.tensor.matmul

            def tr(dst, src):
                k = src.shape[0]
                return nc.tensor.transpose(dst, src, ident[0:k, 0:k])

            pe.wait_ge(S["ident_ready"], 1)
            for c in range(TC):
                pe.wait_ge(S[f"x_in_{c}"], 16)
                for k in range(KD):
                    last = tr(bank(k // 2)[:, (k % 2) * T + c * P:(k % 2) * T + (c + 1) * P],
                              xin[:, c, k:D:KD])
                    if c == TC - 1 and k % 2:
                        last.then_inc(S["xT_psum"], 1)
            pe.wait_ge(S["xh_ready"], 4)
            pe.wait_ge(S["xl_ready"], 4)

            def wait_lo(n):
                if n < LO_FIRST:
                    pe.wait_ge(S["lo_first"], n + 1)
                else:
                    pe.wait_ge(S["lo_ready"], n - LO_FIRST + 1)

            def hi_products(n, dst, w_cols, ks, x_hi, x_lo, js):
                pe.wait_ge(S["hi_ready"], n + 1)
                wh = w_hi[:, n % HI_SLOTS, :].rearrange("p (k n) -> p k n", k=ks)
                for j in js:
                    o = w_cols[j]
                    for k in range(ks):
                        for rhs in (x_hi, x_lo):
                            mm(dst[j], wh[:, k, o:o + P], rhs[:, k, :],
                               start=(k == 0 and rhs is x_hi and j % 2 == 0), stop=False,
                               skip_group_check=True)

            def lo_products(n, dst, w_cols, ks, x_hi, js):
                wait_lo(n)
                wl = w_lo[:, n % RAW_SLOTS, :].rearrange("p (k n) -> p k n", k=ks)
                for j in js:
                    o = w_cols[j]
                    for k in range(ks):
                        last = mm(dst[j], wl[:, k, o:o + P], x_hi[:, k, :], start=False,
                                  stop=(k == ks - 1), skip_group_check=True)
                return last

            def run_unit(u, parts=(0, 1, 2, 3)):
                kind, _, c, n = unit(u)
                if u >= 3 and 0 in parts:
                    pe.wait_ge(S["unit_read"], u - 2)
                dst = [bank(u % 3)[:, j * T:(j + 1) * T] for j in range(2)]
                if n is None:
                    pe.wait_ge(S["xc_ready"], 4)
                    pe.wait_ge(S["bd_in"], 16 * 4)
                    for j in range(2):
                        last = mm(dst[j], w_bd[:, 0 if kind == "ga" else 1, c + j, :], xc[:, c + j, :],
                                  start=True, stop=True)
                else:
                    for part in parts:
                        if part < 2:
                            hi_products(n, dst, (0, P), KD, xh, xl, (part,))
                        else:
                            last = lo_products(n, dst, (0, P), KD, xh, (part - 2,))
                if 3 in parts:
                    last.then_inc(S["unit_psum"], 1)

            run_unit(0)
            pe.wait_ge(S["rows_in"], 16 * 8)
            tr(bank(6)[:, 0:N_ROWS], rows[0:N_ROWS, :]).then_inc(S["rows_psum"], 1)
            pe.wait_ge(S["ba_split"], 1)
            for k in range(KD):
                for n, (a, b) in enumerate(((ba_hi, xh), (ba_hi, xl), (ba_lo, xh))):
                    last = mm(ps[0:8, 7, 0:T], a[:, k, :], b[:, k, :], start=(k == 0 and n == 0),
                              stop=(k == KD - 1 and n == 2))
            last.then_inc(S["ba_psum"], 1)
            run_unit(1)
            pe.wait_ge(S["ba_copied"], 1)
            for c in range(TC):
                last = tr(bank(7)[:, 256 + 8 * c:264 + 8 * c], tinyT[0:8, c * P:(c + 1) * P])
            last.then_inc(S["ba_tok"], 1)
            for u in range(2, 5):
                run_unit(u)

            pe.wait_ge(S["consts"], 1)
            pe.wait_ge(S["g_ready"], 1)
            for c in range(TC):
                mm(bank(7)[:, 272 + 4 * c:276 + 4 * c], upper[:], g[:, 4 * c:4 * c + 4],
                   start=True, stop=True)
            for c in range(TC):
                for h in range(DN_H):
                    last = mm(heads(3 + c)[:, h, :],
                              g[:, 4 * c + h:4 * c + h + 1].broadcast_to([P, P]), upper[:],
                              start=True, stop=True)
            last.then_inc(S["gb_psum"], 1)
            for u in range(5, 9):
                run_unit(u)

            for n in range(2):
                pe.wait_ge(S["sq_ready"], n + 1)
                if n == 1:
                    run_unit(9, (0,))
                    pe.wait_ge(S["dec_ready"], 1)
                for b in range(2):
                    last = mm(bank((5, 3)[n] + b), ones[:], norms[:, n, b * 512:(b + 1) * 512],
                              start=True, stop=True)
                last.then_inc(S["ss_psum"], 1)
            run_unit(9, (1, 2, 3))
            run_unit(10, (0,))

            pe.wait_ge(S["qk_ready"], 1)
            for h in range(DN_H):
                tr(heads(3)[:, h, :], qk[:, h, 0, 0:P])
            for c in range(TC):
                for h in range(DN_H):
                    last = tr(heads(5 + c)[:, h, :], vc[:, h, c * P:(c + 1) * P])
            last.then_inc(S["tok_psum"], 1)
            run_unit(10, (1, 2, 3))

            pe.wait_ge(S["tok_ready"], 1)
            for c in range(TC):
                for h in range(DN_H):
                    last = mm(bank(3 + 2 * c + h // 2).rearrange("p (a b t) -> p a b t", a=2, b=2)[:, h % 2],
                              qk[:, h, 0, c * P:(c + 1) * P], qk[:, h, :, c * P:(c + 1) * P],
                              start=True, stop=True)
            last.then_inc(S["kk_psum"], 1)
            run_unit(11)
            pe.wait_ge(S["a_ready"], 1)
            for c in range(TC):
                for h in range(DN_H):
                    last = tr(heads(3 + c)[:, h, :], Amat[:, c, h, :])
            last.then_inc(S["at_psum"], 1)
            run_unit(12)

            pe.wait_ge(S["at_ready"], TC)
            for n in range(len(LEVELS)):
                for c in range(TC):
                    pe.wait_ge(S["inv_m"], TC * n + c + 1)
                    if n:
                        pe.wait_ge(S["inv_mt"], TC * (n - 1) + c + 1)
                    for h in range(DN_H):
                        last = mm(heads(3 + 2 * c)[:, h, :], AT[:, c, h, :], M[:, c, h, :],
                                  start=True, stop=True)
                    last.then_inc(S["inv_x"], 1)
                run_unit(13 + n, (0,))
                for c in range(TC):
                    pe.wait_ge(S["inv_xs"], TC * n + c + 1)
                    for h in range(DN_H):
                        last = mm(heads(4 + 2 * c)[:, h, :], MT[:, c, h, :], XS[:, c, h, :],
                                  start=True, stop=True)
                    last.then_inc(S["inv_z"], 1)
                run_unit(13 + n, (1, 2))
                for c in range(TC):
                    pe.wait_ge(S["inv_m"], TC * (n + 1) + c + 1)
                    for h in range(DN_H):
                        last = tr(heads(3 + 2 * c)[:, h, :], M[:, c, h, :])
                    last.then_inc(S["inv_t"], 1)
                run_unit(13 + n, (3,))

            run_unit(19, (0,))
            pe.wait_ge(S["inv_mt"], TC * len(LEVELS))
            for h in range(DN_H):
                last = mm(heads(3)[:, h, :], MT[:, 0, h, :], vb[:, 0, h, :], start=True, stop=True)
            last.then_inc(S["v0_psum"], 1)
            run_unit(19, (1,))
            pe.wait_ge(S["v0_ready"], 1)
            for h in range(DN_H):
                last = mm(heads(4)[:, h, :], kdec[:, h, :], V0[:, h, :], start=True, stop=True)
            last.then_inc(S["s1_psum"], 1)

            def o_part(c, h):
                return bank(5 + h // 2).rearrange("p (a c t) -> p a c t", a=2, c=TC)[:, h % 2, c, :]

            for h in range(DN_H):
                mm(o_part(0, h), V0[:, h, :], QKT[:, 0, h, :], start=True, stop=True)
            run_unit(19, (2,))
            pe.wait_ge(S["s1_ready"], 1)
            for h in range(DN_H):
                last = mm(heads(3)[:, h, :], qk[:, h, 0, P:T], S1[:, h, :], start=True, stop=True)
            last.then_inc(S["ks_psum"], 1)
            run_unit(19, (3,))
            pe.wait_ge(S["r_ready"], 1)
            for h in range(DN_H):
                last = mm(heads(4)[:, h, :], MT[:, 1, h, :], R[:, h, :], start=True, stop=True)
            last.then_inc(S["v1_psum"], 1)
            run_unit(20, (0,))
            pe.wait_ge(S["v1_ready"], 1)
            for h in range(DN_H):
                mm(o_part(1, h), S1[:, h, :], qe[:, h, :], start=True, stop=False)
                last = mm(o_part(1, h), V1[:, h, :], QKT[:, 1, h, :], start=False, stop=True)
            last.then_inc(S["o_psum"], 1)
            run_unit(20, (1,))
            pe.wait_ge(S["o_sq"], 2)
            for b in range(2):
                last = mm(bank(3 + b), ones[:], norms[:, 0, b * 512:(b + 1) * 512], start=True, stop=True)
            last.then_inc(S["oss_psum"], 1)
            run_unit(20, (2, 3))
            run_unit(21, (0, 1))

            pe.wait_ge(S["o_rms"], 1)
            for c in range(TC):
                for j in range(4):
                    last = tr(heads(3 + c)[:, j, :], raw["sv"][:, j, c * P:(c + 1) * P])
            last.then_inc(S["sv_psum"], 1)
            run_unit(21, (2, 3))
            pe.wait_ge(S["sv_ready"], TC)
            pe.wait_ge(S["ya_ready"], 2)

            for k in range(SB_H + 2):
                if k < SB_H:
                    if k >= 3:
                        pe.wait_ge(S["r_min"], k - 2)
                    o = SB_D * (k % 2)
                    kt, qt = raw["sk"][o:o + SB_D, k // 2, :], raw["sq"][o:o + SB_D, k // 2, :]
                    zb = bank(3 + k % 3)
                    mm(zb[:, 0:T], kt[:, 0:P], qt, start=True, stop=True, skip_group_check=True)
                    mm(zb[:, T:T + P], kt[:, P:T], qt[:, P:T], start=False, stop=True,
                       skip_group_check=True).then_inc(S["z_psum"], 1)
                    for u in TURN_UNITS[k]:
                        run_unit(u)
                if 1 <= k <= SB_H:
                    h = k - 1
                    pe.wait_ge(S["z_masked"], h + 1)
                    zb = bank(3 + h % 3)
                    mm(zb[:, 0:T + P], negtri[:], zs[:, h, :], start=False, stop=True,
                       skip_group_check=True)
                    mm(zb[:, P:T], negones[:], zs[:, h, T:T + P], start=False, stop=True,
                       skip_group_check=True).then_inc(S["r_psum"], 1)
                if k >= 2:
                    h = k - 2
                    pe.wait_ge(S["att_ready"], h + 1)
                    o = SB_D * (h % 2)
                    yb = ps[o:o + SB_D, 6 + h // 4, (h // 2 % 2) * T:(h // 2 % 2 + 1) * T]
                    mm(yb, vS[:, 0, h * SB_D:(h + 1) * SB_D], att[:, h, 0:T], start=True, stop=False,
                       skip_group_check=True)
                    last = mm(yb[:, P:T], vS[:, 1, h * SB_D:(h + 1) * SB_D], att[:, h, T:T + P],
                              start=False, stop=True, skip_group_check=True)
            last.then_inc(S["yb_psum"], 1)

            for i in range(N_UPS):
                n = i // 2
                pe.wait_ge(S["y_split"], n + 1)
                if i == 1:
                    pe.wait_ge(S["y_split"], 2)
                if i >= 2:
                    pe.wait_ge(S["merged_ready"], i - 1)
                ub = [bank(3 + 2 * (i % 2) + j // 2)[:, (j % 2) * T:(j % 2 + 1) * T] for j in range(4)]
                up_cols = [P * j for j in range(4)]
                hi_products(UP0 + i, ub, up_cols, 4, y_hi[n], y_lo[:, n], range(4))
                lo_products(UP0 + i, ub, up_cols, 4, y_hi[n], range(4)).then_inc(S["up_psum"], 1)

            pe.wait_ge(S["unit_read"], N_ALL)
            for kh in range(2):
                pe.wait_ge(S["merged_split"], kh + 1)
                for c in range(TC):
                    for n in range(2):
                        u = OUT0 + 2 * kh + n
                        wh, wl = (t.rearrange("p (k n) -> p k n", k=4)
                                  for t in (hi_place(u), w_lo[:, u % RAW_SLOTS, :]))
                        mh, ml = (t[:, 4 * kh:4 * kh + 4, c * P:(c + 1) * P] for t in (xh, xl))
                        pe.wait_ge(S["hi_ready"], u + 1)
                        for k in range(4):
                            for part in (mh, ml):
                                mm(bank(2 * c + n), part[:, k, :], wh[:, k, :],
                                   start=(kh == 0 and k == 0 and part is mh), stop=False,
                                   skip_group_check=True)
                        wait_lo(u)
                        for k in range(4):
                            last = mm(bank(2 * c + n), mh[:, k, :], wl[:, k, :], start=False,
                                      stop=(kh == 1 and k == 3), skip_group_check=True)
                        if kh == 1:
                            last.then_inc(S["mix_psum"], 1)

            for c in range(TC):
                pe.wait_ge(S["x1_ready"], c + 1)
                for k in range(KD):
                    last = tr(heads(4 + 2 * c + k // 4)[:, k % 4, :], x1[:, c, k:D:KD])
                    if k % 4 == 3:
                        last.then_inc(S["x1T_psum"], 1)
                pe.wait_ge(S["x1T_ready"], 2 + c)
                if c == 1:
                    pe.wait_ge(S["x1T_last"], 1)
                for k in range(KD):
                    last = mm(bank(4)[:, N_EXP * c:N_EXP * (c + 1)], x1T[:, k, c * P:(c + 1) * P],
                              w_rt[:, k, :], start=(k == 0), stop=(k == KD - 1))
            last.then_inc(S["rt_psum"], 1)
            for c in range(TC):
                for n in range(2):
                    last = mm(bank(2 * c + n), alpha_ident[:], x1[:, c, n * 512:(n + 1) * 512],
                              start=True, stop=False, skip_group_check=True)
            last.then_inc(S["seeded"], 1)
            pe.wait_ge(S["mask_ready"], 1)
            mc = [mask[:, N_EXP * c:N_EXP * (c + 1)] for c in range(TC)]
            mm(bank(5)[:, 0:16], strict[:], mc[0], start=True, stop=True)
            mm(bank(5)[:, 16:32], ones[:], mc[0], start=True, stop=False)
            mm(bank(5)[:, 16:32], strict[:], mc[1], start=False, stop=True)
            mm(bank(5)[:, 32:48], ones[:], mc[0], start=True, stop=False)
            mm(bank(5)[:, 32:48], ones[:], mc[1], start=False, stop=True).then_inc(S["pos_psum"], 1)

            def gather(n):
                pe.wait_ge(S["pick_ready"], n)
                for half in range(2):
                    for c in range(TC):
                        for part in (x1h, x1l):
                            last = mm(bank(6 + half), pick_r[:, c, :], part[:, c, half * 512:(half + 1) * 512],
                                      start=(c == 0 and part is x1h), stop=(c == TC - 1 and part is x1l))
                last.then_inc(S["gathered"], 1)

            def gather_transpose(n):
                pe.wait_ge(S["xg_ready"], 2 * n)
                for k in range(KD):
                    last = tr(heads(6 + k // 4)[:, k % 4, :], xg[:, k:D:KD])
                last.then_inc(S["xgT_psum"], 1)

            pe.wait_ge(S["x1_split"], TC)
            gather(1)
            gather_transpose(1)
            pe.wait_ge(S["rounds_ready"], 1)
            n_rounds = pe.value_load(rounds_i[0:1, 0:1], min_val=1, max_val=T // SLOTS)
            def two_experts(m, loads, dsts, lhsT, steps, done, before_last=None):
                for half in range(2):
                    for e in range(2):
                        pe.wait_ge(expert_loaded[m, e, half], 16 * loads)
                    for k in range(steps // 2):
                        for n, dst in enumerate(dsts):
                            for e in range(2):
                                w = expert_place(m, e, half).rearrange("p (k n) -> p k n", k=steps // 2)
                                last = mm(dst[e * SLOTS:(e + 1) * SLOTS, :],
                                          lhsT[:, half * steps // 2 + k, e * SLOTS:(e + 1) * SLOTS],
                                          w[:, k, n * 512:(n + 1) * 512],
                                          start=(half == 0 and k == 0),
                                          stop=(half == 1 and k == steps // 2 - 1),
                                          skip_group_check=True)
                    last.then_inc(S[done], 1)

            def pe_pair(m1, m3, i, loads):
                pe.wait_ge(S["xgT_ready"], 2 * i + 2)
                two_experts(m1, loads, [bank(4)], xgT, KD, "w1_done")
                two_experts(m3, loads, [bank(5)], xgT, KD, "w3_done")
                gather(i + 2)
                pe.wait_ge(S["h_ready"], i + 1)
                for k in range(KF):
                    last = tr(heads(4)[:, k, :], hS[:, k:FF:KF])
                pe.wait_ge(S["pick_gate_ready"], i + 1)
                for c in range(TC):
                    last = tr(heads(5)[:, c, :], pick_gate[:, c, :])
                last.then_inc(S["hT_psum"], 1)
                gather_transpose(i + 2)
                pe.wait_ge(S["hT_ready"], i + 1)
                pe.wait_ge(S["slot_gate_ready"], i + 1)
                two_experts("w2", i + 1, [bank(4), bank(5)], hT, KF, "w2_done")
                for part, ready in ((y_slot_hi, "y_ready"), (y_slot_lo, "y_lo_ready")):
                    for half in range(2):
                        pe.wait_ge(S[ready], 2 * i + 1 + half)
                        for c in range(TC):
                            last = mm(bank(2 * c + half), pickT[:, c, :],
                                      part[:, half * 512:(half + 1) * 512], start=False, stop=False,
                                      skip_group_check=True)
                last.then_inc(S["scattered"], 1)

            with pe.Fori(0, n_rounds) as r:
                with pe.Fori(0, PAIRS // 2) as p2:
                    for odd, (m1, m3) in enumerate((("w1a", "w3a"), ("w1b", "w3b"))):
                        pe_pair(m1, m3, r * PAIRS + 2 * p2 + odd, r * (PAIRS // 2) + p2 + 1)

        @block.vector
        def _(dve):
            step = in_order(dve, "dve_order")
            tt, ts, stt = nc.vector.tensor_tensor, nc.vector.tensor_scalar, nc.vector.scalar_tensor_tensor
            copy = nc.vector.tensor_copy

            for b in range(4):
                dve.wait_ge(S["xh_ready"], b + 1)
                part = slice(2 * b, 2 * b + 2)
                tt(flat(xl[:, part, :]), bank(b), flat(xh[:, part, :]).bitcast(F32), ALU.subtract
                   ).then_inc(S["xl_ready"], 1)
            for n in range(LO_FIRST):
                dve.wait_ge(S["hi_ready"], n + 1)
                tt(w_lo[:, n, :], raw_unit(n), w_hi[:, n, :].bitcast(F32), ALU.subtract
                   ).then_inc(S["lo_first"], 1)
                if n == 0:
                    dve.wait_ge(S["ba_hi_ready"], 1)
                    tt(ba_lo[:], w_ba[:], ba_hi[:].bitcast(F32), ALU.subtract).then_inc(S["ba_split"], 1)
            dve.wait_ge(S["rows_psum"], 1)
            step(copy(cols[:, 0:N_ROWS], bank(6)[:, 0:N_ROWS]), "cols_ready")

            def conv(dst, src, w0, stride, bias=None):
                def w(tap):
                    return cols[:, w0 + tap * stride:w0 + tap * stride + 1]
                if bias is None:
                    step(ts(dst, src, w(TAPS - 1), None, ALU.mult))
                else:
                    step(ts(dst, src, w(TAPS - 1), bias, ALU.mult, ALU.add))
                for back in range(1, TAPS):
                    last = stt(dst[:, back:T], src[:, 0:T - back], w(TAPS - 1 - back), dst[:, back:T],
                               ALU.mult, ALU.add)
                    if back < TAPS - 1:
                        step(last)
                return last

            def conv_unit(v):
                dve.wait_ge(S["unit_read"], v + 1)
                kind, c = v // 2, 2 * (v % 2)
                for j in range(2):
                    dst = vc[:, c + j, :] if kind == 2 else qk[:, c + j, 1 - kind, :]
                    src = raw[("q", "k", "v")[kind]][:, c + j, :]
                    last = conv(dst, src, C_DNW + 4 * kind + c + j, 12)
                    step(last) if j == 0 else step(last, "conv_done")

            conv_unit(0)
            dve.wait_ge(S["ba_tok"], 1)
            dve.wait_ge(S["small_in"], 16 * 5)
            tok8 = bank(7)[:, 256:272].rearrange("p (c e) -> p c e", c=TC)
            step(tt(v12[:, 0:8].rearrange("p (c h) -> p c h", c=TC), tok8[:, :, 4:8],
                    bc(heads4[:, 1, :], 1, TC), ALU.add))
            step(ts(v12[:, 8:12], cols[:, C_LAM:C_LAM + 4], -1.0, None, ALU.mult))
            step(ts(m12, v12, 0.0, None, ALU.max))
            step(stt(e12, v12, -1.0, v12, ALU.mult, ALU.max), "g_abs")
            conv_unit(1)
            dve.wait_ge(S["g_exp"], 1)
            step(ts(beta, beta, 1.0, None, ALU.add))
            step(nc.vector.reciprocal(beta, beta))
            step(ts(z12, e12, 2.0, None, ALU.add))
            step(nc.vector.reciprocal(z12, z12))
            step(tt(z12, z12, e12, ALU.mult))
            step(tt(e12, z12, z12, ALU.mult))
            step(ts(q12, e12, 1.0 / 17, None, ALU.mult))
            for n in (15, 13, 11, 9, 7, 5, 3):
                step(stt(q12, q12, 1.0 / n, e12, ALU.add, ALU.mult))
            step(stt(q12, q12, 1.0, z12, ALU.add, ALU.mult))
            step(stt(sp12, q12, 2.0, m12, ALU.mult, ALU.add))
            step(ts(n8, sp12[:, 8:12], -LRU_C, None, ALU.mult))
            step(stt(g.rearrange("p (c h) -> p c h", c=TC), sp12[:, 0:8].rearrange("p (c h) -> p c h", c=TC),
                     -1.0, bc(ea, 1, TC), ALU.mult, ALU.mult), "g_ready")
            conv_unit(2)
            conv_unit(3)
            dve.wait_ge(S["gb_psum"], 1)
            step(copy(gc, bank(7)[:, 272:280]), "gc_ready")
            for c in range(TC):
                for h in range(DN_H):
                    gcol = gc[:, 4 * c + h:4 * c + h + 1]
                    ts(dec[:, c, h, :], heads(3 + c)[:, h, :], gcol, 0.0, ALU.subtract, ALU.max)
                    ts(decT[:, c, h, :], heads(3 + c)[:, h, :], gcol, 0.0, ALU.subtract, ALU.min)
            step(tt(kds[:, 0:4], heads(3)[:, :, P - 1], gc[:, 0:4], ALU.subtract), "diff_ready")
            conv_unit(4)
            conv_unit(5)
            dve.wait_ge(S["z_silu"], 1)
            step(ts(flat(raw["z"]), flat(raw["z"]), cols[:, C_NW:C_NW + 1], None, ALU.mult))
            for n in range(2):
                dve.wait_ge(S["rn_ready"], n + 1)
                rn = norms[:, n, :].rearrange("p (h b t) -> p h b t", h=2, b=2)
                for b, scale in ((0, 1.0), (1, P ** -0.5)):
                    t = qk[:, 2 * n:2 * n + 2, b, :]
                    last = stt(t, t, scale, rn[:, :, b, :], ALU.mult, ALU.mult)
            step(last, "qk_ready")
            dve.wait_ge(S["tok_psum"], 1)
            dve.wait_ge(S["dec_ready"], 1)
            for c in range(TC):
                for h in range(DN_H):
                    ts(vb[:, c, h, :], heads(5 + c)[:, h, :], beta[:, 4 * c + h:4 * c + h + 1], None, ALU.mult)
            for h in range(DN_H):
                last = ts(kdec[:, h, :], heads(3)[:, h, :], kds[:, h:h + 1], None, ALU.mult)
            step(last, "tok_ready")
            step(stt(negbeg, beta[:, 4:8], -1.0, eg[:, 4:8], ALU.mult, ALU.mult))
            dve.wait_ge(S["kk_psum"], 1)
            dve.wait_ge(S["dec_masked"], 2)

            def pair_bank(b):
                return bank(b).rearrange("p (a b t) -> p a b t", a=2, b=2)

            for c in range(TC):
                for h in range(DN_H):
                    stt(Amat[:, c, h, :], pair_bank(3 + 2 * c + h // 2)[:, h % 2, 0, :],
                        beta[:, 4 * c + h:4 * c + h + 1], dec[:, c, h, :], ALU.mult, ALU.mult)
                for hp in range(2):
                    last = tt(QKT[:, c, 2 * hp:2 * hp + 2, :], pair_bank(3 + 2 * c + hp)[:, :, 1, :],
                              decT[:, c, 2 * hp:2 * hp + 2, :], ALU.mult)
            step(last, "a_ready")

            def all8(m):
                return m.rearrange("p c h t -> p (c h) t")

            step(tt(all8(M), all8(Amat), bc(level[:, 0, :], 1, 8), ALU.mult))
            for c in range(TC):
                step(tt(M[:, c], bc(ident[:], 1, 4), M[:, c], ALU.subtract), "inv_m")
            dve.wait_ge(S["at_ready"], TC)
            step(tt(all8(MT), all8(AT), bc(level1T, 1, 8), ALU.mult))
            step(tt(all8(MT), bc(ident[:], 1, 8), all8(MT), ALU.subtract))
            step(tt(qe, qk[:, :, 1, P:T], eG1, ALU.mult))
            for n in range(len(LEVELS)):
                for c in range(TC):
                    dve.wait_ge(S["inv_x"], TC * n + c + 1)
                    step(tt(XS[:, c], heads(3 + 2 * c), bc(level[:, n + 1, :], 1, 4), ALU.mult), "inv_xs")
                for c in range(TC):
                    dve.wait_ge(S["inv_z"], TC * n + c + 1)
                    step(tt(M[:, c], M[:, c], heads(4 + 2 * c), ALU.subtract), "inv_m")
            dve.wait_ge(S["v0_psum"], 1)
            step(copy(flat(V0), bank(3)), "v0_ready")
            dve.wait_ge(S["ks_psum"], 1)
            for h in range(DN_H):
                last = stt(R[:, h, :], heads(3)[:, h, :], negbeg[:, h:h + 1], vb[:, 1, h, :],
                           ALU.mult, ALU.add)
            step(last, "r_ready")
            dve.wait_ge(S["v1_psum"], 1)
            step(copy(flat(V1), bank(4)), "v1_ready")
            dve.wait_ge(S["o_rms"], 1)
            for b in range(2):
                ya = flat(yT[:, 0, 2 * b:2 * b + 2, :])
                step(tt(ya, bank(5 + b), norms[:, 1, b * 512:(b + 1) * 512], ALU.mult), "ya_ready")
                step(tt(ya, ya, flat(raw["z"][:, 2 * b:2 * b + 2, :]), ALU.mult))

            def split_y(n):
                y = flat(yT[:, n])
                step(copy(flat(y_hi[n]), y))
                step(tt(flat(y_lo[:, n]), y, flat(y_hi[n]).bitcast(F32), ALU.subtract), "y_split")

            split_y(0)

            for k in range(SB_H + 2):
                for c in ((0, 1), (2, 3))[k] if k < 2 else ():
                    dve.wait_ge(S["unit_read"], 18)
                    last = conv(xc[:, c, :], raw["lx"][:, c, :], C_LW + c, 4,
                                cols[:, C_LCB + c:C_LCB + c + 1])
                    step(last, "xc_ready")
                if k >= 2:
                    h = k - 2
                    dve.wait_ge(S["r_psum"], h + 1)
                    step(stt(att[:, h, :], bank(3 + h % 3)[:, 0:T + P], 0.0, flat(past_bias[:]),
                             ALU.min, ALU.add), "r_min")
                if k < SB_H:
                    dve.wait_ge(S["z_log"], k + 1)
                    step(stt(zs[:, k, :], bank(3 + k % 3)[:, 0:T + P], 0.0, zs[:, k, :],
                             ALU.max, ALU.add), "z_sp")
                    diag = zs[:, k, :].rearrange("p (a t) -> p a t", t=P)[:, 0:3:2, :]
                    step(tt(diag, diag, bc(strict[:], 1, 2), ALU.mult), "z_masked")
                if k == 5:
                    dve.wait_ge(S["lru_gate"], 1)
                    for c in range(LRU_CH):
                        last = ts(lr[:, c, :], lr[:, c, :], n8[:, c:c + 1], None, ALU.mult)
                    step(last, "lru_log_a")
                elif k == 6:
                    dve.wait_ge(S["lru_gate"], 2)
                    step(tt(flat(li), flat(li), flat(xc), ALU.mult))
            for b in range(2):
                dve.wait_ge(S["yb_ready"], b + 1)
                part = slice(2 * b, 2 * b + 2)
                last = tt(flat(y_lo[:, 1, part, :]), bank(6 + b), flat(y_hi[1][:, part, :]).bitcast(F32),
                          ALU.subtract)
                step(last) if b == 0 else step(last, "y_split")

            def merge(i):
                n, half = i // 2, i % 2
                dve.wait_ge(S["gates_ready"], n + 1)
                dve.wait_ge(S["up_psum"], i + 1)
                b = 3 + 2 * (i % 2)
                o = (n * 8 + half * 4) * T
                prod = tmp[:, 2, :]
                dst = flat(merged)[:, half * 1024:(half + 1) * 1024]
                last = tt(prod if n else dst, flat(ps[:, b:b + 2, :]), flat(gates)[:, o:o + 1024], ALU.mult)
                if n:
                    step(last)
                    last = tt(dst, dst, prod, ALU.add)
                step(last, "merged_ready")

            dve.wait_ge(S["lru_a"], 1)
            step(stt(far, far, 1.0, lq, ALU.add, ALU.mult), "lru_var")
            merge(0)
            merge(1)
            dve.wait_ge(S["lru_b"], 1)
            step(tt(flat(li), flat(li), far, ALU.mult))
            for c in range(LRU_CH):
                last = nc.vector.tensor_tensor_scan(lr[:, c, :], la[:, c, :], li[:, c, :], 0.0,
                                                    ALU.mult, ALU.add)
            step(last)
            dve.wait_ge(S["gelu_ready"], 1)
            step(tt(flat(yT[:, 2]), flat(lr), flat(raw["ly"]), ALU.mult), "yc_ready")
            split_y(2)
            for i in range(2, N_UPS):
                merge(i)
                if i >= N_UPS - 2:
                    half = slice((i % 2) * 1024, (i % 2 + 1) * 1024)
                    step(copy(flat(xh[:])[:, half], flat(merged)[:, half]))
                    step(tt(flat(xl[:])[:, half], flat(merged)[:, half],
                            flat(xh[:])[:, half].bitcast(F32), ALU.subtract), "merged_split")


            dve.wait_ge(S["ln_in"], 16 * 2)
            for c in range(TC):
                t = x1[:, c, :]
                for n in range(2):
                    part = slice(n * 512, (n + 1) * 512)
                    dve.wait_ge(S["mix_psum"], 2 * c + n + 1)
                    step(stt(t[:, part], xin[:, c, part], ALPHA, bank(2 * c + n), ALU.mult, ALU.add))
                    last = nc.vector.bn_stats(stats[:, 6 * n:6 * n + 6], t[:, part])
                step(last)
                step(nc.vector.bn_aggr(mv, stats), "ln_var")
                step(stt(t, t, mv[:, 0:1], ln_gb[:, 0, :], ALU.subtract, ALU.mult))
                dve.wait_ge(S["ln_rstd"], c + 1)
                step(stt(t, t, rstd, ln_gb[:, 1, :], ALU.mult, ALU.add), "x1_ready")
            dve.wait_ge(S["x1T_psum"], 4)
            copy(x1T[:, 4:8, P:T], heads(7)).then_inc(S["x1T_last"], 1)

            dve.wait_ge(S["rt_psum"], 1)
            l3, s3 = (t.rearrange("p (c e) -> p c e", c=TC) for t in (bank(4)[:, 0:32], score))
            step(nc.vector.tensor_reduce(mx, l3, AX_X, ALU.max))
            step(tt(s3, l3, bc(mx, 2, N_EXP), ALU.subtract), "sm_in")
            dve.wait_ge(S["sm_exp"], 1)
            step(nc.vector.tensor_reduce(sume, s3, AX_X, ALU.add))
            step(nc.vector.reciprocal(sume, sume))
            step(tt(s3, s3, bc(sume, 2, N_EXP), ALU.mult))
            step(tt(sel.rearrange("p (c e) -> p c e", c=TC), s3, bc(b_rt[:], 1, TC), ALU.add))

            def ranks(dst, vals, n):
                v = vals.rearrange("p (g e) -> p g e", e=PER_GROUP)
                other, own = bc(v, 2, PER_GROUP), bc(v, 3, PER_GROUP)
                c1, c2 = (t[:, 0:16 * n].rearrange("p (g a b) -> p g a b", a=4, b=4) for t in (cmp1, cmp2))
                tt(c2, other, own, ALU.is_gt)
                step(tt(c1, other, own, ALU.is_equal))
                step(tt(c1, c1, bc(before[:], 1, n), ALU.mult))
                step(tt(c1, c1, c2, ALU.add))
                step(nc.vector.tensor_reduce(dst, c1.rearrange("p g a b -> p (g a) b"), AX_X, ALU.add))

            ranks(chosen, sel, 8)
            step(ts(chosen, chosen, 1.5, None, ALU.is_lt))
            step(tt(tk, sel, chosen, ALU.mult))
            step(nc.vector.tensor_reduce(gsum, tk.rearrange("p (g e) -> p g e", e=4), AX_X, ALU.add))
            ranks(gsel, gsum, 2)
            step(ts(gsel, gsel, 0.5, None, ALU.is_lt))
            step(tt(mask.rearrange("p (g e) -> p g e", e=4), chosen.rearrange("p (g e) -> p g e", e=4),
                    bc(gsel, 2, 4), ALU.mult), "mask_ready")
            dve.wait_ge(S["pos_psum"], 1)
            m3 = mask.rearrange("p (c e) -> p c e", c=TC)
            step(stt(posx[:, :, 0:N_EXP], bank(5)[:, 0:32].rearrange("p (c e) -> p c e", c=TC), float(SLOT_BASE), m3,
                     ALU.add, ALU.mult))
            step(ts(posx[:, :, N_EXP:], posx[:, :, 0:2], -float(SLOTS), None, ALU.add))
            def pick_pair(first):
                tt(pick_r[:].rearrange("p c (e s) -> p c e s", e=2),
                   bc(bc(slot_ids[:], 1, 2), 1, TC),
                   bc(posx[:, :, first:first + 2], 3, SLOTS), ALU.is_equal).then_inc(S["pick_ready"], 1)

            def read_gather(n):
                dve.wait_ge(S["gathered"], n)
                copy(xg[:, 512:1024], bank(7)).then_inc(S["xg_ready"], 1)

            def read_gatherT(n):
                dve.wait_ge(S["xgT_psum"], n)
                copy(flat(xgT[:, 4:8, :]), bank(7)).then_inc(S["xgT_ready"], 1)

            pick_pair(0)
            step(tt(tk, score, mask, ALU.mult))
            tk3 = tk.rearrange("p (c e) -> p c e", c=TC)
            step(nc.vector.tensor_reduce(sume, tk3, AX_X, ALU.add))
            step(nc.vector.reciprocal(sume, sume))
            step(tt(gate[:, :, 0:N_EXP], tk3, bc(sume, 2, N_EXP), ALU.mult))
            step(copy(gate[:, :, N_EXP:], gate[:, :, 0:2]))
            step(nc.vector.tensor_reduce(cnt, bank(5)[:, 32:48], AX_X, ALU.max))
            for n in range(1, T // SLOTS):
                step(ts(rnd[:, n:n + 1], cnt, float(n * SLOTS), None, ALU.is_gt))
            step(nc.vector.tensor_reduce(rnd[:, 0:1], rnd[:, 1:4], AX_X, ALU.add))
            step(ts(rounds_i[:], rnd[:, 0:1], 1.0, None, ALU.add), "rounds_ready")

            read_gather(1)
            read_gatherT(1)
            n_rounds = dve.value_load(rounds_i[0:1, 0:1], min_val=1, max_val=T // SLOTS)
            with dve.Fori(0, n_rounds) as r:
                with dve.Fori(0, PAIRS) as p:
                    i = r * PAIRS + p
                    dve.wait_ge(S["pick_ready"], i + 1)
                    tt(pick_gate.rearrange("p c (e s) -> p c e s", e=2),
                       pick.rearrange("p c (e s) -> p c e s", e=2),
                       bc(gate[:, :, bass.ds(2 * p, 2)], 3, SLOTS), ALU.mult
                       ).then_inc(S["pick_gate_ready"], 1)
                    dve.wait_ge(S["pick_gate_ready"], i + 1)
                    tt(pick_r[:].rearrange("p c (e s) -> p c e s", e=2),
                       bc(bc(slot_ids[:], 1, 2), 1, TC),
                       bc(posx[:, :, bass.ds(2 * p + 2, 2)], 3, SLOTS), ALU.is_equal
                       ).then_inc(S["pick_ready"], 1)
                    dve.wait_ge(S["h_silu"], i + 1)
                    dve.wait_ge(S["w3_done"], 2 * i + 2)
                    tt(hS, gS, bank(5), ALU.mult).then_inc(S["h_ready"], 1)
                    read_gather(i + 2)
                    dve.wait_ge(S["hT_psum"], i + 1)
                    copy(flat(hT), bank(4)).then_inc(S["hT_ready"], 1)
                    ts(flat(pickT[:]), bank(5)[:, 0:256], 0.0, None, ALU.is_gt)
                    nc.vector.tensor_reduce(slot_gate, bank(5)[:, 0:256], AX_X, ALU.add
                                            ).then_inc(S["slot_gate_ready"], 1)
                    read_gatherT(i + 2)
                    for half in range(2):
                        dve.wait_ge(S["y_ready"], 2 * i + 1 + half)
                        part = slice(half * 512, (half + 1) * 512)
                        stt(y_slot_lo[:, part], bank(4 + half), slot_gate, y_slot_hi[:, part].bitcast(F32),
                            ALU.mult, ALU.subtract).then_inc(S["y_lo_ready"], 1)
                dve.wait_ge(S["pick_ready"], r * PAIRS + PAIRS + 1)
                ts(posx[:, :, 0:N_EXP], posx[:, :, 0:N_EXP], -float(SLOTS), None, ALU.add
                   ).then_inc(S["slots_moved"], 1)
                dve.wait_ge(S["slots_moved"], 2 * r + 1)
                ts(posx[:, :, N_EXP:], posx[:, :, 0:2], -float(SLOTS), None, ALU.add
                   ).then_inc(S["slots_moved"], 1)
                dve.wait_ge(S["slots_moved"], 2 * r + 2)

            dve.wait_ge(S["scattered"], n_rounds * PAIRS)
            for c in range(TC):
                for n in range(2):
                    last = nc.vector.bn_stats(stats2[:, c, 6 * n:6 * n + 6], bank(2 * c + n))
            step(last)
            nc.vector.bn_aggr(mv2[:, 0, :], stats2[:, 0, :])
            step(nc.vector.bn_aggr(mv2[:, 1, :], stats2[:, 1, :]), "ln_var")
            dve.wait_ge(S["ln2_in"], 16 * 2)
            for c in range(TC):
                for n in range(2):
                    part = slice(n * 512, (n + 1) * 512)
                    last = stt(y_out[:, c, part], bank(2 * c + n), mv2[:, c, 0:1], ln_gb[:, 2, part],
                               ALU.subtract, ALU.mult)
                step(last)
                dve.wait_ge(S["ln_rstd"], TC + 1)
                step(stt(y_out[:, c, :], y_out[:, c, :], rstd2[:, c:c + 1], ln_gb[:, 3, :],
                         ALU.mult, ALU.add), "y_final")


_INS = ['x', 'w_in', 'dn_conv_w', 'dn_a_log', 'dn_dt_bias', 'dn_norm_w', 'lru_conv_w', 'lru_conv_b',
        'lru_w_a', 'lru_b_a', 'lru_w_x', 'lru_b_x', 'lru_lambda', 'w_up_dn', 'w_up_sb', 'w_up_lru',
        'w_merge', 'b_merge', 'w_out', 'ln1_g', 'ln1_b', 'w_router', 'b_router', 'moe_w1', 'moe_w3',
        'moe_w2', 'ln2_g', 'ln2_b']
_OUTS = [((1, 256, 1024), 'float32')]


def kernel(**inputs):
    import numpy as _np
    import concourse.bacc as _bacc
    from concourse import mybir as _mybir
    from concourse.bass_utils import run_bass_kernel_spmd as _run

    nc = _bacc.Bacc("TRN2", target_bir_lowering=False, num_devices=1)
    arrays, args = {}, []
    for name in _INS:
        a = _np.ascontiguousarray(inputs[name])
        arrays[f"in_{name}_dram"] = a
        args.append(nc.dram_tensor(f"in_{name}_dram", a.shape, _mybir.dt.from_np(a.dtype),
                                   kind="ExternalInput").ap())
    for i, (shape, dtype) in enumerate(_OUTS):
        dt = _mybir.dt.from_np(_np.dtype(dtype))
        args.append(nc.dram_tensor(f"out_{i}_dram", shape, dt, kind="ExternalOutput").ap())
    hybrid_layer(nc, *args)
    r = _run(nc, [arrays], core_ids=[0])
    return r.results[0]["out_0_dram"]
```
